# Optimizing a Trainium2 kernel written in Bass

```python
import math
import jax, jax.numpy as jnp
from jax import lax
import numpy as np

D_MODEL = 1024
BATCH = 1
SEQ = 512
DEPTH = 2

CHUNK = 64
N_EVEN = (DEPTH + 1) // 2
N_ODD = DEPTH // 2
RMS_EPS = 1e-6
ROPE_THETA = 10000.0

DN_HEADS = 4
DN_DK = 128
DN_DV = 128
DN_CONV = 4
DN_QK = DN_HEADS * DN_DK
DN_V = DN_HEADS * DN_DV
DIFF_HEADS = 4
DIFF_HD = 64
DIFF_QK = DIFF_HEADS * 2 * DIFF_HD
DIFF_V = DIFF_HEADS * 2 * DIFF_HD
Q_BLOCK = 128
IN0_SPLITS = (3 * DN_QK if DN_QK == DN_V else 2 * DN_QK + DN_V, DN_HEADS, DN_HEADS, DN_V, DIFF_QK, DIFF_QK, DIFF_V)
IN0_WIDTH = sum(IN0_SPLITS)
MIX0_OUT = DN_V + DIFF_V
CA_HEADS = 16
CA_HD = D_MODEL // CA_HEADS
CA_LEFT_CHUNKS = 8
REL_CLIP = 256
D_FF = 2816
FFN_CONV = 3

kernel_name = "hybrid_deltanet_diffattn_chunkband_convffn"

def rmsnorm(x, g):
    xf = x.astype(jnp.float32)
    y = xf * lax.rsqrt(jnp.mean(xf * xf, axis=-1, keepdims=True) + RMS_EPS)
    return (y * g.astype(jnp.float32)).astype(x.dtype)

def l2norm(x):
    return x * lax.rsqrt(jnp.sum(x * x, axis=-1, keepdims=True) + RMS_EPS)

def split_cols(t, sizes):
    return jnp.split(t, [int(v) for v in np.cumsum(sizes)[:-1]], axis=-1)

def causal_dwconv(x, w):
    K, C = w.shape
    return lax.conv_general_dilated(
        x, w[:, None, :].astype(x.dtype), window_strides=(1,), padding=[(K - 1, 0)],
        dimension_numbers=("NWC", "WIO", "NWC"), feature_group_count=C)

def rope_tables(S, dim):
    inv = 1.0 / (ROPE_THETA ** (jnp.arange(0, dim, 2, dtype=jnp.float32) / dim))
    ang = jnp.arange(S, dtype=jnp.float32)[:, None] * inv[None, :]
    return jnp.cos(ang), jnp.sin(ang)

def apply_rope(x, cos, sin):
    half = x.shape[-1] // 2
    x1 = x[..., :half].astype(jnp.float32)
    x2 = x[..., half:].astype(jnp.float32)
    return jnp.concatenate([x1 * cos - x2 * sin, x2 * cos + x1 * sin], axis=-1).astype(x.dtype)

def gated_deltanet(q, k, v, a, b, A_log, dt_bias):
    out_dtype = v.dtype
    Bsz, S, H, dk = q.shape
    dv = v.shape[-1]
    n = S // CHUNK
    q = l2norm(q.astype(jnp.float32)) * (dk ** -0.5)
    k = l2norm(k.astype(jnp.float32))
    v = v.astype(jnp.float32)
    beta = jax.nn.sigmoid(b.astype(jnp.float32))
    g = -jnp.exp(A_log.astype(jnp.float32)) * jax.nn.softplus(a.astype(jnp.float32) + dt_bias.astype(jnp.float32))

    def chunks(t):
        return t.reshape(Bsz, n, CHUNK, H, -1).transpose(0, 3, 1, 2, 4)

    qc, kc, vc = chunks(q), chunks(k), chunks(v)
    bc = beta.reshape(Bsz, n, CHUNK, H).transpose(0, 3, 1, 2)
    gcum = jnp.cumsum(g.reshape(Bsz, n, CHUNK, H).transpose(0, 3, 1, 2), axis=-1)
    tri = jnp.tril(jnp.ones((CHUNK, CHUNK), bool))
    strict = jnp.tril(jnp.ones((CHUNK, CHUNK), bool), -1)
    gdiff = gcum[..., :, None] - gcum[..., None, :]
    decay = jnp.where(tri, jnp.exp(jnp.where(tri, gdiff, 0.0)), 0.0)
    kk = jnp.einsum("bhnid,bhnjd->bhnij", kc, kc)
    Lmat = jnp.where(strict, bc[..., :, None] * kk * decay, 0.0) + jnp.eye(CHUNK, dtype=jnp.float32)
    rhs = jnp.concatenate([vc * bc[..., None], kc * (bc * jnp.exp(gcum))[..., None]], axis=-1)
    sol = lax.linalg.triangular_solve(Lmat, rhs, left_side=True, lower=True, unit_diagonal=True)
    u, w = sol[..., :dv], sol[..., dv:]
    qk = jnp.where(tri, jnp.einsum("bhnid,bhnjd->bhnij", qc, kc) * decay, 0.0)
    q_dec = qc * jnp.exp(gcum)[..., None]
    k_dec = kc * jnp.exp(gcum[..., -1:] - gcum)[..., None]
    g_last = jnp.exp(gcum[..., -1])

    def step(state, xs):
        u_i, w_i, qk_i, qd_i, kd_i, gl_i = xs
        v_new = u_i - jnp.einsum("bhck,bhkv->bhcv", w_i, state)
        o = jnp.einsum("bhck,bhkv->bhcv", qd_i, state) + jnp.einsum("bhij,bhjv->bhiv", qk_i, v_new)
        state = state * gl_i[..., None, None] + jnp.einsum("bhck,bhcv->bhkv", kd_i, v_new)
        return state, o

    xs = tuple(jnp.moveaxis(t, 2, 0) for t in (u, w, qk, q_dec, k_dec, g_last))
    state0 = jnp.zeros((Bsz, H, dk, dv), jnp.float32)
    _, o = lax.scan(step, state0, xs)
    return o.transpose(1, 0, 3, 2, 4).reshape(Bsz, S, H, dv).astype(out_dtype)

def diff_attention(q, k, v, lam):
    Bsz, S, H, _, Dh = q.shape
    nb = S // Q_BLOCK
    scale = Dh ** -0.5
    qb = q.reshape(Bsz, nb, Q_BLOCK, H, 2, Dh).transpose(1, 0, 2, 3, 4, 5)
    key_chunk = jnp.arange(S) // CHUNK

    def block(args):
        q_i, i = args
        s = jnp.einsum("bqhmd,bkhmd->bhmqk", q_i, k, preferred_element_type=jnp.float32) * scale
        q_chunk = (i * Q_BLOCK + jnp.arange(Q_BLOCK)) // CHUNK
        mask = key_chunk[None, :] <= q_chunk[:, None]
        p = jax.nn.softmax(jnp.where(mask, s, -jnp.inf), axis=-1)
        attn = p[:, :, 0] - lam * p[:, :, 1]
        return jnp.einsum("bhqk,bkhd->bqhd", attn, v.astype(jnp.float32))

    o = lax.map(block, (qb, jnp.arange(nb)))
    return o.transpose(1, 0, 2, 3, 4).reshape(Bsz, S, H, 2 * Dh).astype(v.dtype)

def chunk_band_attention(q, k, v, rel_bias):
    Bsz, S, H, Dh = q.shape
    n = S // CHUNK
    band = (CA_LEFT_CHUNKS + 1) * CHUNK
    pad = CA_LEFT_CHUNKS * CHUNK
    kp = jnp.pad(k, ((0, 0), (pad, 0), (0, 0), (0, 0)))
    vp = jnp.pad(v, ((0, 0), (pad, 0), (0, 0), (0, 0)))
    qi = jnp.arange(CHUNK)
    kj = jnp.arange(band)
    rel = kj[None, :] - pad - qi[:, None]
    bias = rel_bias.astype(jnp.float32)[:, jnp.clip(rel, -REL_CLIP, REL_CLIP) + REL_CLIP]
    qc = q.reshape(Bsz, n, CHUNK, H, Dh).transpose(1, 0, 2, 3, 4)
    scale = Dh ** -0.5

    def one(args):
        q_c, c = args
        k_b = lax.dynamic_slice_in_dim(kp, c * CHUNK, band, axis=1)
        v_b = lax.dynamic_slice_in_dim(vp, c * CHUNK, band, axis=1)
        s = jnp.einsum("bqhd,bkhd->bhqk", q_c, k_b, preferred_element_type=jnp.float32) * scale + bias
        valid = kj >= pad - c * CHUNK
        p = jax.nn.softmax(jnp.where(valid, s, -jnp.inf), axis=-1)
        return jnp.einsum("bhqk,bkhd->bqhd", p, v_b.astype(jnp.float32))

    o = lax.map(one, (qc, jnp.arange(n)))
    return o.transpose(1, 0, 2, 3, 4).reshape(Bsz, S, H * Dh).astype(v.dtype)

def conv_gated_mlp(h, w_in, conv_w, conv_b, w_out):
    gate, up = split_cols(h @ w_in, (D_FF, D_FF))
    gate = causal_dwconv(gate, conv_w) + conv_b
    return (jax.nn.silu(gate) * up) @ w_out

def setup_inputs(seed: int = 0) -> dict:
    key = jax.random.key(seed)
    ks = iter(jax.random.split(key, 40))

    def nrm(shape, scale):
        return jax.random.normal(next(ks), shape, jnp.float32) * scale

    def gain(shape):
        return 1.0 + nrm(shape, 0.02)

    dt = jnp.exp(jax.random.uniform(next(ks), (N_EVEN, DN_HEADS), jnp.float32, math.log(1e-3), math.log(1e-1)))
    return {
        "x": nrm((BATCH, SEQ, D_MODEL), 1.0),
        "even_norm_mix": gain((N_EVEN, D_MODEL)),
        "even_w_in": nrm((N_EVEN, D_MODEL, IN0_WIDTH), D_MODEL ** -0.5),
        "even_dn_conv": nrm((N_EVEN, DN_CONV, 2 * DN_QK + DN_V), DN_CONV ** -0.5),
        "even_dn_A_log": jnp.log(jax.random.uniform(next(ks), (N_EVEN, DN_HEADS), jnp.float32, 1.0, 16.0)),
        "even_dn_dt_bias": dt + jnp.log(-jnp.expm1(-dt)),
        "even_dn_norm": gain((N_EVEN, DN_DV)),
        "even_diff_lambda": nrm((N_EVEN, 4, DIFF_HD), 0.1),
        "even_diff_subln": gain((N_EVEN, 2 * DIFF_HD)),
        "even_w_out": nrm((N_EVEN, MIX0_OUT, D_MODEL), MIX0_OUT ** -0.5),
        "odd_norm_mix": gain((N_ODD, D_MODEL)),
        "odd_w_qkv": nrm((N_ODD, D_MODEL, 3 * CA_HEADS * CA_HD), D_MODEL ** -0.5),
        "odd_rel_bias": nrm((N_ODD, CA_HEADS, 2 * REL_CLIP + 1), 0.2),
        "odd_w_out": nrm((N_ODD, CA_HEADS * CA_HD, D_MODEL), (CA_HEADS * CA_HD) ** -0.5),
        "ffn_norm": gain((DEPTH, D_MODEL)),
        "ffn_w_in": nrm((DEPTH, D_MODEL, 2 * D_FF), D_MODEL ** -0.5),
        "ffn_conv_w": nrm((DEPTH, FFN_CONV, D_FF), FFN_CONV ** -0.5),
        "ffn_conv_b": nrm((DEPTH, D_FF), 0.01),
        "ffn_w_out": nrm((DEPTH, D_FF, D_MODEL), D_FF ** -0.5),
        "final_norm": gain((D_MODEL,)),
    }

def reference(x, even_norm_mix, even_w_in, even_dn_conv, even_dn_A_log, even_dn_dt_bias,
              even_dn_norm, even_diff_lambda, even_diff_subln, even_w_out,
              odd_norm_mix, odd_w_qkv, odd_rel_bias, odd_w_out,
              ffn_norm, ffn_w_in, ffn_conv_w, ffn_conv_b, ffn_w_out, final_norm):
    Bsz, S, _ = x.shape
    cos, sin = rope_tables(S, DIFF_HD)
    cos_b, sin_b = cos[:, None, None, :], sin[:, None, None, :]
    for i in range(DEPTH):
        if i % 2 == 0:
            e = i // 2
            h = rmsnorm(x, even_norm_mix[e])
            dn_qkv, dn_a, dn_b, dn_gate, fq, fk, fv = split_cols(h @ even_w_in[e], IN0_SPLITS)
            dn_qkv = jax.nn.silu(causal_dwconv(dn_qkv, even_dn_conv[e]))
            dq, dk, dvv = split_cols(dn_qkv, (DN_QK, DN_QK, DN_V))
            o_a = gated_deltanet(dq.reshape(Bsz, S, DN_HEADS, DN_DK), dk.reshape(Bsz, S, DN_HEADS, DN_DK),
                                 dvv.reshape(Bsz, S, DN_HEADS, DN_DV), dn_a, dn_b,
                                 even_dn_A_log[e], even_dn_dt_bias[e])
            o_a = rmsnorm(o_a, even_dn_norm[e]) * jax.nn.silu(dn_gate.reshape(Bsz, S, DN_HEADS, DN_DV))
            o_a = o_a.reshape(Bsz, S, DN_V)
            lam_init = 0.8 - 0.6 * math.exp(-0.3 * i)
            lp = even_diff_lambda[e].astype(jnp.float32)
            lam = jnp.exp(jnp.sum(lp[0] * lp[1])) - jnp.exp(jnp.sum(lp[2] * lp[3])) + lam_init
            qd = apply_rope(fq.reshape(Bsz, S, DIFF_HEADS, 2, DIFF_HD), cos_b, sin_b)
            kd = apply_rope(fk.reshape(Bsz, S, DIFF_HEADS, 2, DIFF_HD), cos_b, sin_b)
            o_b = diff_attention(qd, kd, fv.reshape(Bsz, S, DIFF_HEADS, 2 * DIFF_HD), lam)
            o_b = (rmsnorm(o_b, even_diff_subln[e]) * (1.0 - lam_init)).reshape(Bsz, S, DIFF_V)
            x = x + jnp.concatenate([o_a, o_b], axis=-1) @ even_w_out[e]
        else:
            o_i = i // 2
            h = rmsnorm(x, odd_norm_mix[o_i])
            cq, ck, cv = split_cols(h @ odd_w_qkv[o_i], (D_MODEL, D_MODEL, D_MODEL))
            shp = (Bsz, S, CA_HEADS, CA_HD)
            o_c = chunk_band_attention(cq.reshape(shp), ck.reshape(shp), cv.reshape(shp), odd_rel_bias[o_i])
            x = x + o_c @ odd_w_out[o_i]
        h = rmsnorm(x, ffn_norm[i])
        x = x + conv_gated_mlp(h, ffn_w_in[i], ffn_conv_w[i], ffn_conv_b[i], ffn_w_out[i])
    return rmsnorm(x, final_norm)


_drawn_inputs = setup_inputs


def setup_inputs(seed=0):
    import zlib

    import numpy as np

    out = dict(_drawn_inputs(seed))
    spreads = {}
    factors = {'even_dn_norm': 6.875,
     'even_diff_subln': 4.756,
     'odd_norm_mix': 8.0,
     'odd_rel_bias': 3.428,
     'ffn_norm': 3.089,
     'ffn_conv_b': 8.0,
     'final_norm': 2.828}
    for name, (base, spread) in spreads.items():
        noise = np.random.default_rng([zlib.crc32(name.encode()), seed]).standard_normal(out[name].shape)
        drawn = base * np.exp(spread * noise) if base else spread * noise
        out[name] = __import__('jax').numpy.asarray(drawn.astype(out[name].dtype))
    for name, factor in factors.items():
        out[name] = (out[name] * factor).astype(out[name].dtype)
    return out
```

```python
import math
from contextlib import ExitStack

import numpy as np

import concourse.bass as bass
from concourse import mybir

F32 = mybir.dt.float32
R32 = mybir.dt.float32r
ALU = mybir.AluOpType
ACT = mybir.ActivationFunctionType

P = 128
S = 512
NB = S // P
D = 1024
KD = D // P
FF = 2816
JF = FF // P
HALVES = ((0, 12), (12, 10))
NH = 4
HD = 64
NPAIR = 8
EPS = 1e-6
QSCALE = HD ** -0.5
LAM_INIT = 0.8 - 0.6 * math.exp(0.0)
NEG = -1e30
REL = 256
GLEN = 640
ALPHA = 4

C_Q, C_K, C_V, C_AB, C_GATE, C_FQ, C_FK, C_FV = 0, 512, 1024, 1536, 1544, 2056, 2568, 3080

PV_EVEN, PV_FFN, PV_ODD, PV_FIN, PV_DNC, PV_DNN, PV_SUB = 0, 8, 24, 32, 40, 88, 89
PV_CW = (P, 2 * P)
PV_CB = P + 66
PV_NORM = (PV_EVEN, PV_FFN, PV_ODD, PV_FFN + 8, PV_FIN)

C_ID, C_ONE, C_TRIU, C_STRICT, C_M16, C_M32, C_M64, C_M128, C_PERM = range(9)
C_COS, C_SIN, C_MASK = 9 * P, 9 * P + S, 9 * P + 2 * S
C_WIDTH = 9 * P + 3 * S


def constants():
    i = np.arange(P)
    row, col = i[:, None], i[None, :]
    c = np.zeros((P, C_WIDTH), np.float32)

    def put(n, m):
        c[:, n * P:(n + 1) * P] = m

    put(C_ID, row == col)
    put(C_ONE, 1.0)
    put(C_TRIU, row <= col)
    put(C_STRICT, col < row)
    put(C_M16, row // 16 == col // 16)
    for n, w in ((C_M32, 32), (C_M64, 64), (C_M128, 128)):
        put(n, (row // w == col // w) & (row // (w // 2) != col // (w // 2)))
    put(C_PERM, row == (col ^ 32))
    inv = np.float32(1.0) / np.power(np.float32(10000.0), np.arange(0, HD, 2, dtype=np.float32) / np.float32(HD))
    ang = np.arange(S, dtype=np.float32)[:, None] * inv[None, :].astype(np.float32)
    cos, sin = np.cos(ang).T, np.sin(ang).T
    c[:, C_COS:C_COS + S] = np.concatenate([cos] * 4)
    c[:, C_SIN:C_SIN + S] = np.concatenate([-sin, sin] * 2)
    c[:64, C_MASK + 448:C_MASK + 512] = NEG
    return c


DN_JOBS = [("sq_q", 0), ("sq_k", 1), ("grow", 2), ("gcol", 3), ("kk", 0), ("qk", 1), ("ktok", 2), ("vtok", 3),
           ("At", 0), ("A2", 1), ("A2t", 2), ("U1", 3), ("A4", 0), ("A4t", 1), ("U2", 2), ("A8", 3), ("U3", 0),
           ("T16", 1), ("Y16", 2), ("X16", 3), ("T32", 0), ("Y32", 1), ("X32", 2), ("T64", 3), ("Y64", 0), ("X64", 1),
           ("u", 2), ("wT", 3), ("o", 0), ("kv0", 1), ("ws1", 2), ("kv1", 3), ("ws2", 1), ("kv2", 2), ("ws3", 3),
           ("sq_o", 1)]
DIFF_JOBS = [(f"s{j}", j % 2) for j in range(8)] + [(f"t{b}", 2) for b in range(4)] + [("sq_o", 2), ("pv", 3)] \
    + [("rot_q", 0), ("rot_k", 1)]
ODD_JOBS = [(f"s{j}", j % 2) for j in range(8)] + [(f"t{j}", 2) for j in range(8)] + [("pv", 3)]
XT_JOBS = [(f"x{k}", k % 4) for k in range(KD)]
NORM_JOBS = [("row", 0), ("col", 1)]
AB_JOBS = [("ab", 2)]


class Bank:

    def __init__(self):
        self.base, self.at = {}, [0] * 4

    def phase(self, name, jobs, times, lead=()):
        for j in lead:
            self.at[dict(jobs)[j]] += 1
        self.base[name] = (list(self.at), jobs)
        for _, b in jobs:
            self.at[b] += times
        for j in lead:
            self.at[dict(jobs)[j]] -= 1

    def use(self, phase, job, i):
        base, jobs = self.base[phase]
        b = dict(jobs)[job]
        mine = [n for n, bank in jobs if bank == b]
        return b, base[b] + len(mine) * i + mine.index(job)


BANK = Bank()
BANK.phase("xt", XT_JOBS, 1)
BANK.phase("norm0", NORM_JOBS, 1)
BANK.phase("ab", AB_JOBS, 1)
BANK.phase("dn", DN_JOBS, NH)
BANK.phase("diff", DIFF_JOBS, NH, lead=("rot_q", "rot_k"))
BANK.phase("norm1", NORM_JOBS, 1)
BANK.phase("norm2", NORM_JOBS, 1)
BANK.phase("odd", ODD_JOBS, NPAIR)
BANK.phase("norm3", NORM_JOBS, 1)
BANK.phase("norm4", NORM_JOBS, 1)
BANK.phase("yt", XT_JOBS, 1)

_turns = [("dn", NH), ("diff", NH), ("out0", 2)]
for _l in (0, 1):
    if _l:
        _turns += [("odd", NPAIR), ("out1", 2)]
    for _n, (_, _c) in enumerate(HALVES):
        _turns += [(f"in{_l}{_n}", _c // 2), (f"ff{_l}{_n}", 4)]
UNIT = {}
_at = 0
for _name, _n in _turns:
    UNIT[_name] = _at
    _at += _n
UNITS = _at


def build(nc, T, out):
    ctx = ExitStack()
    with ctx:
        def sb(name, shape, dt=F32, where=ctx):
            return where.enter_context(nc.sbuf_tensor(name, shape, dt))

        sems = {}

        def sem(name):
            if name not in sems:
                sems[name] = ctx.enter_context(nc.semaphore(name))
            return sems[name]

        x = sb("x", [P, KD, S])
        mh = sb("mh", [P, KD, S], R32)
        ml = sb("ml", [P, KD, S], R32)
        raw = [sb(f"raw{s}", [P, 2048]) for s in (0, 1)]
        wh = [sb(f"wh{s}", [P, 2048], R32) for s in (0, 1)]
        wl = [sb(f"wl{s}", [P, 2048], R32) for s in (0, 1)]
        cst = sb("cst", [P, C_WIDTH])
        pv = sb("pv", [P, 3 * P])
        rstd = sb("rstd", [P, S])
        rcol = sb("rcol", [P, NB])
        sdc = sb("sdc", [P, NB])
        ssum = sb("ssum", [P, S])
        sq = [sb(f"sq{s}", [P, S]) for s in (0, 1)]
        cb = [sb(f"cb{s}", [P, ALPHA + S]) for s in (0, 1)]
        cta = [sb(f"cta{s}", [P, S]) for s in (0, 1)]
        epsc = sb("epsc", [P, 1])

        gall = sb("gall", [P, NH, NB], F32, ctx)
        ball = sb("ball", [P, NH, NB], F32, ctx)
        lamc = sb("lamc", [P, 1], F32, ctx)
        abw = sb("abw", [P, KD, 8], F32, ctx)
        abh = sb("abh", [P, KD, 8], R32, ctx)
        abl = sb("abl", [P, KD, 8], R32, ctx)
        abz = sb("abz", [P, NB, 8], F32, ctx)
        abt = [sb(f"abt{n}", [P, NB, NH], F32, ctx) for n in range(5)]
        dtb = sb("dtb", [P, NH], F32, ctx)
        alog = sb("alog", [P, NH], F32, ctx)
        lp = sb("lp", [P, 256], F32, ctx)
        lt = sb("lt", [P, 2, HD], F32, ctx)
        ls = sb("ls", [P, 4], F32, ctx)
        sub8 = sb("sub8", [P, 1])

        def cblk(n):
            return cst[:, n * P:(n + 1) * P]

        ident, ones, triu = cblk(C_ID), cblk(C_ONE), cblk(C_TRIU)

        def rows(a):
            return a.unsqueeze(1).broadcast_to([P, NB, P])

        def cols(a):
            return a.unsqueeze(2).broadcast_to([P, NB, P])

        def blk(t):
            return t.rearrange("p (b n) -> p b n", b=NB)

        start = ExitStack()
        xin = sb("xin", [P, NB, D], F32, start)
        prow = sb("prow", [P, 3, P], F32, start)
        start.close()
        mixer = ExitStack()
        oh = sb("oh", [P, KD, S], R32, mixer)
        ol = sb("ol", [P, KD, S], R32, mixer)
        mix = ExitStack()
        d = {n: sb("dn_" + n, [P, S], F32, mix)[:, :] for n in
             ("qT", "kT", "vT", "gN", "gC", "sqq", "sqk", "qh", "kh", "decT", "decN", "qd", "qkD",
              "N", "A", "E32", "E64", "At", "A2", "A2t", "U")}
        for new, old in (("gbc", "decT"), ("kd", "kh"), ("kbg", "qh"), ("vb", "decN"), ("E128", "N"), ("A4", "A"),
                         ("A4t", "At"), ("A8", "A2"), ("T", "decT"), ("Y", "A2t"), ("wT", "E32"), ("u", "E64"),
                         ("sqo", "sqq"), ("on", "A")):
            d[new] = d[old]
        gh = sb("gh", [P, NB], F32, mix)
        gc = sb("gc", [P, 3 * NB], F32, mix)
        eg = sb("eg", [P, 3 * NB], F32, mix)
        be = sb("be", [P, NB], F32, mix)
        vn = sb("vn", [P, P], F32, mix)
        st = sb("st", [P, P], F32, mix)
        mix.close()
        att = ExitStack()
        qr0 = sb("qr0", [P, S], F32, att)
        qr1 = sb("qr1", [P, S], F32, att)
        av = sb("av", [P, NB, P], F32, att)
        qc0 = sb("qc0", [P, S], F32, att)
        aq = sb("aq", [P, S], F32, att)
        ak = sb("ak", [P, S], F32, att)
        qc1 = sb("qc1", [P, S], F32, att)
        qr, qc = [qr0, qr1], [qc0, qc1]
        ns2 = sb("ns", [P, 2 * S], F32, att)
        pr2 = sb("pr", [P, 2 * S], F32, att)
        ns = [ns2[:, n * S:(n + 1) * S] for n in (0, 1)]
        pr = [pr2[:, n * S:(n + 1) * S] for n in (0, 1)]
        pn = [sb(f"pn{n}", [P, S], F32, att) for n in (0, 1)]
        pT = [sb(f"pT{n}", [P, S], F32, att) for n in (0, 1)]
        gb = [sb(f"gb{n}", [P, S], F32, att) for n in (0, 1)]
        osb = sb("osb", [P, S], F32, att)
        osd = sb("osd", [P, S], F32, att)
        nm = sb("nm", [P, 8], F32, att)
        rs = sb("rs", [P, 8], F32, att)
        rr = sb("rr", [P, 8], F32, att)
        rb, fx = ns2[0:16, 0:2 * REL + 1], pr2[0:16, 0:GLEN]
        att.close()
        mixer.close()
        mlp = ExitStack()
        ah = sb("ah", [P, 12, S], R32, mlp)
        al = sb("al", [P, 12, S], R32, mlp)
        sl = [sb(f"sl{s}", [P, S], F32, mlp) for s in (0, 1)]
        ur = [sb(f"ur{s}", [P, S], F32, mlp) for s in (0, 1)]
        pd = [sb(f"pd{s}", [P, S], F32, mlp) for s in (0, 1)]
        mlp.close()
        end = ExitStack()
        ob = [sb(f"ob{s}", [P, NB, P], F32, end) for s in (0, 1)]
        end.close()

        gscr = nc.dram_tensor("rel_bias_extended", (16, P, GLEN), F32).ap()

        acc = [ctx.enter_context(nc.psum_tensor(f"acc{n}", [P, S], F32)) for n in range(4)]
        R = [ctx.enter_context(nc.psum_tensor(f"R{n}", [P, S], F32)) for n in range(4)]

        block = ctx.enter_context(nc.Block())

        def full(eng, phase, job, i):
            b, n = BANK.use(phase, job, i)
            eng.wait_ge(sem(f"R{b}_full"), n + 1)
            return R[b]

        def free(ins, phase, job, i):
            b, _ = BANK.use(phase, job, i)
            ins.then_inc(sem(f"R{b}_read"), 1)

        def read(eng, phase, job, i):
            b, n = BANK.use(phase, job, i)
            eng.wait_ge(sem(f"R{b}_read"), n + 1)

        def settled(eng, *waits):
            values = [v if isinstance(v, int) else eng.to_reg(v) for _, v in waits]
            eng.wait_ge(sem("cst_in"), 16)
            for (name, _), v in zip(waits, values):
                eng.wait_ge(sem(name), v)

        def is_full(phase, job, i):
            b, n = BANK.use(phase, job, i)
            return f"R{b}_full", n + 1

        def is_read(phase, job, i):
            b, n = BANK.use(phase, job, i)
            return f"R{b}_read", n + 1

        def dyn(t, k):
            return t[:, k, :] if isinstance(k, int) else t[:, bass.ds(k, 1), :].squeeze(1)

        def units_split_act(act, s, g):
            act.wait_ge(sem(f"raw_full{s}"), 32 * (g + 1))
            if not (isinstance(g, int) and g == 0):
                act.wait_ge(sem(f"tile_full{s}"), 2 * g)
            nc.scalar.activation(wh[s][:, :], raw[s][:, :], ACT.Copy).then_inc(sem(f"w_head{s}"), 1)

        def units_split_dve(dve, s, g):
            dve.wait_ge(sem(f"w_head{s}"), g + 1)
            nc.vector.tensor_tensor(wl[s][:, :], raw[s][:, :], wh[s][:, :].bitcast(F32),
                                    ALU.subtract).then_inc(sem(f"w_tail{s}"), 1)

        @block.sync
        def _(sp):
            def load(s, g, pieces):
                if not (isinstance(g, int) and g == 0):
                    sp.wait_ge(sem(f"w_tail{s}"), g)
                for dst, src in pieces:
                    sp.dma_start(dst, src).then_inc(sem(f"raw_full{s}"), 16)

            def pair(s, w, c0, c1):
                v = raw[s][:, :].rearrange("p (t k n) -> p t k n", t=2, k=KD)
                wv = w.rearrange("(k p) n -> p k n", p=P)
                return [(v[:, 0, :, :], wv[:, :, bass.ds(c0, P)]), (v[:, 1, :, :], wv[:, :, bass.ds(c1, P)])]

            def one(s, w, c0):
                v = raw[s][:, 0:KD * P].rearrange("p (k n) -> p k n", k=KD)
                wv = w.rearrange("(k p) n -> p k n", p=P)
                return [(v[:, 0:4, :], wv[:, 0:4, bass.ds(c0, P)]), (v[:, 4:8, :], wv[:, 4:8, bass.ds(c0, P)])]

            def down(s, w, j0, count, c0):
                v = raw[s][:, 0:count * P].rearrange("p (k n) -> p k n", k=count)
                wv = w[j0 * P:(j0 + count) * P, :].rearrange("(k p) n -> p k n", p=P)
                h = count // 2
                return [(v[:, 0:h, :], wv[:, 0:h, bass.ds(c0, P)]), (v[:, h:count, :], wv[:, h:count, bass.ds(c0, P)])]

            sp.dma_start(cst[:, :], T["consts"]).then_inc(sem("cst_in"), 16)
            xv = T["x"][0].rearrange("(b p) d -> p b d", p=P)
            for b in range(NB):
                sp.dma_start(xin[:, b, :], xv[:, b, :]).then_inc(sem("x_in"), 16)
            w0 = T["even_w_in"][0]
            load(0, 0, pair(0, w0, C_Q, C_K))
            load(1, 0, pair(1, w0, C_V, C_GATE))
            with sp.Fori(1, NH) as i:
                load(0, i, pair(0, w0, i * P + C_Q, i * P + C_K))
                load(1, i, pair(1, w0, i * P + C_V, i * P + C_GATE))
            with sp.Fori(0, NH) as i:
                load(0, i + UNIT["diff"], pair(0, w0, i * P + C_FQ, i * P + C_FK))
                load(1, i + UNIT["diff"], one(1, w0, i * P + C_FV))

            def out_proj(w, base):
                with sp.Fori(0, 2) as i:
                    for s in (0, 1):
                        load(s, i + base, pair(s, w, i * 512 + 256 * s, i * 512 + 256 * s + P))

            def mlp_loads(layer):
                wi, wo = T["ffn_w_in"][layer], T["ffn_w_out"][layer]
                for n, (j0, count) in enumerate(HALVES):
                    with sp.Fori(0, count // 2) as i:
                        for s in (0, 1):
                            c = i * 256 + (j0 + s) * P
                            load(s, i + UNIT[f"in{layer}{n}"], pair(s, wi, c, c + FF))
                    with sp.Fori(0, 4) as i:
                        for s in (0, 1):
                            load(s, i + UNIT[f"ff{layer}{n}"], down(s, wo, j0, count, i * 256 + s * P))

            out_proj(T["even_w_out"][0], UNIT["out0"])
            mlp_loads(0)
            wq = T["odd_w_qkv"][0]
            with sp.Fori(0, NPAIR) as i:
                load(0, i + UNIT["odd"], pair(0, wq, i * P, i * P + D))
                load(1, i + UNIT["odd"], one(1, wq, i * P + 2 * D))
            out_proj(T["odd_w_out"][0], UNIT["out1"])
            mlp_loads(1)
            ov = out.rearrange("(b p) (k n) -> p b k n", p=P, n=P)
            for k in range(KD):
                read(sp, "yt", f"x{k}", 0)
                sp.dma_start(ov[:, :, k, :], ob[k % 2][:, :, :]).then_inc(sem(f"out_done{k % 2}"), 16)
            for s in (0, 1):
                sp.wait_ge(sem(f"out_done{s}"), 16 * KD // 2)

        @block.gpsimd
        def _(pool):
            def pdma(dst, src):
                pool.dma_start(dst, src).then_inc(sem("p_in"), 16)

            def vec(src, r0, t):
                n = src.shape[0]
                pdma(prow[r0:r0 + n, t, :], src)

            v = "(k p) -> k p"
            vec(T["even_norm_mix"][0].rearrange(v, p=P), PV_EVEN, 0)
            for l in (0, 1):
                vec(T["ffn_norm"][l].rearrange(v, p=P), PV_FFN + 8 * l, 0)
            vec(T["odd_norm_mix"][0].rearrange(v, p=P), PV_ODD, 0)
            vec(T["final_norm"].rearrange(v, p=P), PV_FIN, 0)
            vec(T["even_dn_conv"][0].rearrange("t (k p) -> (t k) p", p=P), PV_DNC, 0)
            vec(T["even_dn_norm"], PV_DNN, 0)
            vec(T["even_diff_subln"], PV_SUB, 0)
            vec(T["ffn_conv_w"][0].rearrange("t (k p) -> (t k) p", p=P), 0, 1)
            vec(T["ffn_conv_b"].rearrange("l (k p) -> (l k) p", p=P), 66, 1)
            vec(T["ffn_conv_w"][1].rearrange("t (k p) -> (t k) p", p=P), 0, 2)
            pdma(dtb[:, :], T["even_dn_dt_bias"].broadcast_to([P, NH]))
            pdma(alog[:, :], T["even_dn_A_log"].broadcast_to([P, NH]))
            pdma(lp[:, :], T["even_diff_lambda"].rearrange("a b c -> a (b c)").broadcast_to([P, 256]))
            pdma(abw[:, :, :], T["even_w_in"][0].rearrange("(k p) n -> p k n", p=P)[:, :, C_AB:C_AB + 8])
            for s in (0, 1):
                pool.memset(cb[s][:, 0:ALPHA], 0.0).then_inc(sem("zeros"), 1)
            pool.memset(epsc[:, :], EPS).then_inc(sem("zeros"), 1)

            def sum_squares(norm):
                if norm:
                    read(pool, f"norm{norm - 1}", "col", 0)
                pool.memset(ssum[:, :], 0.0).then_inc(sem("ssum"), 1)
                with pool.Fori(0, KD // 2) as i:
                    for s in (0, 1):
                        pool.wait_ge(sem("sq_full"), 2 * i + (KD * norm + s + 1))
                        pool.wait_ge(sem("ssum"), 2 * i + (9 * norm + s + 1))
                        pool.tensor_tensor(ssum[:, :], ssum[:, :], sq[s][:, :], ALU.add).then_inc(sem("ssum"), 1)

            sum_squares(0)

            with pool.Fori(0, NH) as i:
                settled(pool, ("gate_full", i + 1), ("o_tail", i + 1))
                pool.tensor_copy(d["gC"], d["gN"]).then_inc(sem("gC_full"), 1)
                pool.wait_ge(sem("eT"), i + 1)
                pool.tensor_tensor(blk(d["decT"]), blk(d["decT"]), rows(triu), ALU.mult).then_inc(sem("decT"), 1)
                pool.wait_ge(sem("eN"), i + 1)
                pool.tensor_tensor(blk(d["decN"]), blk(d["decN"]), rows(cblk(C_STRICT)), ALU.mult)\
                    .then_inc(sem("decN"), 1)
                pool.wait_ge(sem("qh"), i + 1)
                read(pool, "dn", "grow", i)
                pool.tensor_tensor(d["qd"], d["qd"], d["qh"], ALU.mult).then_inc(sem("qd"), 1)
                pool.wait_ge(sem("N"), i + 1)
                for n, (e, m) in enumerate((("A", C_M16), ("E32", C_M32), ("E64", C_M64), ("E128", C_M128))):
                    if e == "E128":
                        pool.wait_ge(sem("A_E"), 4 * i + 3)
                    pool.tensor_tensor(blk(d[e]), blk(d["N"]), rows(cblk(m)), ALU.mult).then_inc(sem("A_E"), 1)

            pool.wait_ge(sem("A_E"), 4 * NH)
            with pool.Fori(0, NH) as i:
                for n in (0, 1):
                    pool.wait_ge(sem("acc_free0"), 2 * i + (2 * UNIT["diff"] + n + 1))
                    pool.tensor_tensor(qc[n][:, :], qr[n][:, :], cst[:, C_COS:C_COS + S], ALU.mult)\
                        .then_inc(sem("qc_full"), 1)

            pool.wait_ge(sem("R3_full"), BANK.use("diff", "pv", NH - 1)[1] + 1)
            pool.dma_start(rb, T["odd_rel_bias"][0]).then_inc(sem("rb_in"), 16)
            pool.wait_ge(sem("rb_in"), 16)
            pool.tensor_copy(fx[:, 255:GLEN - 1], rb[:, 0:384]).then_inc(sem("fx"), 1)
            pool.tensor_copy(fx[:, 0:255], rb[:, 0:1].broadcast_to([16, 255])).then_inc(sem("fx"), 1)
            pool.memset(fx[:, GLEN - 1:GLEN], 0.0).then_inc(sem("fx"), 1)
            pool.wait_ge(sem("fx"), 3)
            pool.dma_start(gscr, fx.unsqueeze(1).broadcast_to([16, P, GLEN])).then_inc(sem("fx_out"), 16)
            pool.wait_ge(sem("fx_out"), 16)

            sum_squares(1)
            sum_squares(2)

            def load_bias(m, head):
                row = gscr[bass.ds(head, 1), :, :]
                for p0, p1, n in ((0, 64, 448), (64, P, S)):
                    src = bass.AP(tensor=row.tensor, offset=row.offset + (127 + p0 * (GLEN - 1)),
                                  ap=[[GLEN - 1, p1 - p0], [1, n]])
                    pool.dma_start(gb[m][p0:p1, 0:n], src).then_inc(sem(f"gb_full{m}"), 16)

            for m in (0, 1):
                pool.memset(gb[m][0:64, 448:S], NEG).then_inc(sem("gb_mask"), 1)
                load_bias(m, m)
            with pool.Fori(1, NPAIR) as i:
                for m in (0, 1):
                    read(pool, "odd", f"s{4 * m + 3}", i - 1)
                    load_bias(m, 2 * i + m)
            sum_squares(3)
            sum_squares(4)

        @block.tensor
        def _(pe):
            def job(phase, name, i, first=True):
                b, n = BANK.use(phase, name, i)
                if not (isinstance(n, int) and n == 0):
                    pe.wait_ge(sem(f"R{b}_read"), n)
                return R[b]

            def done(ins, phase, name, i):
                b, _ = BANK.use(phase, name, i)
                ins.then_inc(sem(f"R{b}_full"), 1)

            def mm3(o, ah_, al_, bh_, bl_, first, last):
                nc.tensor.matmul(o, ah_, bh_, start=first, stop=False)
                nc.tensor.matmul(o, ah_, bl_, start=False, stop=False)
                return nc.tensor.matmul(o, al_, bh_, start=False, stop=last)

            def begin(s, g):
                pe.wait_ge(sem(f"w_tail{s}"), g + 1)
                if not (isinstance(g, int) and g == 0):
                    pe.wait_ge(sem(f"acc_free{s}"), 2 * g)

            def features(s, g, mov, tiles=2, kn=KD, norm=None, srcwait=None):
                begin(s, g)
                ws = [w[s][:, 0:tiles * kn * P].rearrange("p (t k n) -> p t k n", t=tiles, k=kn) for w in (wh, wl)]
                for t in range(tiles):
                    for k in range(kn):
                        if norm is not None and s == 0 and t == 0:
                            pe.wait_ge(sem("m_tail"), KD * norm + k + 1)
                        if srcwait is not None and t == 0:
                            srcwait(k)
                        last = mm3(acc[2 * s + t][:, :], ws[0][:, t, k, :], ws[1][:, t, k, :],
                                   mov[0][:, k, :], mov[1][:, k, :], k == 0, k == kn - 1)
                        if k == kn - 1:
                            last.then_inc(sem(f"tile_full{s}"), 3 - tiles)
                        yield

            def tokens(s, g):
                begin(s, g)
                ws = [w[s][:, 0:KD * P].rearrange("p (k n) -> p k n", k=KD) for w in (wh, wl)]
                for b in range(NB):
                    t = slice(b * P, (b + 1) * P)
                    for k in range(KD):
                        last = mm3(acc[2 * s][:, t], mh[:, k, t], ml[:, k, t], ws[0][:, k, :], ws[1][:, k, :],
                                   k == 0, k == KD - 1)
                    if b == NB - 1:
                        last.then_inc(sem(f"tile_full{s}"), 2)
                    yield

            def both(a, b):
                yield from a
                yield from b

            def run(gen, n=1000):
                for _ in range(n):
                    if next(gen, 0) == 0:
                        return

            def norm_sums(n):
                ph = f"norm{n}"
                pe.wait_ge(sem("ssum"), 9 * n + 9)
                r = job(ph, "row", 0)
                done(nc.tensor.matmul(r[:, :], ones, ssum[:, :], start=True, stop=True), ph, "row", 0)
                r = job(ph, "col", 0)
                for b in range(NB):
                    last = nc.tensor.matmul(r[:, b:b + 1], ssum[:, b * P:(b + 1) * P], ones[:, 0:1],
                                            start=True, stop=True)
                done(last, ph, "col", 0)

            pe.wait_ge(sem("cst_in"), 16)
            pe.wait_ge(sem("x_in"), 64)
            for k in range(KD):
                r = job("xt", f"x{k}", 0)
                for b in range(NB):
                    last = nc.tensor.transpose(r[:, b * P:(b + 1) * P], xin[:, b, k * P:(k + 1) * P], ident)
                done(last, "xt", f"x{k}", 0)
            pe.wait_ge(sem("p_in"), 16 * 15)
            for t, n in ((0, 90), (1, 110), (2, 66)):
                last = nc.tensor.transpose(acc[0][:, t * P:t * P + n], prow[0:n, t, :], cst[0:n, 0:n])
            last.then_inc(sem("pv_full"), 1)
            norm_sums(0)

            pe.wait_ge(sem("ab_split"), 1)
            pe.wait_ge(sem("m_tail"), KD)
            r = job("ab", "ab", 0)
            for b in range(NB):
                t = slice(b * P, (b + 1) * P)
                for k in range(KD):
                    last = mm3(r[:, b * 8:b * 8 + 8], mh[:, k, t], ml[:, k, t], abh[:, k, :], abl[:, k, :],
                               k == 0, k == KD - 1)
            done(last, "ab", "ab", 0)

            def dn_units(g):
                return both(features(0, g, (mh, ml)), features(1, g, (mh, ml)))

            def dn_head(i, fill):
                def each(name, a, b, need=(), tr=False):
                    for s_, v_ in need:
                        pe.wait_ge(sem(s_), v_)
                    r = job("dn", name, i)
                    for n in range(NB):
                        t = slice(n * P, (n + 1) * P)
                        lhs = a if a is ones else a[:, t]
                        if tr:
                            last = nc.tensor.transpose(r[:, t], lhs, ident)
                        else:
                            last = nc.tensor.matmul(r[:, t], lhs, triu if b is triu else b[:, t], start=True, stop=True)
                    done(last, "dn", name, i)
                    run(fill, 1)

                for n, src in (("sq_q", "sqq"), ("sq_k", "sqk")):
                    pe.wait_ge(sem(src), i + 1)
                    r = job("dn", n, i)
                    done(nc.tensor.matmul(r[:, :], ones, d[src], start=True, stop=True), "dn", n, i)
                    run(fill, 1)
                each("grow", d["gbc"], triu, [("gbc", i + 1)])
                r = job("dn", "gcol", i)
                nc.tensor.matmul(r[:, 0:NB], triu, gh[:, :], start=True, stop=True)
                done(nc.tensor.matmul(r[:, NB:2 * NB], ones, gh[:, :], start=True, stop=True), "dn", "gcol", i)
                run(fill, 2)
                each("kk", d["kh"], d["kh"], [("kh", i + 1)])
                each("qk", d["kh"], d["qh"], [("qh", i + 1)])
                each("ktok", d["kh"], None, tr=True)
                each("vtok", d["vT"], None, tr=True)
                each("At", d["A"], None, [("A_E", 4 * i + 1)], tr=True)
                read(pe, "dn", "At", i)
                each("A2", d["At"], d["A"])
                each("A2t", d["A"], d["At"])
                read(pe, "dn", "A2", i)
                pe.wait_ge(sem("U0"), i + 1)
                each("U1", d["A2"], d["U"])
                read(pe, "dn", "A2t", i)
                each("A4", d["A2t"], d["A2"])
                each("A4t", d["A2"], d["A2t"])
                read(pe, "dn", "U1", i)
                read(pe, "dn", "A4", i)
                each("U2", d["A4"], d["U"])
                read(pe, "dn", "A4t", i)
                each("A8", d["A4t"], d["A4"])
                read(pe, "dn", "U2", i)
                read(pe, "dn", "A8", i)
                each("U3", d["A8"], d["U"])
                last = "U3"
                pe.wait_ge(sem("A_E"), 4 * i + 4)
                for w, e in (("16", "E32"), ("32", "E64"), ("64", "E128")):
                    read(pe, "dn", last, i)
                    each("T" + w, d["U"], None, tr=True)
                    each("Y" + w, d[e], d["U"])
                    read(pe, "dn", "T" + w, i)
                    read(pe, "dn", "Y" + w, i)
                    each("X" + w, d["T"], d["Y"])
                    last = "X" + w
                read(pe, "dn", last, i)
                read(pe, "dn", "vtok", i)
                each("u", d["U"], d["vb"])
                read(pe, "dn", "ktok", i)
                each("wT", d["kbg"], d["U"])
                o = job("dn", "o", i)
                pe.wait_ge(sem("qd"), i + 1)
                read(pe, "dn", "qk", i)
                for b in range(NB):
                    t = slice(b * P, (b + 1) * P)
                    if b:
                        read(pe, "dn", f"kv{b - 1}", i)
                        if b == 1:
                            read(pe, "dn", "wT", i)
                        r = job("dn", f"ws{b}", i)
                        done(nc.tensor.matmul(r[:, 0:P], d["wT"][:, t], st[:, :], start=True, stop=True),
                             "dn", f"ws{b}", i)
                        nc.tensor.matmul(o[:, t], st[:, :], d["qd"][:, t], start=True, stop=False)
                        run(fill, 1)
                    if b:
                        read(pe, "dn", f"ws{b}", i)
                    else:
                        pe.wait_ge(sem("vn"), i + 1)
                    if b < NB - 1:
                        r = job("dn", f"kv{b}", i)
                        done(nc.tensor.matmul(r[:, 0:P], d["kd"][:, t], vn[:, :], start=True, stop=True),
                             "dn", f"kv{b}", i)
                    last = nc.tensor.matmul(o[:, t], vn[:, :], d["qkD"][:, t], start=(b == 0), stop=True)
                    if b == NB - 1:
                        done(last, "dn", "o", i)
                    else:
                        last.then_inc(sem("o_step"), 1)
                    run(fill, 1)
                run(fill)
                pe.wait_ge(sem("sqo_dn"), i + 1)
                r = job("dn", "sq_o", i)
                done(nc.tensor.matmul(r[:, :], ones, d["sqo"], start=True, stop=True), "dn", "sq_o", i)

            def rope_products(i):
                for n, nm_ in enumerate(("rot_q", "rot_k")):
                    pe.wait_ge(sem("acc_free0"), 2 * i + (2 * UNIT["diff"] + n + 3))
                    r = job("diff", nm_, i)
                    done(nc.tensor.matmul(r[:, :], cblk(C_PERM), qr[n][:, :], start=True, stop=True),
                         "diff", nm_, i)

            def attention(ph, i, fill):
                diff = ph == "diff"
                items = [(m, b) for b in range(NB) for m in (0, 1)] if diff else \
                    [(m, b) for m in (0, 1) for b in range(NB)]
                trs = [b for b in range(NB)] if diff else list(range(8))
                if diff:
                    pe.wait_ge(sem("roped"), 2 * i + 2)
                else:
                    pe.wait_ge(sem("acc_free0"), 2 * i + (2 * UNIT[ph] + 2))
                pe.wait_ge(sem("acc_free1"), 2 * i + (2 * UNIT[ph] + 2))
                o = None
                per = 4 if diff else 8
                for t in range(8 + 4):
                    if t < 8:
                        m, b = items[t]
                        r = job(ph, f"s{t}", i)
                        rw = slice(HD * m, HD * m + HD)
                        done(nc.tensor.matmul(r[:, 0:(b + 1) * P], aq[rw, b * P:(b + 1) * P], ak[rw, 0:(b + 1) * P],
                                              start=True, stop=True), ph, f"s{t}", i)
                    run(fill, 2 if t < 8 else 1)
                    z = (t - 3) // 2 if diff and (t - 3) % 2 == 0 else t - 2 if not diff else -1
                    if 0 <= z < per:
                        b = z if diff else items[z][1]
                        pe.wait_ge(sem("pn_" + ph), per * i + z + 1)
                        r = job(ph, f"t{z}", i)
                        for k in range(b + 1):
                            last = nc.tensor.transpose(r[:, k * P:(k + 1) * P], pn[z % 2][:, k * P:(k + 1) * P], ident)
                        done(last, ph, f"t{z}", i)
                    y = (t - 4) // 2 if diff and (t - 4) % 2 == 0 else t - 3 if not diff else -1
                    if 0 <= y < per:
                        b = y if diff else items[y][1]
                        if o is None:
                            o = job(ph, "pv", i)
                        read(pe, ph, f"t{y}", i)
                        if diff:
                            dst, vc = o[:, b * P:(b + 1) * P], slice(0, P)
                        else:
                            m = items[y][0]
                            dst, vc = o[HD * m:HD * m + HD, b * P:(b + 1) * P], slice(HD * m, HD * m + HD)
                        for k in range(b + 1):
                            last = nc.tensor.matmul(dst, av[:, k, vc], pT[y % 2][:, k * P:(k + 1) * P],
                                                    start=(k == 0), stop=(k == b))
                        if y == per - 1:
                            done(last, ph, "pv", i)
                        else:
                            last.then_inc(sem("pv_" + ph), 1)
                run(fill)
                if diff:
                    pe.wait_ge(sem("sqo_diff"), i + 1)
                    r = job(ph, "sq_o", i)
                    done(nc.tensor.matmul(r[:, :], ones, osd[:, :], start=True, stop=True),
                         ph, "sq_o", i)

            def attn_units(g):
                return both(features(0, g, (mh, ml)), tokens(1, g))

            def out_proj(base, src, srcwait):
                for i in range(2):
                    for s in (0, 1):
                        run(features(s, base + i, src, srcwait=srcwait if (i, s) == (0, 0) else None))

            def mlp_layer(layer, norm):
                for n, (j0, count) in enumerate(HALVES):
                    g0 = UNIT[f"in{layer}{n}"]
                    if n == 0:
                        for s in (0, 1):
                            run(features(s, g0, (mh, ml), norm=norm))
                    with pe.Fori(1 if n == 0 else 0, count // 2) as i:
                        for s in (0, 1):
                            run(features(s, i + g0, (mh, ml)))
                    g0 = UNIT[f"ff{layer}{n}"]
                    before = 12 * n + JF * layer

                    def products(g, src=None):
                        for s in (0, 1):
                            run(features(s, g, (ah, al), tiles=1, kn=count, srcwait=src))

                    products(g0, lambda k: pe.wait_ge(sem("a_tail"), before + k + 1))
                    with pe.Fori(1, 4) as i:
                        products(i + g0)

            run(dn_units(0))
            with pe.Fori(0, NH - 1) as i:
                dn_head(i, dn_units(i + 1))
            dn_head(NH - 1, attn_units(UNIT["diff"]))
            rope_products(-1)
            with pe.Fori(0, NH - 1) as i:
                attention("diff", i, attn_units(i + (UNIT["diff"] + 1)))
                rope_products(i)
            attention("diff", NH - 1, iter(()))
            out_proj(UNIT["out0"], (oh, ol), lambda k: pe.wait_ge(sem("o_tail"), k + 2))
            norm_sums(1)
            mlp_layer(0, 1)
            norm_sums(2)
            run(both(features(0, UNIT["odd"], (mh, ml), norm=2), tokens(1, UNIT["odd"])))
            with pe.Fori(0, NPAIR - 1) as i:
                attention("odd", i, attn_units(i + (UNIT["odd"] + 1)))
            attention("odd", NPAIR - 1, iter(()))
            out_proj(UNIT["out1"], (oh, ol), lambda k: read(pe, "odd", "pv", k))
            norm_sums(3)
            mlp_layer(1, 3)
            norm_sums(4)
            for k in range(KD):
                r = job("yt", f"x{k}", 0)
                pe.wait_ge(sem("x_gain"), k + 1)
                for b in range(NB):
                    last = nc.tensor.transpose(r[:, b * P:(b + 1) * P], x[:, k, b * P:(b + 1) * P], ident)
                done(last, "yt", f"x{k}", 0)

        @block.scalar
        def _(act):
            A = nc.scalar.activation

            def x_tile(norm, k, s):
                g = pv[:, bass.ds(k + PV_NORM[norm], 1)]
                if norm < 4:
                    A(dyn(mh, k), dyn(x, k), ACT.Copy, scale=g).then_inc(sem("m_head"), 1)
                settled(act, ("ssum", k + max(9 * norm, 1)))
                A(sq[s][:, :], dyn(x, k), ACT.Square).then_inc(sem("sq_full"), 1)
                if norm == 4:
                    settled(act, ("sq_full", k + (KD * norm + 1)))
                    A(dyn(x, k), dyn(x, k), ACT.Copy, scale=g).then_inc(sem("x_gain"), 1)

            def norm_roots(n):
                ph = f"norm{n}"
                if n:
                    act.wait_ge(sem("rstd"), 2 * n)
                r = full(act, ph, "row", 0)
                free(A(rstd[:, :], r[:, :], ACT.Sqrt, bias=epsc[:, :], scale=1.0 / D), ph, "row", 0)
                r = full(act, ph, "col", 0)
                free(A(sdc[:, :], r[:, 0:NB], ACT.Sqrt, bias=epsc[:, :], scale=1.0 / D), ph, "col", 0)

            for k in range(KD):
                r = full(act, "xt", f"x{k}", 0)
                free(A(x[:, k, :], r[:, :], ACT.Copy), "xt", f"x{k}", 0)
            act.wait_ge(sem("zeros"), 3)
            act.wait_ge(sem("pv_copied"), 1)
            for k in range(KD):
                read(act, "xt", f"x{k}", 0)
                x_tile(0, k, k % 2)
            act.wait_ge(sem("p_in"), 16 * 15)
            A(abh[:, :, :], abw[:, :, :], ACT.Copy).then_inc(sem("ab_head"), 1)
            for s in (0, 1):
                units_split_act(act, s, 0)
            norm_roots(0)

            act.wait_ge(sem("ab_in"), 1)
            A(abt[1][:, :, :], abt[1][:, :, :], ACT.Exp, scale=-1.0).then_inc(sem("ab_e"), 1)
            A(abt[2][:, :, :], abz[:, :, 4:8], ACT.Exp, scale=-1.0).then_inc(sem("ab_e"), 1)
            A(alog[:, :], alog[:, :], ACT.Exp).then_inc(sem("ab_e"), 1)
            A(ls[:, 0:2], ls[:, 0:2], ACT.Exp).then_inc(sem("ab_e"), 1)
            act.wait_ge(sem("ab_e"), 4)
            A(abt[1][:, :, :], abt[1][:, :, :], ACT.Ln, bias=1.0).then_inc(sem("ab_e"), 1)

            def conv(i, c, slot, g, tile, dst):
                waits = [(f"acc_free{slot}", g)]
                if c or not isinstance(i, int):
                    waits.append(("silu", 3 * i + c))
                settled(act, *waits)
                A(cta[0][:, :], cb[c % 2][:, ALPHA - 3:ALPHA - 3 + S], ACT.Copy,
                  scale=pv[:, bass.ds(i + (PV_DNC + tile), 1)]).then_inc(sem("tap"), 1)
                act.wait_ge(sem("conv"), 9 * i + (3 * c + 3))
                A(d[dst], cta[0][:, :], ACT.Silu).then_inc(sem("silu"), 1)

            def dn_evac(i, g):
                yield conv(i, 0, 0, 2 * g + 1, 0, "qT")
                conv(i, 1, 0, 2 * g + 2, 4, "kT")
                yield units_split_act(act, 0, g + 1)
                yield conv(i, 2, 1, 2 * g + 1, 8, "vT")
                act.wait_ge(sem("acc_free1"), 2 * g + 2)
                A(d["gN"], d["gN"], ACT.Silu).then_inc(sem("gate_full"), 1)
                yield units_split_act(act, 1, g + 1)

            def feat_evac(ph, g):
                yield
                yield units_split_act(act, 0, g + 1)
                yield
                yield units_split_act(act, 1, g + 1)

            def copy_out(name, dst, i):
                r = full(act, "dn", name, i)
                free(A(dst, r[:, :], ACT.Copy), "dn", name, i)

            def dn_head(i, evac):
                act.wait_ge(sem("o_tail"), i + 1)
                act.wait_ge(sem("silu"), 3 * i + 3)
                for n, src in (("sqq", "qT"), ("sqk", "kT")):
                    A(d[n], d[src], ACT.Square).then_inc(sem(n), 1)
                for n, j in (("sqq", "sq_q"), ("sqk", "sq_k")):
                    r = full(act, "dn", j, i)
                    free(A(d[n], r[:, :], ACT.Sqrt, bias=epsc[:, :]), "dn", j, i)
                act.wait_ge(sem("gc"), i + 1)
                A(eg[:, :], gc[:, :], ACT.Exp).then_inc(sem("eg"), 1)
                r = full(act, "dn", "grow", i)
                act.wait_ge(sem("dm"), i + 1)
                free(A(d["qd"], r[:, :], ACT.Exp), "dn", "grow", i)
                A(d["decT"], d["decT"], ACT.Exp).then_inc(sem("eT"), 1)
                A(d["decN"], d["decN"], ACT.Exp, scale=-1.0).then_inc(sem("eN"), 1)
                copy_out("At", d["At"], i)
                copy_out("A2", d["A2"], i)
                copy_out("A4", d["A4"], i)
                next(evac, 0)
                copy_out("A8", d["A8"], i)
                copy_out("T16", d["T"], i)
                next(evac, 0)
                copy_out("T32", d["T"], i)
                copy_out("T64", d["T"], i)
                next(evac, 0)
                copy_out("wT", d["wT"], i)
                next(evac, 0)
                r = full(act, "dn", "o", i)
                A(d["sqo"], r[:, :], ACT.Square).then_inc(sem("sqo_dn"), 1)
                r = full(act, "dn", "sq_o", i)
                free(A(d["sqo"], r[:, :], ACT.Sqrt, bias=epsc[:, :], scale=1.0 / P), "dn", "sq_o", i)
                settled(act, ("on", i + 1))
                A(dyn(oh, i), d["on"], ACT.Copy).then_inc(sem("o_head"), 1)

            def each4(gen):
                for _ in range(4):
                    next(gen, 0)

            each4(dn_evac(0, 0))
            with act.Fori(0, NH - 1) as i:
                dn_head(i, dn_evac(i + 1, i + 1))
            dn_head(NH - 1, feat_evac("diff", UNIT["diff"]))

            def attention(ph, i, o0, evac):
                diff = ph == "diff"
                items = [(m, b) for b in range(NB) for m in (0, 1)] if diff else \
                    [(m, b) for m in (0, 1) for b in range(NB)]
                per = 4 if diff else 8
                for t in range(8 + 4):
                    if t < 8:
                        w = (items[t][1] + 1) * P
                        read(act, ph, f"s{t}", i)
                        if t >= 2 and diff:
                            act.wait_ge(sem("pn_diff"), 4 * i + t // 2)
                        elif t >= 2:
                            act.wait_ge(sem("pn_odd"), 8 * i + (t - 1))
                        A(pr[t % 2][:, 0:w], ns[t % 2][:, 0:w], ACT.Exp, bias=nm[:, t:t + 1], scale=-1.0,
                          accum_out=rs[:, t:t + 1]).then_inc(sem("exp_" + ph), 1)
                    z = (t - 3) // 2 if diff and (t - 3) % 2 == 0 else t - 2 if not diff else -1
                    if 0 <= z < per:
                        b = z if diff else items[z][1]
                        pv_wait(ph, i, z, per)
                        r = full(act, ph, f"t{z}", i)
                        free(A(pT[z % 2][:, 0:(b + 1) * P], r[:, 0:(b + 1) * P], ACT.Copy), ph, f"t{z}", i)
                    if t == 8:
                        next(evac, 0)
                        next(evac, 0)
                if diff:
                    r = full(act, ph, "pv", i)
                    A(osd[:, :], r[:, :], ACT.Square).then_inc(sem("sqo_diff"), 1)
                    r = full(act, ph, "sq_o", i)
                    free(A(osd[:, :], r[:, :], ACT.Sqrt, bias=epsc[:, :], scale=1.0 / P), ph, "sq_o", i)
                    settled(act, is_read(ph, "pv", i))
                    A(dyn(oh, i + o0), osb[:, :], ACT.Copy).then_inc(sem("o_head"), 1)
                else:
                    settled(act, is_full(ph, "pv", i))
                    A(dyn(oh, i + o0), R[3][:, :], ACT.Copy).then_inc(sem("o_head"), 1)
                next(evac, 0)
                next(evac, 0)

            def pv_wait(ph, i, z, per):
                if z >= 2:
                    act.wait_ge(sem("pv_" + ph), (per - 1) * i + z - 1)
                elif z == 1:
                    if not (isinstance(i, int) and i == 0):
                        b, n = BANK.use(ph, "pv", i)
                        act.wait_ge(sem(f"R{b}_full"), n)

            with act.Fori(0, NH - 1) as i:
                attention("diff", i, NH, feat_evac("diff", i + (UNIT["diff"] + 1)))
            attention("diff", NH - 1, NH, iter(()))

            def out_proj(base, norm):
                with act.Fori(0, 2) as i:
                    for s in (0, 1):
                        for t in (0, 1):
                            settled(act, (f"acc_free{s}", 2 * i + (2 * base + t + 1)))
                            x_tile(norm, 4 * i + (2 * s + t), t)
                        units_split_act(act, s, i + (base + 1))

            def mlp(layer, norm_after, last):
                for n, (j0, count) in enumerate(HALVES):
                    g0 = UNIT[f"in{layer}{n}"]
                    base = 11 * layer + 6 * n
                    with act.Fori(0, count // 2) as i:
                        for s in (0, 1):
                            j = 2 * i + (j0 + s)
                            settled(act, (f"acc_free{s}", 2 * i + (2 * g0 + 1)))
                            A(cta[s][:, :], cb[s][:, ALPHA - 2:ALPHA - 2 + S], ACT.Identity,
                              bias=pv[:, bass.ds(j + (PV_CB + JF * layer), 1)],
                              scale=pv[:, bass.ds(j + PV_CW[layer], 1)]).then_inc(sem("mtap"), 1)
                            act.wait_ge(sem(f"mconv{s}"), 2 * i + (2 * base + 2))
                            A(sl[s][:, :], cta[s][:, :], ACT.Silu).then_inc(sem("msilu"), 1)
                            units_split_act(act, s, i + (g0 + 1))
                            settled(act, ("prod", 2 * i + (2 * base + s + 1)))
                            A(dyn(ah, 2 * i + s), pd[s][:, :], ACT.Copy).then_inc(sem("a_head"), 1)
                    g0 = UNIT[f"ff{layer}{n}"]

                    def x_tiles(i, g, split):
                        for s in (0, 1):
                            if n == 1:
                                settled(act, (f"acc_free{s}", 2 * g + 2))
                                x_tile(norm_after, 2 * i + s, s)
                            if split:
                                units_split_act(act, s, g + 1)

                    with act.Fori(0, 3 if last and n == 1 else 4) as i:
                        x_tiles(i, i + g0, True)
                    if last and n == 1:
                        x_tiles(3, g0 + 3, False)

            out_proj(UNIT["out0"], 1)
            norm_roots(1)
            mlp(0, 2, False)
            norm_roots(2)
            each4(feat_evac("odd", UNIT["odd"]))
            with act.Fori(0, NPAIR - 1) as i:
                attention("odd", i, 0, feat_evac("odd", i + (UNIT["odd"] + 1)))
            attention("odd", NPAIR - 1, 0, iter(()))
            out_proj(UNIT["out1"], 3)
            norm_roots(3)
            mlp(1, 4, True)
            norm_roots(4)

        @block.vector
        def _(dve):
            V = nc.vector
            step = sem("dve_step")

            def norm_rstd(n):
                ph = f"norm{n}"
                read(dve, ph, "row", 0)
                V.reciprocal(rstd[:, :], rstd[:, :]).then_inc(sem("rstd"), 1)
                read(dve, ph, "col", 0)
                V.reciprocal(rcol[:, :], sdc[:, :]).then_inc(sem("rstd"), 1)
                dve.wait_ge(sem("rstd"), 2 * n + 2)

            def x_tail(norm, k):
                dve.wait_ge(sem("m_head"), k + (KD * norm + 1))
                V.scalar_tensor_tensor(out=dyn(ml, k), in0=dyn(x, k), scalar=pv[:, bass.ds(k + PV_NORM[norm], 1)],
                                       in1=dyn(mh, k).bitcast(F32), op0=ALU.mult, op1=ALU.subtract)\
                    .then_inc(sem("m_tail"), 1)

            dve.wait_ge(sem("pv_full"), 1)
            for t, n in ((0, 90), (1, 110), (2, 66)):
                ins = V.tensor_copy(pv[:, t * P:t * P + n], acc[0][:, t * P:t * P + n])
            ins.then_inc(sem("pv_copied"), 1)
            dve.wait_ge(sem("pv_copied"), 1)
            for k in range(KD):
                x_tail(0, k)
            dve.wait_ge(sem("ab_head"), 1)
            V.tensor_tensor(abl[:, :, :], abw[:, :, :], abh[:, :, :].bitcast(F32), ALU.subtract)\
                .then_inc(sem("ab_split"), 1)
            for s in (0, 1):
                units_split_dve(dve, s, 0)
            V.tensor_scalar(sub8[:, :], pv[:, PV_SUB:PV_SUB + 1], 1.0 - LAM_INIT, None, ALU.mult).then_inc(step, 1)
            norm_rstd(0)

            n_step = [1]

            def chain(ins):
                n_step[0] += 1
                ins.then_inc(step, 1)
                dve.wait_ge(step, n_step[0])

            r = full(dve, "ab", "ab", 0)
            ins = V.tensor_tensor(abz[:, :, :], r[:, 0:NB * 8].rearrange("p (b n) -> p b n", n=8),
                                  rcol[:, :].unsqueeze(2).broadcast_to([P, NB, 8]), ALU.mult)
            free(ins, "ab", "ab", 0)
            read(dve, "ab", "ab", 0)
            chain(V.tensor_tensor(abt[0][:, :, :], abz[:, :, 0:4], dtb[:, :].unsqueeze(1).broadcast_to([P, NB, NH]),
                                  ALU.add))
            chain(V.tensor_tensor(lt[:, :, :], lp[:, :].rearrange("p (a b n) -> p a b n", a=2, b=2)[:, :, 0, :],
                                  lp[:, :].rearrange("p (a b n) -> p a b n", a=2, b=2)[:, :, 1, :], ALU.mult))
            chain(V.reduce_sum(ls[:, 0:2], lt[:, :, :], mybir.AxisListType.X))
            chain(V.tensor_scalar(abt[4][:, :, :], abt[0][:, :, :], -1.0, None, ALU.mult))
            V.tensor_tensor(abt[1][:, :, :], abt[0][:, :, :], abt[4][:, :, :], ALU.max).then_inc(sem("ab_in"), 1)
            chain(V.tensor_scalar(abt[0][:, :, :], abt[0][:, :, :], 0.0, None, ALU.max))
            dve.wait_ge(sem("ab_e"), 5)
            chain(V.tensor_tensor(abt[0][:, :, :], abt[0][:, :, :], abt[1][:, :, :], ALU.add))
            chain(V.tensor_tensor(abt[3][:, :, :], abt[0][:, :, :], alog[:, :].unsqueeze(1).broadcast_to([P, NB, NH]),
                                  ALU.mult))
            chain(V.tensor_scalar(gall[:, :, :], abt[3][:, :, :].rearrange("p b h -> p h b"), -1.0, None, ALU.mult))
            chain(V.tensor_scalar(abt[2][:, :, :], abt[2][:, :, :], 1.0, None, ALU.add))
            chain(V.reciprocal(ball[:, :, :], abt[2][:, :, :].rearrange("p b h -> p h b")))
            chain(V.tensor_tensor(ls[:, 2:3], ls[:, 1:2], ls[:, 0:1], ALU.subtract))
            V.tensor_scalar(lamc[:, :], ls[:, 2:3], -LAM_INIT, None, ALU.add).then_inc(sem("o_tail"), 1)

            def conv(i, c, slot, g, tile):
                buf = cb[c % 2]
                dve.wait_ge(sem(f"tile_full{slot}"), g)
                if c or not isinstance(i, int):
                    dve.wait_ge(sem("conv"), 9 * i + 3 * c)
                V.tensor_tensor(buf[:, ALPHA:ALPHA + S], acc[c][:, :], rstd[:, :], ALU.mult)\
                    .then_inc(sem(f"acc_free{slot}"), 1)
                dve.wait_ge(sem("tap"), 3 * i + (c + 1))
                for tap in (1, 2, 3):
                    if tap > 1:
                        dve.wait_ge(sem("conv"), 9 * i + (3 * c + tap - 1))
                    o = ALPHA - 3 + tap
                    V.scalar_tensor_tensor(out=cta[0][:, :], in0=buf[:, o:o + S],
                                           scalar=pv[:, bass.ds(i + (PV_DNC + 12 * tap + tile), 1)],
                                           in1=cta[0][:, :], op0=ALU.mult, op1=ALU.add).then_inc(sem("conv"), 1)

            def dn_evac(i, g):
                yield conv(i, 0, 0, 2 * g + 1, 0)
                conv(i, 1, 0, 2 * g + 2, 4)
                yield units_split_dve(dve, 0, g + 1)
                yield conv(i, 2, 1, 2 * g + 1, 8)
                dve.wait_ge(sem("tile_full1"), 2 * g + 2)
                if not (isinstance(i, int) and i == 0):
                    dve.wait_ge(sem("gC_full"), i)
                V.tensor_tensor(d["gN"], acc[3][:, :], rstd[:, :], ALU.mult).then_inc(sem("acc_free1"), 1)
                yield units_split_dve(dve, 1, g + 1)

            def att_evac(ph, i, g):
                diff = ph == "diff"
                prev = not (isinstance(i, int) and i == 0)
                dve.wait_ge(sem("tile_full0"), 2 * g + 1)
                if diff:
                    V.scalar_tensor_tensor(out=qr[0][:, :], in0=acc[0][:, :], scalar=QSCALE, in1=rstd[:, :],
                                           op0=ALU.mult, op1=ALU.mult).then_inc(sem("acc_free0"), 1)
                    dve.wait_ge(sem("tile_full0"), 2 * g + 2)
                    V.tensor_tensor(qr[1][:, :], acc[1][:, :], rstd[:, :], ALU.mult).then_inc(sem("acc_free0"), 1)
                else:
                    if prev:
                        full(dve, ph, "s7", i - 1)
                    V.scalar_tensor_tensor(out=aq[:, :], in0=acc[0][:, :], scalar=QSCALE, in1=rstd[:, :],
                                           op0=ALU.mult, op1=ALU.mult).then_inc(sem("acc_free0"), 1)
                    dve.wait_ge(sem("tile_full0"), 2 * g + 2)
                    V.tensor_tensor(ak[:, :], acc[1][:, :], rstd[:, :], ALU.mult).then_inc(sem("acc_free0"), 1)
                yield
                yield units_split_dve(dve, 0, g + 1)
                dve.wait_ge(sem("tile_full1"), 2 * g + 2)
                if prev:
                    full(dve, ph, "pv", i - 1)
                V.tensor_tensor(av[:, :, :], blk(acc[2][:, :]), cols(rcol[:, :]), ALU.mult)\
                    .then_inc(sem("acc_free1"), 2)
                yield
                yield units_split_dve(dve, 1, g + 1)

            def rope(i):
                for n, (name, dst) in enumerate((("rot_q", aq), ("rot_k", ak))):
                    b, u = BANK.use("diff", name, i - 1)
                    dve.wait_ge(sem(f"R{b}_full"), u + 1)
                    V.tensor_tensor(dst[:, :], R[b][:, :], cst[:, C_SIN:C_SIN + S], ALU.mult)\
                        .then_inc(sem(f"R{b}_read"), 1)
                    dve.wait_ge(sem(f"R{b}_read"), u + 1)
                    dve.wait_ge(sem("qc_full"), 2 * i + n + 1)
                    V.tensor_tensor(dst[:, :], dst[:, :], qc[n][:, :], ALU.add).then_inc(sem("roped"), 1)

            def dn_head(i, evac):
                def own(ins, name, n):
                    ins.then_inc(sem(name), 1)
                    dve.wait_ge(sem(name), n)

                g_i = gall[:, i, :] if isinstance(i, int) else gall[:, bass.ds(i, 1), :].squeeze(1)
                b_i = ball[:, i, :] if isinstance(i, int) else ball[:, bass.ds(i, 1), :].squeeze(1)
                V.tensor_copy(gh[:, :], g_i)
                V.tensor_copy(blk(d["gbc"]), cols(g_i)).then_inc(sem("gbc"), 1)
                read(dve, "dn", "sq_k", i)
                own(V.reciprocal(d["sqk"], d["sqk"]), "inv", 2 * i + 1)
                V.tensor_tensor(d["kh"], d["kT"], d["sqk"], ALU.mult).then_inc(sem("kh"), 1)
                own(V.reciprocal(d["sqq"], d["sqq"]), "inv", 2 * i + 2)
                V.scalar_tensor_tensor(out=d["qh"], in0=d["qT"], scalar=float(P) ** -0.5, in1=d["sqq"],
                                       op0=ALU.mult, op1=ALU.mult).then_inc(sem("qh"), 1)
                r = full(dve, "dn", "gcol", i)
                free(V.tensor_copy(gc[:, 0:2 * NB], r[:, 0:2 * NB]), "dn", "gcol", i)
                read(dve, "dn", "gcol", i)
                own(V.tensor_tensor(gc[:, 2 * NB:], gc[:, NB:2 * NB], gc[:, 0:NB], ALU.subtract), "gc", i + 1)
                r = full(dve, "dn", "grow", i)
                own(V.tensor_tensor(blk(d["decT"]), blk(r[:, :]), cols(gc[:, 0:NB]), ALU.subtract), "diffs", 2 * i + 1)
                own(V.tensor_scalar(d["decN"], d["decT"], 0.0, None, ALU.max), "diffs", 2 * i + 2)
                V.tensor_scalar(d["decT"], d["decT"], 0.0, None, ALU.min).then_inc(sem("dm"), 1)
                dve.wait_ge(sem("eg"), i + 1)
                V.tensor_tensor(be[:, :], b_i, eg[:, 0:NB], ALU.mult).then_inc(sem("be"), 1)
                r = full(dve, "dn", "kk", i)
                free(V.tensor_tensor(blk(d["N"]), blk(r[:, :]), cols(b_i), ALU.mult), "dn", "kk", i)
                read(dve, "dn", "kk", i)
                dve.wait_ge(sem("decN"), i + 1)
                own(V.tensor_tensor(d["N"], d["N"], d["decN"], ALU.mult), "N", i + 1)
                r = full(dve, "dn", "qk", i)
                dve.wait_ge(sem("decT"), i + 1)
                free(V.tensor_tensor(d["qkD"], r[:, :], d["decT"], ALU.mult), "dn", "qk", i)
                r = full(dve, "dn", "ktok", i)
                dve.wait_ge(sem("qd"), i + 1)
                dve.wait_ge(sem("be"), i + 1)
                V.tensor_tensor(blk(d["kbg"]), blk(r[:, :]), cols(be[:, :]), ALU.mult)
                free(V.tensor_tensor(blk(d["kd"]), blk(r[:, :]), cols(eg[:, 2 * NB:]), ALU.mult), "dn", "ktok", i)
                r = full(dve, "dn", "vtok", i)
                free(V.tensor_tensor(blk(d["vb"]), blk(r[:, :]), cols(b_i), ALU.mult), "dn", "vtok", i)
                read(dve, "dn", "At", i)
                V.tensor_tensor(blk(d["U"]), rows(ident), blk(d["At"]), ALU.subtract).then_inc(sem("U0"), 1)

                def copy(name, dst):
                    r = full(dve, "dn", name, i)
                    free(V.tensor_copy(dst, r[:, :]), "dn", name, i)

                def update(name, op, before=None):
                    r = full(dve, "dn", name, i)
                    if before:
                        read(dve, "dn", before, i)
                    else:
                        dve.wait_ge(sem("U0"), i + 1)
                    free(V.tensor_tensor(d["U"], d["U"], r[:, :], op), "dn", name, i)

                copy("A2t", d["A2t"])
                update("U1", ALU.add)
                copy("A4t", d["A4t"])
                next(evac, 0)
                update("U2", ALU.add, "U1")
                update("U3", ALU.add, "U2")
                copy("Y16", d["Y"])
                next(evac, 0)
                update("X16", ALU.subtract, "U3")
                copy("Y32", d["Y"])
                update("X32", ALU.subtract, "X16")
                copy("Y64", d["Y"])
                update("X64", ALU.subtract, "X32")
                next(evac, 0)
                r = full(dve, "dn", "u", i)
                V.tensor_copy(vn[:, :], r[:, 0:P]).then_inc(sem("vn"), 1)
                free(V.tensor_copy(d["u"], r[:, :]), "dn", "u", i)
                read(dve, "dn", "u", i)
                for b in range(NB - 1):
                    r = full(dve, "dn", f"kv{b}", i)
                    if b == 0:
                        ins = V.tensor_copy(st[:, :], r[:, 0:P])
                    else:
                        read(dve, "dn", f"kv{b - 1}", i)
                        ins = V.scalar_tensor_tensor(out=st[:, :], in0=st[:, :], scalar=eg[:, NB + b:NB + b + 1],
                                                     in1=r[:, 0:P], op0=ALU.mult, op1=ALU.add)
                    free(ins, "dn", f"kv{b}", i)
                    dve.wait_ge(sem("o_step"), 3 * i + b + 1)
                    r = full(dve, "dn", f"ws{b + 1}", i)
                    free(V.tensor_tensor(vn[:, :], d["u"][:, (b + 1) * P:(b + 2) * P], r[:, 0:P], ALU.subtract),
                         "dn", f"ws{b + 1}", i)
                next(evac, 0)
                read(dve, "dn", "sq_o", i)
                own(V.reciprocal(d["sqo"], d["sqo"]), "inv_o", i + 1)
                r = full(dve, "dn", "o", i)
                free(V.scalar_tensor_tensor(out=d["on"], in0=r[:, :], scalar=pv[:, PV_DNN:PV_DNN + 1], in1=d["sqo"],
                                            op0=ALU.mult, op1=ALU.mult), "dn", "o", i)
                read(dve, "dn", "o", i)
                dve.wait_ge(sem("gC_full"), i + 1)
                V.tensor_tensor(d["on"], d["on"], d["gC"], ALU.mult).then_inc(sem("on"), 1)
                dve.wait_ge(sem("o_head"), i + 1)
                V.tensor_tensor(dyn(ol, i), d["on"], dyn(oh, i).bitcast(F32), ALU.subtract).then_inc(sem("o_tail"), 1)

            for _ in dn_evac(0, 0):
                pass
            with dve.Fori(0, NH - 1) as i:
                dn_head(i, dn_evac(i + 1, i + 1))
            dn_head(NH - 1, att_evac("diff", 0, UNIT["diff"]))
            rope(0)

            def attention(ph, i, o0, h0, evac):
                diff = ph == "diff"
                items = [(m, b) for b in range(NB) for m in (0, 1)] if diff else \
                    [(m, b) for m in (0, 1) for b in range(NB)]
                for t in range(8 + 2):
                    if t < 8:
                        m, b = items[t]
                        w = (b + 1) * P
                        waits = [is_full(ph, f"s{t}", i)]
                        if t >= 2:
                            waits.append(("exp_" + ph, 8 * i + (t - 1)))
                        bias = cst[:, C_MASK + S - w:C_MASK + S] if diff else gb[m][:, S - w:S]
                        if not diff and b == 0:
                            waits += [(f"gb_full{m}", 32 * i + 32), ("gb_mask", 2)]
                        settled(dve, *waits)
                        r = R[BANK.use(ph, f"s{t}", i)[0]]
                        free(V.tensor_tensor_reduce(out=ns[t % 2][:, 0:w], in0=r[:, 0:w], in1=bias, scale=-1.0,
                                                    scalar=3e38, op0=ALU.add, op1=ALU.min,
                                                    accum_out=nm[:, t:t + 1]), ph, f"s{t}", i)
                    if diff:
                        if t % 2 == 0 and 2 <= t:
                            z = (t - 2) // 2
                            w = (z + 1) * P
                            dve.wait_ge(sem("exp_diff"), 8 * i + (2 * z + 2))
                            if z:
                                dve.wait_ge(sem("pn_diff"), 4 * i + z)
                            V.reciprocal(rr[:, 0:2], rs[:, 2 * z:2 * z + 2]).then_inc(sem("nrm_diff"), 1)
                            dve.wait_ge(sem("nrm_diff"), 12 * i + (3 * z + 1))
                            V.tensor_tensor(rr[:, 2:3], rr[:, 1:2], lamc[:, :], ALU.mult).then_inc(sem("nrm_diff"), 1)
                            dve.wait_ge(sem("nrm_diff"), 12 * i + (3 * z + 2))
                            if z >= 2:
                                tb, tu = BANK.use("diff", f"t{z - 2}", i)
                                dve.wait_ge(sem(f"R{tb}_full"), tu + 1)
                            V.tensor_scalar(pn[z % 2][:, 0:w], pr[1][:, 0:w], rr[:, 2:3], None, ALU.mult)\
                                .then_inc(sem("nrm_diff"), 1)
                            dve.wait_ge(sem("nrm_diff"), 12 * i + (3 * z + 3))
                            V.scalar_tensor_tensor(out=pn[z % 2][:, 0:w], in0=pr[0][:, 0:w], scalar=rr[:, 0:1],
                                                   in1=pn[z % 2][:, 0:w], op0=ALU.mult, op1=ALU.add)\
                                .then_inc(sem("pn_diff"), 1)
                    elif 1 <= t <= 8:
                        z = t - 1
                        w = (items[z][1] + 1) * P
                        dve.wait_ge(sem("exp_odd"), 8 * i + (z + 1))
                        if z >= 2:
                            dve.wait_ge(sem("pn_odd"), 8 * i + (z - 1))
                        V.reciprocal(rr[:, z % 2:z % 2 + 1], rs[:, z:z + 1]).then_inc(sem("nrm_odd"), 1)
                        dve.wait_ge(sem("nrm_odd"), 8 * i + (z + 1))
                        if z >= 2:
                            tb, tu = BANK.use("odd", f"t{z - 2}", i)
                            dve.wait_ge(sem(f"R{tb}_full"), tu + 1)
                        V.tensor_scalar(pn[z % 2][:, 0:w], pr[z % 2][:, 0:w], rr[:, z % 2:z % 2 + 1], None, ALU.mult)\
                            .then_inc(sem("pn_odd"), 1)
                    if t == 8:
                        next(evac, 0)
                        next(evac, 0)
                next(evac, 0)
                r = full(dve, ph, "pv", i)
                if diff:
                    read(dve, ph, "sq_o", i)
                    V.reciprocal(osd[:, :], osd[:, :]).then_inc(sem("inv_od"), 1)
                    dve.wait_ge(sem("inv_od"), i + 1)
                    free(V.scalar_tensor_tensor(out=osb[:, :], in0=r[:, :], scalar=sub8[:, :], in1=osd[:, :],
                                                op0=ALU.mult, op1=ALU.mult), ph, "pv", i)
                    src = osb[:, :]
                    dve.wait_ge(sem("o_head"), i + (h0 + 1))
                    V.tensor_tensor(dyn(ol, i + o0), src, dyn(oh, i + o0).bitcast(F32), ALU.subtract)\
                        .then_inc(sem("o_tail"), 1)
                else:
                    dve.wait_ge(sem("o_head"), i + (h0 + 1))
                    free(V.tensor_tensor(dyn(ol, i + o0), r[:, :], dyn(oh, i + o0).bitcast(F32), ALU.subtract),
                         ph, "pv", i)
                next(evac, 0)

            def out_proj(base, norm):
                with dve.Fori(0, 2) as i:
                    for s in (0, 1):
                        for t in (0, 1):
                            k = 4 * i + (2 * s + t)
                            dve.wait_ge(sem(f"tile_full{s}"), 2 * i + (2 * base + t + 1))
                            V.tensor_tensor(dyn(x, k), dyn(x, k), acc[2 * s + t][:, :], ALU.add)\
                                .then_inc(sem(f"acc_free{s}"), 1)
                            x_tail(norm, k)
                        units_split_dve(dve, s, i + (base + 1))

            def mlp(layer, norm_after, last):
                for n, (j0, count) in enumerate(HALVES):
                    g0 = UNIT[f"in{layer}{n}"]
                    base = 11 * layer + 6 * n
                    with dve.Fori(0, count // 2) as i:
                        for s in (0, 1):
                            j = 2 * i + (j0 + s)
                            w0 = PV_CW[layer]
                            dve.wait_ge(sem(f"tile_full{s}"), 2 * i + (2 * g0 + 1))
                            V.tensor_tensor(cb[s][:, ALPHA:ALPHA + S], acc[2 * s][:, :], rstd[:, :], ALU.mult)\
                                .then_inc(sem(f"acc_free{s}"), 1)
                            dve.wait_ge(sem("mtap"), 2 * i + (2 * base + s + 1))
                            for tap in (1, 2):
                                if tap == 2:
                                    dve.wait_ge(sem(f"mconv{s}"), 2 * i + (2 * base + 1))
                                o = ALPHA - 2 + tap
                                V.scalar_tensor_tensor(out=cta[s][:, :], in0=cb[s][:, o:o + S],
                                                       scalar=pv[:, bass.ds(j + (w0 + JF * tap), 1)],
                                                       in1=cta[s][:, :], op0=ALU.mult, op1=ALU.add)\
                                    .then_inc(sem(f"mconv{s}"), 1)
                            dve.wait_ge(sem(f"tile_full{s}"), 2 * i + (2 * g0 + 2))
                            V.tensor_tensor(ur[s][:, :], acc[2 * s + 1][:, :], rstd[:, :], ALU.mult)\
                                .then_inc(sem(f"acc_free{s}"), 1)
                            units_split_dve(dve, s, i + (g0 + 1))
                            dve.wait_ge(sem("msilu"), 2 * i + (2 * base + s + 1))
                            dve.wait_ge(sem(f"acc_free{s}"), 2 * i + (2 * g0 + 2))
                            dve.wait_ge(sem(f"w_tail{1 - s}"), i + (g0 + 1 + s))
                            V.tensor_tensor(pd[s][:, :], ur[s][:, :], sl[s][:, :], ALU.mult).then_inc(sem("prod"), 1)
                            dve.wait_ge(sem("a_head"), 2 * i + (2 * base + s + 1))
                            V.tensor_tensor(dyn(al, 2 * i + s), pd[s][:, :], dyn(ah, 2 * i + s).bitcast(F32),
                                            ALU.subtract).then_inc(sem("a_tail"), 1)
                    g0 = UNIT[f"ff{layer}{n}"]

                    def x_tiles(i, g, split):
                        for s in (0, 1):
                            k = 2 * i + s
                            dve.wait_ge(sem(f"tile_full{s}"), 2 * g + 2)
                            V.tensor_tensor(dyn(x, k), dyn(x, k), acc[2 * s][:, :], ALU.add)\
                                .then_inc(sem(f"acc_free{s}"), 2)
                            if n == 1 and norm_after < 4:
                                x_tail(norm_after, k)
                            if split:
                                units_split_dve(dve, s, g + 1)

                    with dve.Fori(0, 3 if last and n == 1 else 4) as i:
                        x_tiles(i, i + g0, True)
                    if last and n == 1:
                        x_tiles(3, g0 + 3, False)

            with dve.Fori(0, NH - 1) as i:
                attention("diff", i, NH, NH, att_evac("diff", i + 1, i + (UNIT["diff"] + 1)))
                rope(i + 1)
            attention("diff", NH - 1, NH, NH, iter(()))
            out_proj(UNIT["out0"], 1)
            norm_rstd(1)
            mlp(0, 2, False)
            norm_rstd(2)
            for _ in att_evac("odd", 0, UNIT["odd"]):
                pass
            with dve.Fori(0, NPAIR - 1) as i:
                attention("odd", i, 0, 2 * NH, att_evac("odd", i + 1, i + (UNIT["odd"] + 1)))
            attention("odd", NPAIR - 1, 0, 2 * NH, iter(()))
            out_proj(UNIT["out1"], 3)
            norm_rstd(3)
            mlp(1, 4, True)
            norm_rstd(4)
            for k in range(KD):
                r = full(dve, "yt", f"x{k}", 0)
                if k >= 2:
                    dve.wait_ge(sem(f"out_done{k % 2}"), 16 * (k // 2))
                free(V.tensor_tensor(ob[k % 2][:, :, :], blk(r[:, :]), cols(rcol[:, :]), ALU.mult), "yt", f"x{k}", 0)


_INS = ["x", "even_norm_mix", "even_w_in", "even_dn_conv", "even_dn_A_log", "even_dn_dt_bias", "even_dn_norm",
        "even_diff_lambda", "even_diff_subln", "even_w_out", "odd_norm_mix", "odd_w_qkv", "odd_rel_bias",
        "odd_w_out", "ffn_norm", "ffn_w_in", "ffn_conv_w", "ffn_conv_b", "ffn_w_out", "final_norm"]


def kernel(**inputs):
    import numpy as _np
    import concourse.bacc as _bacc
    from concourse import mybir as _mybir
    from concourse.bass_utils import run_bass_kernel_spmd as _run

    nc = _bacc.Bacc("TRN2", target_bir_lowering=False, num_devices=1)
    arrays, aps = {}, {}
    given = {name: _np.ascontiguousarray(inputs[name]) for name in _INS}
    given["consts"] = constants()
    for name, a in given.items():
        arrays[f"in_{name}"] = a
        aps[name] = nc.dram_tensor(f"in_{name}", a.shape, _mybir.dt.from_np(a.dtype), kind="ExternalInput").ap()
    out = nc.dram_tensor("out_0", (S, D), _mybir.dt.float32, kind="ExternalOutput").ap()
    build(nc, aps, out)
    r = _run(nc, [arrays], core_ids=[0])
    return r.results[0]["out_0"].reshape(1, S, D)
```

```python
import math
from contextlib import ExitStack

import numpy as np

import concourse.bass as bass
from concourse import mybir

F32 = mybir.dt.float32
R32 = mybir.dt.float32r
ALU = mybir.AluOpType
ACT = mybir.ActivationFunctionType

P = 128
S = 512
NB = S // P
D = 1024
KD = D // P
FF = 2816
JF = FF // P
HALVES = ((0, 12), (12, 10))
NH = 4
HD = 64
NPAIR = 8
EPS = 1e-6
QSCALE = HD ** -0.5
LAM_INIT = 0.8 - 0.6 * math.exp(0.0)
NEG = -1e30
REL = 256
GLEN = 640
ALPHA = 4

C_Q, C_K, C_V, C_AB, C_GATE, C_FQ, C_FK, C_FV = 0, 512, 1024, 1536, 1544, 2056, 2568, 3080

PV_EVEN, PV_FFN, PV_ODD, PV_FIN, PV_DNC, PV_DNN, PV_SUB = 0, 8, 24, 32, 40, 88, 89
PV_CW = (P, 2 * P)
PV_CB = P + 66
PV_NORM = (PV_EVEN, PV_FFN, PV_ODD, PV_FFN + 8, PV_FIN)

C_ID, C_ONE, C_TRIU, C_STRICT, C_M16, C_M32, C_M64, C_M128, C_PERM = range(9)
C_COS, C_SIN, C_MASK = 9 * P, 9 * P + S, 9 * P + 2 * S
C_WIDTH = 9 * P + 3 * S


def constants():
    i = np.arange(P)
    row, col = i[:, None], i[None, :]
    c = np.zeros((P, C_WIDTH), np.float32)

    def put(n, m):
        c[:, n * P:(n + 1) * P] = m

    put(C_ID, row == col)
    put(C_ONE, 1.0)
    put(C_TRIU, row <= col)
    put(C_STRICT, col < row)
    put(C_M16, row // 16 == col // 16)
    for n, w in ((C_M32, 32), (C_M64, 64), (C_M128, 128)):
        put(n, (row // w == col // w) & (row // (w // 2) != col // (w // 2)))
    put(C_PERM, row == (col ^ 32))
    inv = np.float32(1.0) / np.power(np.float32(10000.0), np.arange(0, HD, 2, dtype=np.float32) / np.float32(HD))
    ang = np.arange(S, dtype=np.float32)[:, None] * inv[None, :].astype(np.float32)
    cos, sin = np.cos(ang).T, np.sin(ang).T
    c[:, C_COS:C_COS + S] = np.concatenate([cos] * 4)
    c[:, C_SIN:C_SIN + S] = np.concatenate([-sin, sin] * 2)
    c[:64, C_MASK + 448:C_MASK + 512] = NEG
    return c


_DN = [("sq_q", 0), ("sq_k", 1), ("grow", 0), ("gcol", 1), ("kk", 1), ("qk", 0), ("ktok", 1), ("vtok", 0),
       ("At", 1), ("A2", 0), ("A2t", 1), ("U1", 0), ("A4", 1), ("A4t", 0), ("U2", 1), ("A8", 0), ("U3", 1),
       ("T16", 0), ("Y16", 1), ("X16", 0), ("T32", 1), ("Y32", 0), ("X32", 1), ("T64", 0), ("Y64", 1), ("X64", 0),
       ("u", 1), ("wT", 0), ("o", 0), ("kv0", 1), ("ws1", 1), ("kv1", 1), ("ws2", 1), ("kv2", 1), ("ws3", 1),
       ("sq_o", 1)]
DN_JOBS = [(f"{n}{h}", h + 2 * b) for n, b in _DN for h in (0, 1)]
DIFF_JOBS = [(f"s{j}", j % 2) for j in range(8)] + [("vt", 2)] + [(f"t{b}", 2) for b in range(4)] + [("sq_o", 2), ("pv", 3)] \
    + [("rot_q", 0), ("rot_k", 1)]
ODD_JOBS = [(f"s{j}", j % 2) for j in range(8)] + [("vt", 2)] + [(f"t{j}", 2) for j in range(8)] + [("pv", 3)]
XT_JOBS = [(f"x{k}", k % 4) for k in range(KD)]
NORM_JOBS = [("row", 0), ("col", 1)]
AB_JOBS = [("abT", 2), ("ab", 3)]


class Bank:

    def __init__(self):
        self.base, self.at = {}, [0] * 4

    def phase(self, name, jobs, times, lead=()):
        for j in lead:
            self.at[dict(jobs)[j]] += 1
        self.base[name] = (list(self.at), jobs)
        for _, b in jobs:
            self.at[b] += times
        for j in lead:
            self.at[dict(jobs)[j]] -= 1

    def use(self, phase, job, i):
        base, jobs = self.base[phase]
        b = dict(jobs)[job]
        mine = [n for n, bank in jobs if bank == b]
        return b, base[b] + len(mine) * i + mine.index(job)


BANK = Bank()
BANK.phase("xt", XT_JOBS, 1)
BANK.phase("ab", AB_JOBS, 1)
BANK.phase("norm0", NORM_JOBS, 1)
BANK.phase("dn", DN_JOBS, NH // 2)
BANK.phase("diff", DIFF_JOBS, NH, lead=("rot_q", "rot_k"))
BANK.phase("norm1", NORM_JOBS, 1)
BANK.phase("norm2", NORM_JOBS, 1)
BANK.phase("odd", ODD_JOBS, NPAIR)
BANK.phase("norm3", NORM_JOBS, 1)
BANK.phase("norm4", NORM_JOBS, 1)
BANK.phase("yt", XT_JOBS, 1)

_turns = [("dn", NH), ("diff", NH), ("out0", 2)]
for _l in (0, 1):
    if _l:
        _turns += [("odd", NPAIR), ("out1", 2)]
    for _n, (_, _c) in enumerate(HALVES):
        _turns += [(f"in{_l}{_n}", _c // 2), (f"ff{_l}{_n}", 4)]
UNIT = {}
_at = 0
for _name, _n in _turns:
    UNIT[_name] = _at
    _at += _n
UNITS = _at


def build(nc, T, out):
    ctx = ExitStack()
    with ctx:
        def sb(name, shape, dt=F32, where=ctx):
            return where.enter_context(nc.sbuf_tensor(name, shape, dt))

        sems = {}

        def sem(name):
            if name not in sems:
                sems[name] = ctx.enter_context(nc.semaphore(name))
            return sems[name]

        place = ExitStack()
        xs = sb("x_start", [P, KD, S], F32, place)
        place.close()
        om = sb("om", [P, NH, S], F32, place)
        dx = {(n, h): sb(f"dn_{n}{h}", [P, S], F32, place)[:, :] for n in ("E32", "E64") for h in (0, 1)}
        place.close()
        x = sb("x", [P, KD, S])
        mh = sb("mh", [P, KD, S], R32)
        ml = sb("ml", [P, KD, S], R32)
        raw = [sb(f"raw{s}", [P, 2048]) for s in (0, 1)]
        wh = [sb(f"wh{s}", [P, 2048], R32) for s in (0, 1)]
        wl = [sb(f"wl{s}", [P, 2048], R32) for s in (0, 1)]
        cst = sb("cst", [P, C_WIDTH])
        pv = sb("pv", [P, 3 * P])
        rstd = sb("rstd", [P, S])
        rcol = sb("rcol", [P, NB])
        sdc = sb("sdc", [P, NB])
        ssum = sb("ssum", [P, S])
        sq = [sb(f"sq{s}", [P, S]) for s in (0, 1)]
        cb = [sb(f"cb{s}", [P, ALPHA + S]) for s in (0, 1)]
        cta = [sb(f"cta{s}", [P, S]) for s in (0, 1)]
        epsc = sb("epsc", [P, 1])

        gall = sb("gall", [P, NH, NB], F32, ctx)
        ball = sb("ball", [P, NH, NB], F32, ctx)
        lamc = sb("lamc", [P, 1], F32, ctx)
        abz = sb("abz", [P, NB, 8], F32, ctx)
        abt = [sb(f"abt{n}", [P, NB, NH], F32, ctx) for n in range(5)]
        dtb = sb("dtb", [P, NH], F32, ctx)
        alog = sb("alog", [P, NH], F32, ctx)
        ls = sb("ls", [P, 4], F32, ctx)
        sub8 = sb("sub8", [P, 1])

        def cblk(n):
            return cst[:, n * P:(n + 1) * P]

        ident, ones, triu = cblk(C_ID), cblk(C_ONE), cblk(C_TRIU)

        def rows(a):
            return a.unsqueeze(1).broadcast_to([P, NB, P])

        def cols(a):
            return a.unsqueeze(2).broadcast_to([P, NB, P])

        def blk(t):
            return t.rearrange("p (b n) -> p b n", b=NB)

        start = ExitStack()
        xin = sb("xin", [P, NB, D], F32, start)
        prow = sb("prow", [P, 3, P], F32, start)
        abw = sb("abw", [P, KD, 8], F32, start)
        abh = sb("abh", [P, KD, 8], R32, start)
        abl = sb("abl", [P, KD, 8], R32, start)
        abs_ = sb("abs", [8, S], F32, start)
        lp = sb("lp", [P, 256], F32, start)
        lt = sb("lt", [P, 2, HD], F32, start)
        start.close()
        mix = ExitStack()
        own = ("gC", "sqq", "sqk", "qh", "kh", "decT", "decN", "qd", "qkD", "N", "A", "At", "A2", "A2t", "U")
        d = [{}, {}]
        for n in ("gC", "sqq", "sqk", "qh", "kh", "decT", "decN", "qd"):
            for h in (0, 1):
                d[h][n] = sb(f"dn_{n}{h}", [P, S], F32, mix)[:, :]
        for h, n in ((0, "qT"), (0, "kT"), (0, "vT"), (1, "qT"), (1, "kT"), (1, "vT"), (0, "gN"), (1, "gN")):
            d[h][n] = sb(f"dn_{n}{h}", [P, S], F32, mix)[:, :]
        for n in own[8:]:
            for h in (0, 1):
                d[h][n] = sb(f"dn_{n}{h}", [P, S], F32, mix)[:, :]
        gh, gc, eg, be, vn, st = [], [], [], [], [], []
        for h in (0, 1):
            for n in ("E32", "E64"):
                d[h][n] = dx[n, h]
            for new, old in (("gbc", "decT"), ("kd", "kh"), ("kbg", "qh"), ("vb", "decN"), ("E128", "N"),
                             ("A4", "A"), ("A4t", "At"), ("A8", "A2"), ("T", "decT"), ("Y", "A2t"), ("wT", "E32"),
                             ("u", "E64"), ("sqo", "qd"), ("on", "A")):
                d[h][new] = d[h][old]
            gh.append(sb(f"gh{h}", [P, NB], F32, mix))
            gc.append(sb(f"gc{h}", [P, 3 * NB], F32, mix))
            eg.append(sb(f"eg{h}", [P, 3 * NB], F32, mix))
            be.append(sb(f"be{h}", [P, NB], F32, mix))
            vn.append(sb(f"vn{h}", [P, P], F32, mix))
            st.append(sb(f"st{h}", [P, P], F32, mix))
        mix.close()
        mixer = ExitStack()
        oh = sb("oh", [P, KD, S], R32, mixer)
        ol = sb("ol", [P, KD, S], R32, mixer)
        att = ExitStack()
        qr0 = sb("qr0", [P, S], F32, att)
        qr1 = sb("qr1", [P, S], F32, att)
        vf = sb("vf", [P, S], F32, att)
        qc0 = sb("qc0", [P, S], F32, att)
        aq = sb("aq", [P, S], F32, att)
        ak = sb("ak", [P, S], F32, att)
        qc1 = sb("qc1", [P, S], F32, att)
        av = sb("av", [P, NB, P], F32, att)
        qr, qc = [qr0, qr1], [qc0, qc1]
        ns2 = sb("ns", [P, 2 * S], F32, att)
        pr2 = sb("pr", [P, 2 * S], F32, att)
        ns = [ns2[:, n * S:(n + 1) * S] for n in (0, 1)]
        pr = [pr2[:, n * S:(n + 1) * S] for n in (0, 1)]
        pn = [sb(f"pn{n}", [P, S], F32, att) for n in (0, 1)]
        pT = [sb(f"pT{n}", [P, S], F32, att) for n in (0, 1)]
        gb = [sb(f"gb{n}", [P, S], F32, att) for n in (0, 1)]
        osb = sb("osb", [P, S], F32, att)
        osd = sb("osd", [P, S], F32, att)
        nm = sb("nm", [P, 8], F32, att)
        rs = sb("rs", [P, 8], F32, att)
        rr = sb("rr", [P, 8], F32, att)
        rb, fx = ns2[0:16, 0:2 * REL + 1], pr2[0:16, 0:GLEN]
        att.close()
        mixer.close()
        mlp = ExitStack()
        ah = sb("ah", [P, 12, S], R32, mlp)
        al = sb("al", [P, 12, S], R32, mlp)
        sl = [sb(f"sl{s}", [P, S], F32, mlp) for s in (0, 1)]
        ur = [sb(f"ur{s}", [P, S], F32, mlp) for s in (0, 1)]
        pd = [sb(f"pd{s}", [P, S], F32, mlp) for s in (0, 1)]
        mlp.close()
        end = ExitStack()
        ob = [sb(f"ob{s}", [P, NB, P], F32, end) for s in (0, 1)]
        end.close()

        xscr = nc.dram_tensor("x_kept", (P, KD, S), F32).ap()
        gscr = nc.dram_tensor("rel_bias_extended", (16, P, GLEN), F32).ap()

        acc = [ctx.enter_context(nc.psum_tensor(f"acc{n}", [P, S], F32)) for n in range(4)]
        R = [ctx.enter_context(nc.psum_tensor(f"R{n}", [P, S], F32)) for n in range(4)]

        block = ctx.enter_context(nc.Block())

        def full(eng, phase, job, i):
            b, n = BANK.use(phase, job, i)
            eng.wait_ge(sem(f"R{b}_full"), n + 1)
            return R[b]

        def free(ins, phase, job, i):
            b, _ = BANK.use(phase, job, i)
            ins.then_inc(sem(f"R{b}_read"), 1)

        def read(eng, phase, job, i):
            b, n = BANK.use(phase, job, i)
            eng.wait_ge(sem(f"R{b}_read"), n + 1)

        def settled(eng, *waits):
            values = [v if isinstance(v, int) else eng.to_reg(v) for _, v in waits]
            eng.wait_ge(sem("cst_in"), 16)
            for (name, _), v in zip(waits, values):
                eng.wait_ge(sem(name), v)

        def is_full(phase, job, i):
            b, n = BANK.use(phase, job, i)
            return f"R{b}_full", n + 1

        def is_read(phase, job, i):
            b, n = BANK.use(phase, job, i)
            return f"R{b}_read", n + 1

        def dyn(t, k):
            return t[:, k, :] if isinstance(k, int) else t[:, bass.ds(k, 1), :].squeeze(1)

        def units_split_act(act, s, g):
            act.wait_ge(sem(f"raw_full{s}"), 32 * (g + 1))
            if not (isinstance(g, int) and g == 0):
                act.wait_ge(sem(f"tile_full{s}"), 2 * g)
            nc.scalar.activation(wh[s][:, :], raw[s][:, :], ACT.Copy).then_inc(sem(f"w_head{s}"), 1)

        def units_split_dve(dve, s, g):
            dve.wait_ge(sem(f"w_head{s}"), g + 1)
            nc.vector.tensor_tensor(wl[s][:, :], raw[s][:, :], wh[s][:, :].bitcast(F32),
                                    ALU.subtract).then_inc(sem(f"w_tail{s}"), 1)

        @block.sync
        def _(sp):
            def load(s, g, pieces):
                if not (isinstance(g, int) and g == 0):
                    sp.wait_ge(sem(f"w_tail{s}"), g)
                for dst, src in pieces:
                    sp.dma_start(dst, src).then_inc(sem(f"raw_full{s}"), 16)

            def pair(s, w, c0, c1):
                v = raw[s][:, :].rearrange("p (t k n) -> p t k n", t=2, k=KD)
                wv = w.rearrange("(k p) n -> p k n", p=P)
                return [(v[:, 0, :, :], wv[:, :, bass.ds(c0, P)]), (v[:, 1, :, :], wv[:, :, bass.ds(c1, P)])]

            def one(s, w, c0):
                v = raw[s][:, 0:KD * P].rearrange("p (k n) -> p k n", k=KD)
                wv = w.rearrange("(k p) n -> p k n", p=P)
                return [(v[:, 0:4, :], wv[:, 0:4, bass.ds(c0, P)]), (v[:, 4:8, :], wv[:, 4:8, bass.ds(c0, P)])]

            def down(s, w, j0, count, c0):
                v = raw[s][:, 0:count * P].rearrange("p (k n) -> p k n", k=count)
                wv = w[j0 * P:(j0 + count) * P, :].rearrange("(k p) n -> p k n", p=P)
                h = count // 2
                return [(v[:, 0:h, :], wv[:, 0:h, bass.ds(c0, P)]), (v[:, h:count, :], wv[:, h:count, bass.ds(c0, P)])]

            sp.dma_start(cst[:, 0:P], T["consts"][:, 0:P]).then_inc(sem("cst_in"), 16)
            xv = T["x"][0].rearrange("(b p) d -> p b d", p=P)
            for b in range(NB):
                sp.dma_start(xin[:, b, :], xv[:, b, :]).then_inc(sem("x_in"), 16)
            sp.dma_start(cst[:, P:], T["consts"][:, P:]).then_inc(sem("cst_rest"), 16)
            w0 = T["even_w_in"][0]
            load(0, 0, pair(0, w0, C_Q, C_K))
            load(1, 0, pair(1, w0, C_V, C_GATE))
            for k in range(4):
                read(sp, "xt", f"x{k + 4}", 0)
            sp.dma_start(xscr, xs[:, :, :]).then_inc(sem("x_kept"), 16)
            with sp.Fori(1, NH) as i:
                load(0, i, pair(0, w0, i * P + C_Q, i * P + C_K))
                load(1, i, pair(1, w0, i * P + C_V, i * P + C_GATE))
            with sp.Fori(0, NH) as i:
                load(0, i + UNIT["diff"], pair(0, w0, i * P + C_FQ, i * P + C_FK))
                load(1, i + UNIT["diff"], one(1, w0, i * P + C_FV))

            def out_proj(w, base):
                with sp.Fori(0, 2) as i:
                    for s in (0, 1):
                        load(s, i + base, pair(s, w, i * 512 + 256 * s, i * 512 + 256 * s + P))

            def mlp_loads(layer):
                wi, wo = T["ffn_w_in"][layer], T["ffn_w_out"][layer]
                for n, (j0, count) in enumerate(HALVES):
                    with sp.Fori(0, count // 2) as i:
                        for s in (0, 1):
                            c = i * 256 + (j0 + s) * P
                            load(s, i + UNIT[f"in{layer}{n}"], pair(s, wi, c, c + FF))
                    with sp.Fori(0, 4) as i:
                        for s in (0, 1):
                            load(s, i + UNIT[f"ff{layer}{n}"], down(s, wo, j0, count, i * 256 + s * P))

            out_proj(T["even_w_out"][0], UNIT["out0"])
            mlp_loads(0)
            wq = T["odd_w_qkv"][0]
            with sp.Fori(0, NPAIR) as i:
                load(0, i + UNIT["odd"], pair(0, wq, i * P, i * P + D))
                load(1, i + UNIT["odd"], one(1, wq, i * P + 2 * D))
            out_proj(T["odd_w_out"][0], UNIT["out1"])
            mlp_loads(1)
            ov = out.rearrange("(b p) (k n) -> p b k n", p=P, n=P)
            for k in range(KD):
                read(sp, "yt", f"x{k}", 0)
                sp.dma_start(ov[:, :, k, :], ob[k % 2][:, :, :]).then_inc(sem(f"out_done{k % 2}"), 16)
            for s in (0, 1):
                sp.wait_ge(sem(f"out_done{s}"), 16 * KD // 2)

        @block.gpsimd
        def _(pool):
            def pdma(dst, src):
                pool.dma_start(dst, src).then_inc(sem("p_in"), 16)

            def vec(src, r0, t):
                n = src.shape[0]
                pdma(prow[r0:r0 + n, t, :], src)

            v = "(k p) -> k p"
            vec(T["even_norm_mix"][0].rearrange(v, p=P), PV_EVEN, 0)
            for l in (0, 1):
                vec(T["ffn_norm"][l].rearrange(v, p=P), PV_FFN + 8 * l, 0)
            vec(T["odd_norm_mix"][0].rearrange(v, p=P), PV_ODD, 0)
            vec(T["final_norm"].rearrange(v, p=P), PV_FIN, 0)
            vec(T["even_dn_conv"][0].rearrange("t (k p) -> (t k) p", p=P), PV_DNC, 0)
            vec(T["even_dn_norm"], PV_DNN, 0)
            vec(T["even_diff_subln"], PV_SUB, 0)
            vec(T["ffn_conv_w"][0].rearrange("t (k p) -> (t k) p", p=P), 0, 1)
            vec(T["ffn_conv_b"].rearrange("l (k p) -> (l k) p", p=P), 66, 1)
            vec(T["ffn_conv_w"][1].rearrange("t (k p) -> (t k) p", p=P), 0, 2)
            pdma(dtb[:, :], T["even_dn_dt_bias"].broadcast_to([P, NH]))
            pdma(alog[:, :], T["even_dn_A_log"].broadcast_to([P, NH]))
            pdma(lp[:, :], T["even_diff_lambda"].rearrange("a b c -> a (b c)").broadcast_to([P, 256]))
            pdma(abw[:, :, :], T["even_w_in"][0].rearrange("(k p) n -> p k n", p=P)[:, :, C_AB:C_AB + 8])
            for s in (0, 1):
                pool.memset(cb[s][:, 0:ALPHA], 0.0).then_inc(sem("zeros"), 1)
            pool.memset(epsc[:, :], EPS).then_inc(sem("zeros"), 1)

            def sum_squares(norm):
                if norm:
                    read(pool, f"norm{norm - 1}", "col", 0)
                pool.memset(ssum[:, :], 0.0).then_inc(sem("ssum"), 1)
                with pool.Fori(0, KD // 2) as i:
                    for s in (0, 1):
                        pool.wait_ge(sem("sq_full"), 2 * i + (KD * norm + s + 1))
                        pool.wait_ge(sem("ssum"), 2 * i + (9 * norm + s + 1))
                        pool.tensor_tensor(ssum[:, :], ssum[:, :], sq[s][:, :], ALU.add).then_inc(sem("ssum"), 1)

            sum_squares(0)

            pool.wait_ge(sem("x_kept"), 16)
            for p in range(NH // 2):
                for h in (0, 1):
                    e = d[h]
                    pool.wait_ge(sem(f"gate_full{h}"), p + 1)
                    if p:
                        pool.wait_ge(sem("o_done"), 2 * p)
                    pool.tensor_copy(e["gC"], e["gN"]).then_inc(sem(f"gC_full{h}"), 1)
                for h in (0, 1):
                    pool.wait_ge(sem(f"eT{h}"), p + 1)
                    pool.tensor_tensor(blk(d[h]["decT"]), blk(d[h]["decT"]), rows(triu), ALU.mult)\
                        .then_inc(sem(f"decT{h}"), 1)
                    pool.wait_ge(sem(f"eN{h}"), p + 1)
                    pool.tensor_tensor(blk(d[h]["decN"]), blk(d[h]["decN"]), rows(cblk(C_STRICT)), ALU.mult)\
                        .then_inc(sem(f"decN{h}"), 1)
                for h in (0, 1):
                    e = d[h]
                    pool.wait_ge(sem(f"N{h}"), p + 1)
                    pool.tensor_tensor(blk(e["A"]), blk(e["N"]), rows(cblk(C_M16)), ALU.mult).then_inc(sem(f"A_E{h}"), 1)
                for h in (0, 1):
                    e = d[h]
                    pool.wait_ge(sem(f"qh{h}"), p + 1)
                    read(pool, "dn", f"grow{h}", p)
                    pool.tensor_tensor(e["qd"], e["qd"], e["qh"], ALU.mult).then_inc(sem(f"qd{h}"), 1)
                for h in (0, 1):
                    e = d[h]
                    for n, m in (("E32", C_M32), ("E64", C_M64), ("E128", C_M128)):
                        if n == "E128":
                            pool.wait_ge(sem(f"A_E{h}"), 4 * p + 3)
                        pool.tensor_tensor(blk(e[n]), blk(e["N"]), rows(cblk(m)), ALU.mult)\
                            .then_inc(sem(f"A_E{h}"), 1)

            pool.wait_ge(sem("A_E1"), 4 * (NH // 2))
            with pool.Fori(0, NH) as i:
                for n in (0, 1):
                    pool.wait_ge(sem("acc_free0"), 2 * i + (2 * UNIT["diff"] + n + 1))
                    pool.tensor_tensor(qc[n][:, :], qr[n][:, :], cst[:, C_COS:C_COS + S], ALU.mult)\
                        .then_inc(sem("qc_full"), 1)

            pool.wait_ge(sem("oc_tail"), NH)
            for k in range(0, KD, 2):
                pool.dma_start(x[:, k:k + 2, :], xscr[:, k:k + 2, :]).then_inc(sem("x_back"), 16)

            pool.wait_ge(sem("R3_full"), BANK.use("diff", "pv", NH - 1)[1] + 1)
            pool.dma_start(rb, T["odd_rel_bias"][0]).then_inc(sem("rb_in"), 16)
            pool.wait_ge(sem("rb_in"), 16)
            pool.tensor_copy(fx[:, 255:GLEN - 1], rb[:, 0:384]).then_inc(sem("fx"), 1)
            pool.tensor_copy(fx[:, 0:255], rb[:, 0:1].broadcast_to([16, 255])).then_inc(sem("fx"), 1)
            pool.memset(fx[:, GLEN - 1:GLEN], 0.0).then_inc(sem("fx"), 1)
            pool.wait_ge(sem("fx"), 3)
            pool.dma_start(gscr, fx.unsqueeze(1).broadcast_to([16, P, GLEN])).then_inc(sem("fx_out"), 16)
            pool.wait_ge(sem("fx_out"), 16)

            sum_squares(1)
            sum_squares(2)

            def load_bias(m, head):
                row = gscr[bass.ds(head, 1), :, :]
                for p0, p1, n in ((0, 64, 448), (64, P, S)):
                    src = bass.AP(tensor=row.tensor, offset=row.offset + (127 + p0 * (GLEN - 1)),
                                  ap=[[GLEN - 1, p1 - p0], [1, n]])
                    pool.dma_start(gb[m][p0:p1, 0:n], src).then_inc(sem(f"gb_full{m}"), 16)

            for m in (0, 1):
                pool.memset(gb[m][0:64, 448:S], NEG).then_inc(sem("gb_mask"), 1)
                load_bias(m, m)
            with pool.Fori(1, NPAIR) as i:
                for m in (0, 1):
                    read(pool, "odd", f"s{4 * m + 3}", i - 1)
                    load_bias(m, 2 * i + m)
            sum_squares(3)
            sum_squares(4)

        @block.tensor
        def _(pe):
            def job(phase, name, i, first=True):
                b, n = BANK.use(phase, name, i)
                if not (isinstance(n, int) and n == 0):
                    pe.wait_ge(sem(f"R{b}_read"), n)
                return R[b]

            def done(ins, phase, name, i):
                b, _ = BANK.use(phase, name, i)
                ins.then_inc(sem(f"R{b}_full"), 1)

            def mm3(o, ah_, al_, bh_, bl_, first, last):
                nc.tensor.matmul(o, ah_, bh_, start=first, stop=False)
                nc.tensor.matmul(o, ah_, bl_, start=False, stop=False)
                return nc.tensor.matmul(o, al_, bh_, start=False, stop=last)

            def begin(s, g):
                pe.wait_ge(sem(f"w_tail{s}"), g + 1)
                if not (isinstance(g, int) and g == 0):
                    pe.wait_ge(sem(f"acc_free{s}"), 2 * g)

            def features(s, g, mov, tiles=2, kn=KD, norm=None, srcwait=None):
                begin(s, g)
                ws = [w[s][:, 0:tiles * kn * P].rearrange("p (t k n) -> p t k n", t=tiles, k=kn) for w in (wh, wl)]
                for t in range(tiles):
                    for k in range(kn):
                        if norm is not None and s == 0 and t == 0:
                            pe.wait_ge(sem("m_tail"), KD * norm + k + 1)
                        if srcwait is not None and t == 0:
                            srcwait(k)
                        last = mm3(acc[2 * s + t][:, :], ws[0][:, t, k, :], ws[1][:, t, k, :],
                                   mov[0][:, k, :], mov[1][:, k, :], k == 0, k == kn - 1)
                        if k == kn - 1:
                            last.then_inc(sem(f"tile_full{s}"), 3 - tiles)
                        yield

            def both(a, b):
                yield from a
                yield from b

            def run(gen, n=1000):
                for _ in range(n):
                    if next(gen, 0) == 0:
                        return

            def norm_sums(n):
                ph = f"norm{n}"
                pe.wait_ge(sem("ssum"), 9 * n + 9)
                r = job(ph, "row", 0)
                done(nc.tensor.matmul(r[:, :], ones, ssum[:, :], start=True, stop=True), ph, "row", 0)
                r = job(ph, "col", 0)
                for b in range(NB):
                    last = nc.tensor.matmul(r[:, b:b + 1], ssum[:, b * P:(b + 1) * P], ones[:, 0:1],
                                            start=True, stop=True)
                done(last, ph, "col", 0)

            pe.wait_ge(sem("cst_in"), 16)
            pe.wait_ge(sem("x_in"), 64)
            for k in range(KD):
                r = job("xt", f"x{k}", 0)
                for b in range(NB):
                    last = nc.tensor.transpose(r[:, b * P:(b + 1) * P], xin[:, b, k * P:(k + 1) * P], ident)
                done(last, "xt", f"x{k}", 0)
            pe.wait_ge(sem("p_in"), 16 * 15)
            for t, n in ((0, 90), (1, 110), (2, 66)):
                last = nc.tensor.transpose(acc[0][:, t * P:t * P + n], prow[0:n, t, :], cst[0:n, 0:n])
            last.then_inc(sem("pv_full"), 1)
            pe.wait_ge(sem("cst_rest"), 16)

            pe.wait_ge(sem("ab_split"), 1)
            r = job("ab", "abT", 0)
            for k in range(KD):
                pe.wait_ge(sem("m_tail"), k + 1)
                last = mm3(r[0:8, :], abh[:, k, :], abl[:, k, :], mh[:, k, :], ml[:, k, :], k == 0, k == KD - 1)
            done(last, "ab", "abT", 0)

            def ab_tokens():
                read(pe, "ab", "abT", 0)
                r = job("ab", "ab", 0)
                for b in range(NB):
                    last = nc.tensor.transpose(r[:, b * 8:b * 8 + 8], abs_[:, b * P:(b + 1) * P], cst[0:8, 0:8])
                done(last, "ab", "ab", 0)

            def dn_units(g):
                return both(features(0, g, (mh, ml)), features(1, g, (mh, ml)))

            def dn_pair(p, fill):
                def each(name, h, a, b, tr=False):
                    r = job("dn", f"{name}{h}", p)
                    for n in range(NB):
                        t = slice(n * P, (n + 1) * P)
                        lhs = a if a is ones else a[:, t]
                        if tr:
                            last = nc.tensor.transpose(r[:, t], lhs, ident)
                        else:
                            last = nc.tensor.matmul(r[:, t], lhs, triu if b is triu else b[:, t], start=True, stop=True)
                    done(last, "dn", f"{name}{h}", p)
                    run(fill, 1)

                def step(name, a, b, reads=(), need=()):
                    for h in (0, 1):
                        for s_, v_ in need:
                            pe.wait_ge(sem(f"{s_}{h}"), v_)
                        for n in reads:
                            read(pe, "dn", f"{n}{h}", p)
                        e = d[h]
                        each(name, h, e[a] if a else ones, triu if b == "triu" else e[b] if b else None, tr=b is None)

                def whole(name, src):
                    for h in (0, 1):
                        pe.wait_ge(sem(f"{src}{h}"), p + 1)
                        r = job("dn", f"{name}{h}", p)
                        done(nc.tensor.matmul(r[:, :], ones, d[h]["sqo" if name == "sq_o" else src],
                                              start=True, stop=True), "dn", f"{name}{h}", p)

                whole("sq_q", "sqq")
                whole("sq_k", "sqk")
                for h in (0, 1):
                    pe.wait_ge(sem(f"gbc{h}"), p + 1)
                    each("grow", h, d[h]["gbc"], triu)
                    r = job("dn", f"gcol{h}", p)
                    nc.tensor.matmul(r[:, 0:NB], triu, gh[h][:, :], start=True, stop=True)
                    done(nc.tensor.matmul(r[:, NB:2 * NB], ones, gh[h][:, :], start=True, stop=True), "dn", f"gcol{h}", p)
                    run(fill, 1)
                step("kk", "kh", "kh", need=[("kh", p + 1)])
                step("qk", "kh", "qh", need=[("qh", p + 1)])
                step("ktok", "kh", None)
                step("vtok", "vT", None)
                step("At", "A", None, need=[("A_E", 4 * p + 1)])
                step("A2", "At", "A", ["At"])
                step("A2t", "A", "At")
                step("U1", "A2", "U", ["A2"], [("U0", p + 1)])
                step("A4", "A2t", "A2", ["A2t"])
                step("A4t", "A2", "A2t")
                step("U2", "A4", "U", ["U1", "A4"])
                step("A8", "A4t", "A4", ["A4t"])
                step("U3", "A8", "U", ["U2", "A8"])
                last = "U3"
                for w, e in (("16", "E32"), ("32", "E64"), ("64", "E128")):
                    step("T" + w, "U", None, [last], [("A_E", 4 * p + 4)] if w == "16" else [])
                    step("Y" + w, e, "U")
                    step("X" + w, "T", "Y", ["T" + w, "Y" + w])
                    last = "X" + w
                step("u", "U", "vb", [last, "vtok"])
                step("wT", "kbg", "U", ["ktok"])
                o = []
                for b in range(NB):
                    t = slice(b * P, (b + 1) * P)
                    for h in (0, 1) if b else ():
                        e = d[h]
                        read(pe, "dn", f"kv{b - 1}{h}", p)
                        if b == 1:
                            read(pe, "dn", f"wT{h}", p)
                        r = job("dn", f"ws{b}{h}", p)
                        done(nc.tensor.matmul(r[:, 0:P], e["wT"][:, t], st[h][:, :], start=True, stop=True),
                             "dn", f"ws{b}{h}", p)
                        nc.tensor.matmul(o[h][:, t], st[h][:, :], e["qd"][:, t], start=True, stop=False)
                        run(fill, 1)
                    for h in (0, 1):
                        e = d[h]
                        if b:
                            read(pe, "dn", f"ws{b}{h}", p)
                        else:
                            pe.wait_ge(sem(f"vn{h}"), p + 1)
                        if b < NB - 1:
                            r = job("dn", f"kv{b}{h}", p)
                            done(nc.tensor.matmul(r[:, 0:P], e["kd"][:, t], vn[h][:, :], start=True, stop=True),
                                 "dn", f"kv{b}{h}", p)
                        if b == 0:
                            o.append(job("dn", f"o{h}", p))
                            pe.wait_ge(sem(f"qd{h}"), p + 1)
                            read(pe, "dn", f"qk{h}", p)
                        last = nc.tensor.matmul(o[h][:, t], vn[h][:, :], e["qkD"][:, t], start=(b == 0), stop=True)
                        if b == NB - 1:
                            done(last, "dn", f"o{h}", p)
                        else:
                            last.then_inc(sem(f"o_step{h}"), 1)
                        run(fill, 1)
                run(fill)
                whole("sq_o", "sqo_dn")

            def rope_products(i):
                for n, nm_ in enumerate(("rot_q", "rot_k")):
                    pe.wait_ge(sem("acc_free0"), 2 * i + (2 * UNIT["diff"] + n + 3))
                    r = job("diff", nm_, i)
                    done(nc.tensor.matmul(r[:, :], cblk(C_PERM), qr[n][:, :], start=True, stop=True),
                         "diff", nm_, i)

            def attention(ph, i, fill, more=True):
                diff = ph == "diff"
                items = [(m, b) for b in range(NB) for m in (0, 1)] if diff else \
                    [(m, b) for m in (0, 1) for b in range(NB)]
                trs = [b for b in range(NB)] if diff else list(range(8))
                if diff:
                    pe.wait_ge(sem("roped"), 2 * i + 2)
                else:
                    pe.wait_ge(sem("acc_free0"), 2 * i + (2 * UNIT[ph] + 2))
                o = None
                per = 4 if diff else 8
                for t in range(8 + 4):
                    if t < 8:
                        m, b = items[t]
                        r = job(ph, f"s{t}", i)
                        rw = slice(HD * m, HD * m + HD)
                        done(nc.tensor.matmul(r[:, 0:(b + 1) * P], aq[rw, b * P:(b + 1) * P], ak[rw, 0:(b + 1) * P],
                                              start=True, stop=True), ph, f"s{t}", i)
                    if t == 1:
                        pe.wait_ge(sem("acc_free1"), 2 * i + (2 * UNIT[ph] + 2))
                        r = job(ph, "vt", i)
                        for b in range(NB):
                            last = nc.tensor.transpose(r[:, b * P:(b + 1) * P], vf[:, b * P:(b + 1) * P], ident)
                        done(last, ph, "vt", i)
                    run(fill, 2 if t < 8 else 1)
                    z = (t - 3) // 2 if diff and (t - 3) % 2 == 0 else t - 2 if not diff else -1
                    if 0 <= z < per:
                        b = z if diff else items[z][1]
                        pe.wait_ge(sem("pn_" + ph), per * i + z + 1)
                        r = job(ph, f"t{z}", i)
                        for k in range(b + 1):
                            last = nc.tensor.transpose(r[:, k * P:(k + 1) * P], pn[z % 2][:, k * P:(k + 1) * P], ident)
                        done(last, ph, f"t{z}", i)
                    y = (t - 4) // 2 if diff and (t - 4) % 2 == 0 else t - 3 if not diff else -1
                    if 0 <= y < per:
                        b = y if diff else items[y][1]
                        if o is None:
                            o = job(ph, "pv", i)
                        read(pe, ph, f"t{y}", i)
                        if diff:
                            dst, vc = o[:, b * P:(b + 1) * P], slice(0, P)
                        else:
                            m = items[y][0]
                            dst, vc = o[HD * m:HD * m + HD, b * P:(b + 1) * P], slice(HD * m, HD * m + HD)
                        for k in range(b + 1):
                            last = nc.tensor.matmul(dst, av[:, k, vc], pT[y % 2][:, k * P:(k + 1) * P],
                                                    start=(k == 0), stop=(k == b))
                        if y == per - 1:
                            done(last, ph, "pv", i)
                        else:
                            last.then_inc(sem("pv_" + ph), 1)
                    if t == 9 and diff and more:
                        rope_products(i)
                run(fill)
                if diff:
                    pe.wait_ge(sem("sqo_diff"), i + 1)
                    r = job(ph, "sq_o", i)
                    done(nc.tensor.matmul(r[:, :], ones, osd[:, :], start=True, stop=True),
                         ph, "sq_o", i)

            def attn_units(g):
                return both(features(0, g, (mh, ml)), features(1, g, (mh, ml), tiles=1))

            def out_proj(base, src, srcwait):
                for i in range(2):
                    for s in (0, 1):
                        run(features(s, base + i, src, srcwait=srcwait if (i, s) == (0, 0) else None))

            def mlp_layer(layer, norm):
                for n, (j0, count) in enumerate(HALVES):
                    g0 = UNIT[f"in{layer}{n}"]
                    if n == 0:
                        first = features(0, g0, (mh, ml), norm=norm)
                        run(first, KD)
                        norm_sums(norm)
                        run(first)
                        run(features(1, g0, (mh, ml)))
                    with pe.Fori(1 if n == 0 else 0, count // 2) as i:
                        for s in (0, 1):
                            run(features(s, i + g0, (mh, ml)))
                    g0 = UNIT[f"ff{layer}{n}"]
                    before = 12 * n + JF * layer

                    def products(g, src=None):
                        for s in (0, 1):
                            run(features(s, g, (ah, al), tiles=1, kn=count, srcwait=src))

                    products(g0, lambda k: pe.wait_ge(sem("a_tail"), before + k + 1))
                    with pe.Fori(1, 4) as i:
                        products(i + g0)

            first = dn_units(0)
            run(first, KD)
            ab_tokens()
            norm_sums(0)
            run(both(first, dn_units(1)))
            dn_pair(0, both(dn_units(2), dn_units(3)))
            dn_pair(1, attn_units(UNIT["diff"]))
            rope_products(-1)
            with pe.Fori(0, NH - 1) as i:
                attention("diff", i, attn_units(i + (UNIT["diff"] + 1)))
            attention("diff", NH - 1, iter(()), more=False)
            out_proj(UNIT["out0"], (oh, ol),
                     lambda k: pe.wait_ge(sem("oc_tail" if k < NH else "o_tail"), k % NH + 1))
            mlp_layer(0, 1)
            first = both(features(0, UNIT["odd"], (mh, ml), norm=2), features(1, UNIT["odd"], (mh, ml), tiles=1))
            run(first, KD)
            norm_sums(2)
            run(first)
            with pe.Fori(0, NPAIR - 1) as i:
                attention("odd", i, attn_units(i + (UNIT["odd"] + 1)))
            attention("odd", NPAIR - 1, iter(()))
            out_proj(UNIT["out1"], (oh, ol), lambda k: read(pe, "odd", "pv", k))
            mlp_layer(1, 3)
            norm_sums(4)
            for k in range(KD):
                r = job("yt", f"x{k}", 0)
                pe.wait_ge(sem("x_gain"), k + 1)
                for b in range(NB):
                    last = nc.tensor.transpose(r[:, b * P:(b + 1) * P], x[:, k, b * P:(b + 1) * P], ident)
                done(last, "yt", f"x{k}", 0)

        @block.scalar
        def _(act):
            A = nc.scalar.activation

            def x_tile(norm, k, s):
                g = pv[:, bass.ds(k + PV_NORM[norm], 1)]
                if norm < 4:
                    A(dyn(mh, k), dyn(x, k), ACT.Copy, scale=g).then_inc(sem("m_head"), 1)
                settled(act, ("ssum", k + max(9 * norm, 1)))
                A(sq[s][:, :], dyn(x, k), ACT.Square).then_inc(sem("sq_full"), 1)
                if norm == 4:
                    settled(act, ("sq_full", k + (KD * norm + 1)))
                    A(dyn(x, k), dyn(x, k), ACT.Copy, scale=g).then_inc(sem("x_gain"), 1)

            def norm_roots(n):
                ph = f"norm{n}"
                if n:
                    act.wait_ge(sem("rstd"), 2 * n)
                r = full(act, ph, "row", 0)
                free(A(rstd[:, :], r[:, :], ACT.Sqrt, bias=epsc[:, :], scale=1.0 / D), ph, "row", 0)
                r = full(act, ph, "col", 0)
                free(A(sdc[:, :], r[:, 0:NB], ACT.Sqrt, bias=epsc[:, :], scale=1.0 / D), ph, "col", 0)

            for k in range(KD):
                r = full(act, "xt", f"x{k}", 0)
                free(A(xs[:, k, :], r[:, :], ACT.Copy), "xt", f"x{k}", 0)
            act.wait_ge(sem("zeros"), 3)
            act.wait_ge(sem("pv_copied"), 1)
            act.wait_ge(sem("p_in"), 16 * 15)
            A(abh[:, :, :], abw[:, :, :], ACT.Copy).then_inc(sem("ab_head"), 1)
            for k in range(KD):
                read(act, "xt", f"x{k}", 0)
                A(mh[:, k, :], xs[:, k, :], ACT.Copy, scale=pv[:, k:k + 1]).then_inc(sem("m_head"), 1)
            units_split_act(act, 0, 0)
            for k in range(KD):
                act.wait_ge(sem("ssum"), k + 1)
                A(sq[k % 2][:, :], xs[:, k, :], ACT.Square).then_inc(sem("sq_full"), 1)
                if k == KD // 2 - 1:
                    units_split_act(act, 1, 0)
            norm_roots(0)

            act.wait_ge(sem("ab_in"), 1)
            A(abt[1][:, :, :], abt[1][:, :, :], ACT.Exp, scale=-1.0).then_inc(sem("ab_e"), 1)
            A(abt[2][:, :, :], abz[:, :, 4:8], ACT.Exp, scale=-1.0).then_inc(sem("ab_e"), 1)
            A(alog[:, :], alog[:, :], ACT.Exp).then_inc(sem("ab_e"), 1)
            A(ls[:, 0:2], ls[:, 0:2], ACT.Exp).then_inc(sem("ab_e"), 1)
            act.wait_ge(sem("ab_e"), 4)
            A(abt[1][:, :, :], abt[1][:, :, :], ACT.Ln, bias=1.0).then_inc(sem("ab_e"), 1)

            def conv(i, c, slot, g, tile, dst):
                waits = [(f"acc_free{slot}", g)]
                if 3 * i + c:
                    waits.append(("silu", 3 * i + c))
                settled(act, *waits)
                A(cta[0][:, :], cb[c % 2][:, ALPHA - 3:ALPHA - 3 + S], ACT.Copy,
                  scale=pv[:, PV_DNC + tile + i:PV_DNC + tile + i + 1]).then_inc(sem("tap"), 1)
                act.wait_ge(sem("conv"), 9 * i + (3 * c + 3))
                A(dst, cta[0][:, :], ACT.Silu).then_inc(sem("silu"), 1)

            def dn_evac(i, g):
                h, p = i % 2, i // 2
                e = d[h]
                yield conv(i, 0, 0, 2 * g + 1, 0, e["qT"])
                conv(i, 1, 0, 2 * g + 2, 4, e["kT"])
                act.wait_ge(sem("silu"), 3 * i + 2)
                if p:
                    act.wait_ge(sem(f"qh{h}"), p)
                for n, src in (("sqq", "qT"), ("sqk", "kT")):
                    A(e[n], e[src], ACT.Square).then_inc(sem(f"{n}{h}"), 1)
                yield units_split_act(act, 0, g + 1)
                yield conv(i, 2, 1, 2 * g + 1, 8, e["vT"])
                act.wait_ge(sem("acc_free1"), 2 * g + 2)
                A(e["gN"], e["gN"], ACT.Silu).then_inc(sem(f"gate_full{h}"), 1)
                yield units_split_act(act, 1, g + 1)

            def feat_evac(ph, g):
                yield
                yield units_split_act(act, 0, g + 1)
                yield
                yield units_split_act(act, 1, g + 1)

            def each4(gen):
                for _ in range(4):
                    next(gen, 0)

            def chained(*gens):
                for g in gens:
                    yield from g

            def copy_out(name, dst, p):
                for h in (0, 1):
                    r = full(act, "dn", f"{name}{h}", p)
                    free(A(d[h][dst], r[:, :], ACT.Copy), "dn", f"{name}{h}", p)

            def dn_pair(p, evac):
                for h in (0, 1):
                    for n, j in (("sqk", "sq_k"), ("sqq", "sq_q")):
                        r = full(act, "dn", f"{j}{h}", p)
                        free(A(d[h][n], r[:, :], ACT.Sqrt, bias=epsc[:, :]), "dn", f"{j}{h}", p)
                for h in (0, 1):
                    e = d[h]
                    act.wait_ge(sem(f"gc{h}"), p + 1)
                    A(eg[h][:, :], gc[h][:, :], ACT.Exp).then_inc(sem(f"eg{h}"), 1)
                    r = full(act, "dn", f"grow{h}", p)
                    act.wait_ge(sem(f"dm{h}"), p + 1)
                    free(A(e["qd"], r[:, :], ACT.Exp), "dn", f"grow{h}", p)
                    A(e["decN"], e["decN"], ACT.Exp, scale=-1.0).then_inc(sem(f"eN{h}"), 1)
                    A(e["decT"], e["decT"], ACT.Exp).then_inc(sem(f"eT{h}"), 1)
                copy_out("At", "At", p)
                copy_out("A2", "A2", p)
                next(evac, 0)
                copy_out("A4", "A4", p)
                next(evac, 0)
                copy_out("A8", "A8", p)
                next(evac, 0)
                copy_out("T16", "T", p)
                next(evac, 0)
                copy_out("T32", "T", p)
                next(evac, 0)
                copy_out("T64", "T", p)
                next(evac, 0)
                copy_out("wT", "wT", p)
                next(evac, 0)
                next(evac, 0)
                for h in (0, 1):
                    r = full(act, "dn", f"o{h}", p)
                    A(d[h]["sqo"], r[:, :], ACT.Square).then_inc(sem(f"sqo_dn{h}"), 1)
                for h in (0, 1):
                    r = full(act, "dn", f"sq_o{h}", p)
                    free(A(d[h]["sqo"], r[:, :], ACT.Sqrt, bias=epsc[:, :], scale=1.0 / P), "dn", f"sq_o{h}", p)

            each4(dn_evac(0, 0))
            each4(dn_evac(1, 1))
            dn_pair(0, chained(dn_evac(2, 2), dn_evac(3, 3)))
            dn_pair(1, feat_evac("diff", UNIT["diff"]))

            def attention(ph, i, o0, evac):
                diff = ph == "diff"
                items = [(m, b) for b in range(NB) for m in (0, 1)] if diff else \
                    [(m, b) for m in (0, 1) for b in range(NB)]
                per = 4 if diff else 8
                for t in range(8 + 4):
                    if t < 8:
                        w = (items[t][1] + 1) * P
                        read(act, ph, f"s{t}", i)
                        if t >= 2 and diff:
                            act.wait_ge(sem("pn_diff"), 4 * i + t // 2)
                        elif t >= 2:
                            act.wait_ge(sem("pn_odd"), 8 * i + (t - 1))
                        A(pr[t % 2][:, 0:w], ns[t % 2][:, 0:w], ACT.Exp, bias=nm[:, t:t + 1], scale=-1.0,
                          accum_out=rs[:, t:t + 1]).then_inc(sem("exp_" + ph), 1)
                    if t == 1:
                        r = full(act, ph, "vt", i)
                        free(A(av[:, :, :], blk(r[:, :]), ACT.Copy), ph, "vt", i)
                    z = (t - 3) // 2 if diff and (t - 3) % 2 == 0 else t - 2 if not diff else -1
                    if 0 <= z < per:
                        b = z if diff else items[z][1]
                        pv_wait(ph, i, z, per)
                        r = full(act, ph, f"t{z}", i)
                        free(A(pT[z % 2][:, 0:(b + 1) * P], r[:, 0:(b + 1) * P], ACT.Copy), ph, f"t{z}", i)
                    if t == 8:
                        next(evac, 0)
                        next(evac, 0)
                if diff:
                    act.wait_ge(sem("o_done"), NH)
                    A(dyn(oh, i), dyn(om, i), ACT.Copy).then_inc(sem("oc_head"), 1)
                    r = full(act, ph, "pv", i)
                    A(osd[:, :], r[:, :], ACT.Square).then_inc(sem("sqo_diff"), 1)
                    r = full(act, ph, "sq_o", i)
                    free(A(osd[:, :], r[:, :], ACT.Sqrt, bias=epsc[:, :], scale=1.0 / P), ph, "sq_o", i)
                    settled(act, is_read(ph, "pv", i))
                    A(dyn(oh, i + o0), osb[:, :], ACT.Copy).then_inc(sem("o_head"), 1)
                else:
                    settled(act, is_full(ph, "pv", i))
                    A(dyn(oh, i + o0), R[3][:, :], ACT.Copy).then_inc(sem("o_head"), 1)
                next(evac, 0)
                next(evac, 0)

            def pv_wait(ph, i, z, per):
                if z >= 2:
                    act.wait_ge(sem("pv_" + ph), (per - 1) * i + z - 1)
                elif z == 1:
                    if not (isinstance(i, int) and i == 0):
                        b, n = BANK.use(ph, "pv", i)
                        act.wait_ge(sem(f"R{b}_full"), n)

            with act.Fori(0, NH - 1) as i:
                attention("diff", i, NH, feat_evac("diff", i + (UNIT["diff"] + 1)))
            attention("diff", NH - 1, NH, iter(()))

            def out_proj(base, norm):
                with act.Fori(0, 2) as i:
                    for s in (0, 1):
                        for t in (0, 1):
                            settled(act, (f"acc_free{s}", 2 * i + (2 * base + t + 1)))
                            x_tile(norm, 4 * i + (2 * s + t), t)
                        units_split_act(act, s, i + (base + 1))

            def mlp(layer, norm_after, last):
                for n, (j0, count) in enumerate(HALVES):
                    g0 = UNIT[f"in{layer}{n}"]
                    base = 11 * layer + 6 * n
                    with act.Fori(0, count // 2) as i:
                        for s in (0, 1):
                            j = 2 * i + (j0 + s)
                            settled(act, (f"acc_free{s}", 2 * i + (2 * g0 + 1)))
                            A(cta[s][:, :], cb[s][:, ALPHA - 2:ALPHA - 2 + S], ACT.Identity,
                              bias=pv[:, bass.ds(j + (PV_CB + JF * layer), 1)],
                              scale=pv[:, bass.ds(j + PV_CW[layer], 1)]).then_inc(sem("mtap"), 1)
                            act.wait_ge(sem(f"mconv{s}"), 2 * i + (2 * base + 2))
                            A(sl[s][:, :], cta[s][:, :], ACT.Silu).then_inc(sem("msilu"), 1)
                            settled(act, ("prod", 2 * i + (2 * base + s + 1)))
                            A(dyn(ah, 2 * i + s), pd[s][:, :], ACT.Copy).then_inc(sem("a_head"), 1)
                            units_split_act(act, s, i + (g0 + 1))
                    g0 = UNIT[f"ff{layer}{n}"]

                    def x_tiles(i, g, split):
                        for s in (0, 1):
                            if n == 1:
                                settled(act, (f"acc_free{s}", 2 * g + 2))
                                x_tile(norm_after, 2 * i + s, s)
                            if split:
                                units_split_act(act, s, g + 1)

                    with act.Fori(0, 3 if last and n == 1 else 4) as i:
                        x_tiles(i, i + g0, True)
                    if last and n == 1:
                        x_tiles(3, g0 + 3, False)

            out_proj(UNIT["out0"], 1)
            norm_roots(1)
            mlp(0, 2, False)
            norm_roots(2)
            each4(feat_evac("odd", UNIT["odd"]))
            with act.Fori(0, NPAIR - 1) as i:
                attention("odd", i, 0, feat_evac("odd", i + (UNIT["odd"] + 1)))
            attention("odd", NPAIR - 1, 0, iter(()))
            out_proj(UNIT["out1"], 3)
            norm_roots(3)
            mlp(1, 4, True)
            norm_roots(4)

        @block.vector
        def _(dve):
            V = nc.vector
            step = sem("dve_step")

            def norm_rstd(n):
                ph = f"norm{n}"
                read(dve, ph, "row", 0)
                V.reciprocal(rstd[:, :], rstd[:, :]).then_inc(sem("rstd"), 1)
                read(dve, ph, "col", 0)
                V.reciprocal(rcol[:, :], sdc[:, :]).then_inc(sem("rstd"), 1)
                dve.wait_ge(sem("rstd"), 2 * n + 2)

            def x_tail(norm, k):
                dve.wait_ge(sem("m_head"), k + (KD * norm + 1))
                V.scalar_tensor_tensor(out=dyn(ml, k), in0=dyn(x if norm else xs, k), scalar=pv[:, bass.ds(k + PV_NORM[norm], 1)],
                                       in1=dyn(mh, k).bitcast(F32), op0=ALU.mult, op1=ALU.subtract)\
                    .then_inc(sem("m_tail"), 1)

            dve.wait_ge(sem("pv_full"), 1)
            for t, n in ((0, 90), (1, 110), (2, 66)):
                ins = V.tensor_copy(pv[:, t * P:t * P + n], acc[0][:, t * P:t * P + n])
            ins.then_inc(sem("pv_copied"), 1)
            dve.wait_ge(sem("pv_copied"), 1)
            dve.wait_ge(sem("ab_head"), 1)
            V.tensor_tensor(abl[:, :, :], abw[:, :, :], abh[:, :, :].bitcast(F32), ALU.subtract)\
                .then_inc(sem("ab_split"), 1)
            for k in range(KD):
                x_tail(0, k)
            for s in (0, 1):
                units_split_dve(dve, s, 0)
            r = full(dve, "ab", "abT", 0)
            free(V.tensor_copy(abs_[:, :], r[0:8, :]), "ab", "abT", 0)
            V.tensor_scalar(sub8[:, :], pv[:, PV_SUB:PV_SUB + 1], 1.0 - LAM_INIT, None, ALU.mult).then_inc(step, 1)
            norm_rstd(0)

            n_step = [1]

            def chain(ins):
                n_step[0] += 1
                ins.then_inc(step, 1)
                dve.wait_ge(step, n_step[0])

            r = full(dve, "ab", "ab", 0)
            ins = V.tensor_tensor(abz[:, :, :], r[:, 0:NB * 8].rearrange("p (b n) -> p b n", n=8),
                                  rcol[:, :].unsqueeze(2).broadcast_to([P, NB, 8]), ALU.mult)
            free(ins, "ab", "ab", 0)
            read(dve, "ab", "ab", 0)
            chain(V.tensor_tensor(abt[0][:, :, :], abz[:, :, 0:4], dtb[:, :].unsqueeze(1).broadcast_to([P, NB, NH]),
                                  ALU.add))
            chain(V.tensor_tensor(lt[:, :, :], lp[:, :].rearrange("p (a b n) -> p a b n", a=2, b=2)[:, :, 0, :],
                                  lp[:, :].rearrange("p (a b n) -> p a b n", a=2, b=2)[:, :, 1, :], ALU.mult))
            chain(V.reduce_sum(ls[:, 0:2], lt[:, :, :], mybir.AxisListType.X))
            chain(V.tensor_scalar(abt[4][:, :, :], abt[0][:, :, :], -1.0, None, ALU.mult))
            V.tensor_tensor(abt[1][:, :, :], abt[0][:, :, :], abt[4][:, :, :], ALU.max).then_inc(sem("ab_in"), 1)
            chain(V.tensor_scalar(abt[0][:, :, :], abt[0][:, :, :], 0.0, None, ALU.max))
            dve.wait_ge(sem("ab_e"), 5)
            chain(V.tensor_tensor(abt[0][:, :, :], abt[0][:, :, :], abt[1][:, :, :], ALU.add))
            chain(V.tensor_tensor(abt[3][:, :, :], abt[0][:, :, :], alog[:, :].unsqueeze(1).broadcast_to([P, NB, NH]),
                                  ALU.mult))
            chain(V.tensor_scalar(gall[:, :, :], abt[3][:, :, :].rearrange("p b h -> p h b"), -1.0, None, ALU.mult))
            chain(V.tensor_scalar(abt[2][:, :, :], abt[2][:, :, :], 1.0, None, ALU.add))
            chain(V.reciprocal(ball[:, :, :], abt[2][:, :, :].rearrange("p b h -> p h b")))
            chain(V.tensor_tensor(ls[:, 2:3], ls[:, 1:2], ls[:, 0:1], ALU.subtract))
            chain(V.tensor_scalar(lamc[:, :], ls[:, 2:3], -LAM_INIT, None, ALU.add))

            def conv(i, c, slot, g, tile):
                buf = cb[c % 2]
                dve.wait_ge(sem(f"tile_full{slot}"), g)
                if 3 * i + c:
                    dve.wait_ge(sem("conv"), 9 * i + 3 * c)
                V.tensor_tensor(buf[:, ALPHA:ALPHA + S], acc[c][:, :], rstd[:, :], ALU.mult)\
                    .then_inc(sem(f"acc_free{slot}"), 1)
                dve.wait_ge(sem("tap"), 3 * i + (c + 1))
                for tap in (1, 2, 3):
                    if tap > 1:
                        dve.wait_ge(sem("conv"), 9 * i + (3 * c + tap - 1))
                    o = ALPHA - 3 + tap
                    V.scalar_tensor_tensor(out=cta[0][:, :], in0=buf[:, o:o + S],
                                           scalar=pv[:, PV_DNC + 12 * tap + tile + i:PV_DNC + 12 * tap + tile + i + 1],
                                           in1=cta[0][:, :], op0=ALU.mult, op1=ALU.add).then_inc(sem("conv"), 1)

            def dn_evac(i, g):
                h, p = i % 2, i // 2
                yield conv(i, 0, 0, 2 * g + 1, 0)
                conv(i, 1, 0, 2 * g + 2, 4)
                yield units_split_dve(dve, 0, g + 1)
                yield conv(i, 2, 1, 2 * g + 1, 8)
                dve.wait_ge(sem("tile_full1"), 2 * g + 2)
                if p:
                    dve.wait_ge(sem(f"gC_full{h}"), p)
                V.tensor_tensor(d[h]["gN"], acc[3][:, :], rstd[:, :], ALU.mult).then_inc(sem("acc_free1"), 1)
                yield units_split_dve(dve, 1, g + 1)

            def att_evac(ph, i, g):
                diff = ph == "diff"
                prev = not (isinstance(i, int) and i == 0)
                dve.wait_ge(sem("tile_full0"), 2 * g + 1)
                if diff:
                    V.scalar_tensor_tensor(out=qr[0][:, :], in0=acc[0][:, :], scalar=QSCALE, in1=rstd[:, :],
                                           op0=ALU.mult, op1=ALU.mult).then_inc(sem("acc_free0"), 1)
                    dve.wait_ge(sem("tile_full0"), 2 * g + 2)
                    V.tensor_tensor(qr[1][:, :], acc[1][:, :], rstd[:, :], ALU.mult).then_inc(sem("acc_free0"), 1)
                else:
                    if prev:
                        full(dve, ph, "s7", i - 1)
                    V.scalar_tensor_tensor(out=aq[:, :], in0=acc[0][:, :], scalar=QSCALE, in1=rstd[:, :],
                                           op0=ALU.mult, op1=ALU.mult).then_inc(sem("acc_free0"), 1)
                    dve.wait_ge(sem("tile_full0"), 2 * g + 2)
                    V.tensor_tensor(ak[:, :], acc[1][:, :], rstd[:, :], ALU.mult).then_inc(sem("acc_free0"), 1)
                yield
                yield units_split_dve(dve, 0, g + 1)
                dve.wait_ge(sem("tile_full1"), 2 * g + 2)
                if prev:
                    full(dve, ph, "vt", i - 1)
                V.tensor_tensor(vf[:, :], acc[2][:, :], rstd[:, :], ALU.mult)\
                    .then_inc(sem("acc_free1"), 2)
                yield
                yield units_split_dve(dve, 1, g + 1)

            def rope(i):
                for n, (name, dst) in enumerate((("rot_q", aq), ("rot_k", ak))):
                    b, u = BANK.use("diff", name, i - 1)
                    dve.wait_ge(sem(f"R{b}_full"), u + 1)
                    V.tensor_tensor(dst[:, :], R[b][:, :], cst[:, C_SIN:C_SIN + S], ALU.mult)\
                        .then_inc(sem(f"R{b}_read"), 1)
                    dve.wait_ge(sem(f"R{b}_read"), u + 1)
                    dve.wait_ge(sem("qc_full"), 2 * i + n + 1)
                    V.tensor_tensor(dst[:, :], dst[:, :], qc[n][:, :], ALU.add).then_inc(sem("roped"), 1)

            def dn_pair(p, evac):
                def own(ins, name, n):
                    ins.then_inc(sem(name), 1)
                    dve.wait_ge(sem(name), n)

                def beta(h):
                    return ball[:, 2 * p + h, :]

                for h in (0, 1):
                    g_i = gall[:, 2 * p + h, :]
                    V.tensor_copy(gh[h][:, :], g_i)
                    V.tensor_copy(blk(d[h]["gbc"]), cols(g_i)).then_inc(sem(f"gbc{h}"), 1)
                for h in (0, 1):
                    e = d[h]
                    read(dve, "dn", f"sq_k{h}", p)
                    own(V.reciprocal(e["sqk"], e["sqk"]), f"inv{h}", 2 * p + 1)
                    V.tensor_tensor(e["kh"], e["kT"], e["sqk"], ALU.mult).then_inc(sem(f"kh{h}"), 1)
                for h in (0, 1):
                    e = d[h]
                    r = full(dve, "dn", f"gcol{h}", p)
                    free(V.tensor_copy(gc[h][:, 0:2 * NB], r[:, 0:2 * NB]), "dn", f"gcol{h}", p)
                    read(dve, "dn", f"gcol{h}", p)
                    own(V.tensor_tensor(gc[h][:, 2 * NB:], gc[h][:, NB:2 * NB], gc[h][:, 0:NB], ALU.subtract),
                        f"gc{h}", p + 1)
                    r = full(dve, "dn", f"grow{h}", p)
                    own(V.tensor_tensor(blk(e["decT"]), blk(r[:, :]), cols(gc[h][:, 0:NB]), ALU.subtract),
                        f"diffs{h}", 2 * p + 1)
                    own(V.tensor_scalar(e["decN"], e["decT"], 0.0, None, ALU.max), f"diffs{h}", 2 * p + 2)
                    V.tensor_scalar(e["decT"], e["decT"], 0.0, None, ALU.min).then_inc(sem(f"dm{h}"), 1)
                for h in (0, 1):
                    e = d[h]
                    read(dve, "dn", f"sq_q{h}", p)
                    own(V.reciprocal(e["sqq"], e["sqq"]), f"inv{h}", 2 * p + 2)
                    V.scalar_tensor_tensor(out=e["qh"], in0=e["qT"], scalar=float(P) ** -0.5, in1=e["sqq"],
                                           op0=ALU.mult, op1=ALU.mult).then_inc(sem(f"qh{h}"), 1)
                for h in (0, 1):
                    e = d[h]
                    r = full(dve, "dn", f"kk{h}", p)
                    free(V.tensor_tensor(blk(e["N"]), blk(r[:, :]), cols(beta(h)), ALU.mult), "dn", f"kk{h}", p)
                    read(dve, "dn", f"kk{h}", p)
                    dve.wait_ge(sem(f"decN{h}"), p + 1)
                    own(V.tensor_tensor(e["N"], e["N"], e["decN"], ALU.mult), f"N{h}", p + 1)
                for h in (0, 1):
                    e = d[h]
                    dve.wait_ge(sem(f"eg{h}"), p + 1)
                    V.tensor_tensor(be[h][:, :], beta(h), eg[h][:, 0:NB], ALU.mult).then_inc(sem(f"be{h}"), 1)
                    r = full(dve, "dn", f"qk{h}", p)
                    dve.wait_ge(sem(f"decT{h}"), p + 1)
                    free(V.tensor_tensor(e["qkD"], r[:, :], e["decT"], ALU.mult), "dn", f"qk{h}", p)
                for h in (0, 1):
                    e = d[h]
                    r = full(dve, "dn", f"ktok{h}", p)
                    dve.wait_ge(sem(f"be{h}"), p + 1)
                    V.tensor_tensor(blk(e["kd"]), blk(r[:, :]), cols(eg[h][:, 2 * NB:]), ALU.mult)
                    dve.wait_ge(sem(f"qd{h}"), p + 1)
                    free(V.tensor_tensor(blk(e["kbg"]), blk(r[:, :]), cols(be[h][:, :]), ALU.mult), "dn", f"ktok{h}", p)
                    r = full(dve, "dn", f"vtok{h}", p)
                    free(V.tensor_tensor(blk(e["vb"]), blk(r[:, :]), cols(beta(h)), ALU.mult), "dn", f"vtok{h}", p)
                for h in (0, 1):
                    e = d[h]
                    read(dve, "dn", f"At{h}", p)
                    V.tensor_tensor(blk(e["U"]), rows(ident), blk(e["At"]), ALU.subtract).then_inc(sem(f"U0{h}"), 1)

                def copy(name, dst):
                    for h in (0, 1):
                        r = full(dve, "dn", f"{name}{h}", p)
                        free(V.tensor_copy(d[h][dst], r[:, :]), "dn", f"{name}{h}", p)

                def update(name, op, before=None):
                    for h in (0, 1):
                        r = full(dve, "dn", f"{name}{h}", p)
                        if before:
                            read(dve, "dn", f"{before}{h}", p)
                        else:
                            dve.wait_ge(sem(f"U0{h}"), p + 1)
                        free(V.tensor_tensor(d[h]["U"], d[h]["U"], r[:, :], op), "dn", f"{name}{h}", p)

                copy("A2t", "A2t")
                update("U1", ALU.add)
                next(evac, 0)
                copy("A4t", "A4t")
                update("U2", ALU.add, "U1")
                next(evac, 0)
                update("U3", ALU.add, "U2")
                next(evac, 0)
                copy("Y16", "Y")
                update("X16", ALU.subtract, "U3")
                next(evac, 0)
                copy("Y32", "Y")
                update("X32", ALU.subtract, "X16")
                next(evac, 0)
                copy("Y64", "Y")
                update("X64", ALU.subtract, "X32")
                next(evac, 0)
                for h in (0, 1):
                    e = d[h]
                    r = full(dve, "dn", f"u{h}", p)
                    V.tensor_copy(vn[h][:, :], r[:, 0:P]).then_inc(sem(f"vn{h}"), 1)
                    free(V.tensor_copy(e["u"], r[:, :]), "dn", f"u{h}", p)
                    read(dve, "dn", f"u{h}", p)
                for b in range(NB - 1):
                    for h in (0, 1):
                        r = full(dve, "dn", f"kv{b}{h}", p)
                        if b == 0:
                            ins = V.tensor_copy(st[h][:, :], r[:, 0:P])
                        else:
                            read(dve, "dn", f"kv{b - 1}{h}", p)
                            ins = V.scalar_tensor_tensor(out=st[h][:, :], in0=st[h][:, :],
                                                         scalar=eg[h][:, NB + b:NB + b + 1],
                                                         in1=r[:, 0:P], op0=ALU.mult, op1=ALU.add)
                        free(ins, "dn", f"kv{b}{h}", p)
                    for h in (0, 1):
                        dve.wait_ge(sem(f"o_step{h}"), 3 * p + b + 1)
                        r = full(dve, "dn", f"ws{b + 1}{h}", p)
                        free(V.tensor_tensor(vn[h][:, :], d[h]["u"][:, (b + 1) * P:(b + 2) * P], r[:, 0:P],
                                             ALU.subtract), "dn", f"ws{b + 1}{h}", p)
                next(evac, 0)
                next(evac, 0)
                for h in (0, 1):
                    e = d[h]
                    read(dve, "dn", f"sq_o{h}", p)
                    own(V.reciprocal(e["sqo"], e["sqo"]), f"inv_o{h}", p + 1)
                    r = full(dve, "dn", f"o{h}", p)
                    free(V.scalar_tensor_tensor(out=e["on"], in0=r[:, :], scalar=pv[:, PV_DNN:PV_DNN + 1],
                                                in1=e["sqo"], op0=ALU.mult, op1=ALU.mult), "dn", f"o{h}", p)
                    read(dve, "dn", f"o{h}", p)
                    dve.wait_ge(sem(f"gC_full{h}"), p + 1)
                    dve.wait_ge(sem("x_kept"), 16)
                    V.tensor_tensor(om[:, 2 * p + h, :], e["on"], e["gC"], ALU.mult).then_inc(sem("o_done"), 1)

            def chained(*gens):
                for g in gens:
                    yield from g

            for _ in chained(dn_evac(0, 0), dn_evac(1, 1)):
                pass
            dn_pair(0, chained(dn_evac(2, 2), dn_evac(3, 3)))
            dn_pair(1, att_evac("diff", 0, UNIT["diff"]))
            rope(0)

            def attention(ph, i, o0, h0, evac, more=True):
                diff = ph == "diff"
                items = [(m, b) for b in range(NB) for m in (0, 1)] if diff else \
                    [(m, b) for m in (0, 1) for b in range(NB)]
                for t in range(8 + 2):
                    if t == 9 and diff and more:
                        next(evac, 0)
                        rope(i + 1)
                    if t < 8:
                        m, b = items[t]
                        w = (b + 1) * P
                        waits = [is_full(ph, f"s{t}", i)]
                        if t >= 2:
                            waits.append(("exp_" + ph, 8 * i + (t - 1)))
                        bias = cst[:, C_MASK + S - w:C_MASK + S] if diff else gb[m][:, S - w:S]
                        if not diff and b == 0:
                            waits += [(f"gb_full{m}", 32 * i + 32), ("gb_mask", 2)]
                        settled(dve, *waits)
                        r = R[BANK.use(ph, f"s{t}", i)[0]]
                        free(V.tensor_tensor_reduce(out=ns[t % 2][:, 0:w], in0=r[:, 0:w], in1=bias, scale=-1.0,
                                                    scalar=3e38, op0=ALU.add, op1=ALU.min,
                                                    accum_out=nm[:, t:t + 1]), ph, f"s{t}", i)
                    if diff:
                        if t % 2 == 0 and 2 <= t:
                            z = (t - 2) // 2
                            w = (z + 1) * P
                            dve.wait_ge(sem("exp_diff"), 8 * i + (2 * z + 2))
                            if z:
                                dve.wait_ge(sem("pn_diff"), 4 * i + z)
                            V.reciprocal(rr[:, 0:2], rs[:, 2 * z:2 * z + 2]).then_inc(sem("nrm_diff"), 1)
                            dve.wait_ge(sem("nrm_diff"), 12 * i + (3 * z + 1))
                            V.tensor_tensor(rr[:, 2:3], rr[:, 1:2], lamc[:, :], ALU.mult).then_inc(sem("nrm_diff"), 1)
                            dve.wait_ge(sem("nrm_diff"), 12 * i + (3 * z + 2))
                            if z >= 2:
                                tb, tu = BANK.use("diff", f"t{z - 2}", i)
                                dve.wait_ge(sem(f"R{tb}_full"), tu + 1)
                            V.tensor_scalar(pn[z % 2][:, 0:w], pr[1][:, 0:w], rr[:, 2:3], None, ALU.mult)\
                                .then_inc(sem("nrm_diff"), 1)
                            dve.wait_ge(sem("nrm_diff"), 12 * i + (3 * z + 3))
                            V.scalar_tensor_tensor(out=pn[z % 2][:, 0:w], in0=pr[0][:, 0:w], scalar=rr[:, 0:1],
                                                   in1=pn[z % 2][:, 0:w], op0=ALU.mult, op1=ALU.add)\
                                .then_inc(sem("pn_diff"), 1)
                    elif 1 <= t <= 8:
                        z = t - 1
                        w = (items[z][1] + 1) * P
                        dve.wait_ge(sem("exp_odd"), 8 * i + (z + 1))
                        if z >= 2:
                            dve.wait_ge(sem("pn_odd"), 8 * i + (z - 1))
                        V.reciprocal(rr[:, z % 2:z % 2 + 1], rs[:, z:z + 1]).then_inc(sem("nrm_odd"), 1)
                        dve.wait_ge(sem("nrm_odd"), 8 * i + (z + 1))
                        if z >= 2:
                            tb, tu = BANK.use("odd", f"t{z - 2}", i)
                            dve.wait_ge(sem(f"R{tb}_full"), tu + 1)
                        V.tensor_scalar(pn[z % 2][:, 0:w], pr[z % 2][:, 0:w], rr[:, z % 2:z % 2 + 1], None, ALU.mult)\
                            .then_inc(sem("pn_odd"), 1)
                    if t == 8 and not diff:
                        next(evac, 0)
                        next(evac, 0)
                next(evac, 0)
                if diff:
                    next(evac, 0)
                    dve.wait_ge(sem("oc_head"), i + 1)
                    V.tensor_tensor(dyn(ol, i), dyn(om, i), dyn(oh, i).bitcast(F32), ALU.subtract)\
                        .then_inc(sem("oc_tail"), 1)
                r = full(dve, ph, "pv", i)
                if diff:
                    read(dve, ph, "sq_o", i)
                    V.reciprocal(osd[:, :], osd[:, :]).then_inc(sem("inv_od"), 1)
                    dve.wait_ge(sem("inv_od"), i + 1)
                    free(V.scalar_tensor_tensor(out=osb[:, :], in0=r[:, :], scalar=sub8[:, :], in1=osd[:, :],
                                                op0=ALU.mult, op1=ALU.mult), ph, "pv", i)
                    src = osb[:, :]
                    dve.wait_ge(sem("o_head"), i + (h0 + 1))
                    V.tensor_tensor(dyn(ol, i + o0), src, dyn(oh, i + o0).bitcast(F32), ALU.subtract)\
                        .then_inc(sem("o_tail"), 1)
                else:
                    dve.wait_ge(sem("o_head"), i + (h0 + 1))
                    free(V.tensor_tensor(dyn(ol, i + o0), r[:, :], dyn(oh, i + o0).bitcast(F32), ALU.subtract),
                         ph, "pv", i)
                next(evac, 0)

            def out_proj(base, norm):
                with dve.Fori(0, 2) as i:
                    for s in (0, 1):
                        for t in (0, 1):
                            k = 4 * i + (2 * s + t)
                            dve.wait_ge(sem(f"tile_full{s}"), 2 * i + (2 * base + t + 1))
                            if norm == 1:
                                dve.wait_ge(sem("x_back"), 16 * KD // 2)
                            V.tensor_tensor(dyn(x, k), dyn(x, k), acc[2 * s + t][:, :], ALU.add)\
                                .then_inc(sem(f"acc_free{s}"), 1)
                            x_tail(norm, k)
                        units_split_dve(dve, s, i + (base + 1))

            def mlp(layer, norm_after, last):
                for n, (j0, count) in enumerate(HALVES):
                    g0 = UNIT[f"in{layer}{n}"]
                    base = 11 * layer + 6 * n
                    with dve.Fori(0, count // 2) as i:
                        for s in (0, 1):
                            j = 2 * i + (j0 + s)
                            w0 = PV_CW[layer]
                            dve.wait_ge(sem(f"tile_full{s}"), 2 * i + (2 * g0 + 1))
                            V.tensor_tensor(cb[s][:, ALPHA:ALPHA + S], acc[2 * s][:, :], rstd[:, :], ALU.mult)\
                                .then_inc(sem(f"acc_free{s}"), 1)
                            dve.wait_ge(sem("mtap"), 2 * i + (2 * base + s + 1))
                            for tap in (1, 2):
                                if tap == 2:
                                    dve.wait_ge(sem(f"mconv{s}"), 2 * i + (2 * base + 1))
                                o = ALPHA - 2 + tap
                                V.scalar_tensor_tensor(out=cta[s][:, :], in0=cb[s][:, o:o + S],
                                                       scalar=pv[:, bass.ds(j + (w0 + JF * tap), 1)],
                                                       in1=cta[s][:, :], op0=ALU.mult, op1=ALU.add)\
                                    .then_inc(sem(f"mconv{s}"), 1)
                            dve.wait_ge(sem(f"tile_full{s}"), 2 * i + (2 * g0 + 2))
                            V.tensor_tensor(ur[s][:, :], acc[2 * s + 1][:, :], rstd[:, :], ALU.mult)\
                                .then_inc(sem(f"acc_free{s}"), 1)
                            dve.wait_ge(sem("msilu"), 2 * i + (2 * base + s + 1))
                            dve.wait_ge(sem(f"acc_free{s}"), 2 * i + (2 * g0 + 2))
                            V.tensor_tensor(pd[s][:, :], ur[s][:, :], sl[s][:, :], ALU.mult).then_inc(sem("prod"), 1)
                            dve.wait_ge(sem("a_head"), 2 * i + (2 * base + s + 1))
                            V.tensor_tensor(dyn(al, 2 * i + s), pd[s][:, :], dyn(ah, 2 * i + s).bitcast(F32),
                                            ALU.subtract).then_inc(sem("a_tail"), 1)
                            units_split_dve(dve, s, i + (g0 + 1))
                    g0 = UNIT[f"ff{layer}{n}"]

                    def x_tiles(i, g, split):
                        for s in (0, 1):
                            k = 2 * i + s
                            dve.wait_ge(sem(f"tile_full{s}"), 2 * g + 2)
                            V.tensor_tensor(dyn(x, k), dyn(x, k), acc[2 * s][:, :], ALU.add)\
                                .then_inc(sem(f"acc_free{s}"), 2)
                            if n == 1 and norm_after < 4:
                                x_tail(norm_after, k)
                            if split:
                                units_split_dve(dve, s, g + 1)

                    with dve.Fori(0, 3 if last and n == 1 else 4) as i:
                        x_tiles(i, i + g0, True)
                    if last and n == 1:
                        x_tiles(3, g0 + 3, False)

            with dve.Fori(0, NH - 1) as i:
                attention("diff", i, NH, 0, att_evac("diff", i + 1, i + (UNIT["diff"] + 1)))
            attention("diff", NH - 1, NH, 0, iter(()), more=False)
            out_proj(UNIT["out0"], 1)
            norm_rstd(1)
            mlp(0, 2, False)
            norm_rstd(2)
            for _ in att_evac("odd", 0, UNIT["odd"]):
                pass
            with dve.Fori(0, NPAIR - 1) as i:
                attention("odd", i, 0, NH, att_evac("odd", i + 1, i + (UNIT["odd"] + 1)))
            attention("odd", NPAIR - 1, 0, NH, iter(()))
            out_proj(UNIT["out1"], 3)
            norm_rstd(3)
            mlp(1, 4, True)
            norm_rstd(4)
            for k in range(KD):
                r = full(dve, "yt", f"x{k}", 0)
                if k >= 2:
                    dve.wait_ge(sem(f"out_done{k % 2}"), 16 * (k // 2))
                free(V.tensor_tensor(ob[k % 2][:, :, :], blk(r[:, :]), cols(rcol[:, :]), ALU.mult), "yt", f"x{k}", 0)


_INS = ["x", "even_norm_mix", "even_w_in", "even_dn_conv", "even_dn_A_log", "even_dn_dt_bias", "even_dn_norm",
        "even_diff_lambda", "even_diff_subln", "even_w_out", "odd_norm_mix", "odd_w_qkv", "odd_rel_bias",
        "odd_w_out", "ffn_norm", "ffn_w_in", "ffn_conv_w", "ffn_conv_b", "ffn_w_out", "final_norm"]


def kernel(**inputs):
    import numpy as _np
    import concourse.bacc as _bacc
    from concourse import mybir as _mybir
    from concourse.bass_utils import run_bass_kernel_spmd as _run

    nc = _bacc.Bacc("TRN2", target_bir_lowering=False, num_devices=1)
    arrays, aps = {}, {}
    given = {name: _np.ascontiguousarray(inputs[name]) for name in _INS}
    given["consts"] = constants()
    for name, a in given.items():
        arrays[f"in_{name}"] = a
        aps[name] = nc.dram_tensor(f"in_{name}", a.shape, _mybir.dt.from_np(a.dtype), kind="ExternalInput").ap()
    out = nc.dram_tensor("out_0", (S, D), _mybir.dt.float32, kind="ExternalOutput").ap()
    build(nc, aps, out)
    r = _run(nc, [arrays], core_ids=[0])
    return r.results[0]["out_0"].reshape(1, S, D)
```

```python
import math
from contextlib import ExitStack

import numpy as np

import concourse.bass as bass
from concourse import mybir

F32 = mybir.dt.float32
R32 = mybir.dt.float32r
ALU = mybir.AluOpType
ACT = mybir.ActivationFunctionType

P = 128
S = 512
NB = S // P
D = 1024
KD = D // P
FF = 2816
JF = FF // P
HALVES = ((0, 12), (12, 10))
NH = 4
HD = 64
NPAIR = 8
EPS = 1e-6
QSCALE = HD ** -0.5
LAM_INIT = 0.8 - 0.6 * math.exp(0.0)
NEG = -1e30
REL = 256
GLEN = 640
ALPHA = 4

C_Q, C_K, C_V, C_AB, C_GATE, C_FQ, C_FK, C_FV = 0, 512, 1024, 1536, 1544, 2056, 2568, 3080

PV_EVEN, PV_FFN, PV_ODD, PV_FIN, PV_DNC, PV_DNN, PV_SUB = 0, 8, 24, 32, 40, 88, 89
PV_CW = (P, 2 * P)
PV_CB = P + 66
PV_NORM = (PV_EVEN, PV_FFN, PV_ODD, PV_FFN + 8, PV_FIN)

C_ID, C_ONE, C_TRIU, C_STRICT, C_M16, C_M32, C_M64, C_M128, C_PERM = range(9)
C_COS, C_SIN, C_MASK = 9 * P, 9 * P + S, 9 * P + 2 * S
C_WIDTH = 9 * P + 3 * S


def constants():
    i = np.arange(P)
    row, col = i[:, None], i[None, :]
    c = np.zeros((P, C_WIDTH), np.float32)

    def put(n, m):
        c[:, n * P:(n + 1) * P] = m

    put(C_ID, row == col)
    put(C_ONE, 1.0)
    put(C_TRIU, row <= col)
    put(C_STRICT, col < row)
    put(C_M16, row // 16 == col // 16)
    for n, w in ((C_M32, 32), (C_M64, 64), (C_M128, 128)):
        put(n, (row // w == col // w) & (row // (w // 2) != col // (w // 2)))
    put(C_PERM, row == (col ^ 32))
    inv = np.float32(1.0) / np.power(np.float32(10000.0), np.arange(0, HD, 2, dtype=np.float32) / np.float32(HD))
    ang = np.arange(S, dtype=np.float32)[:, None] * inv[None, :].astype(np.float32)
    cos, sin = np.cos(ang).T, np.sin(ang).T
    c[:, C_COS:C_COS + S] = np.concatenate([cos] * 4)
    c[:, C_SIN:C_SIN + S] = np.concatenate([-sin, sin] * 2)
    c[:64, C_MASK + 448:C_MASK + 512] = NEG
    return c


_DN = [("sq_c", 0), ("grow", 1), ("gcol", 0), ("rk", 0), ("kk", 0), ("rq", 0), ("qk", 1), ("ktok", 0), ("vtok", 1),
       ("At", 0), ("A2", 1), ("A2t", 0), ("U1", 1), ("A4", 0), ("A4t", 1), ("U2", 0), ("A8", 1), ("U3", 0),
       ("T16", 1), ("Y16", 0), ("X16", 1), ("T32", 0), ("Y32", 1), ("X32", 0), ("T64", 1), ("Y64", 0), ("X64", 1),
       ("u", 0), ("wT", 1), ("o", 1), ("kv0", 0), ("ws1", 0), ("kv1", 0), ("ws2", 0), ("kv2", 0), ("ws3", 0),
       ("oc", 0), ("ro", 0)]
DN_JOBS = [(f"{n}{h}", h + 2 * b) for n, b in _DN for h in (0, 1)]
DIFF_JOBS = [(f"s{j}", j % 2) for j in range(8)] + [("vt", 2)] + [(f"t{b}", 2) for b in range(4)] + [("oc", 2), ("ro", 2), ("pv", 3)] \
    + [("rot_q", 0), ("rot_k", 1)]
ODD_JOBS = [(f"s{j}", j % 2) for j in range(8)] + [("vt", 2)] + [(f"t{j}", 2) for j in range(8)] + [("pv", 3)]
XT_JOBS = [(f"x{k}", k % 4) for k in range(KD)]
NORM_JOBS = [("col", 1), ("row", 0)]
AB_JOBS = [("abT", 2), ("ab", 3)]


class Bank:

    def __init__(self):
        self.base, self.at = {}, [0] * 4

    def phase(self, name, jobs, times, lead=()):
        for j in lead:
            self.at[dict(jobs)[j]] += 1
        self.base[name] = (list(self.at), jobs)
        for _, b in jobs:
            self.at[b] += times
        for j in lead:
            self.at[dict(jobs)[j]] -= 1

    def use(self, phase, job, i):
        base, jobs = self.base[phase]
        b = dict(jobs)[job]
        mine = [n for n, bank in jobs if bank == b]
        return b, base[b] + len(mine) * i + mine.index(job)


BANK = Bank()
BANK.phase("xt", XT_JOBS, 1)
BANK.phase("ab", AB_JOBS, 1)
BANK.phase("norm0", NORM_JOBS, 1)
BANK.phase("dn", DN_JOBS, NH // 2)
BANK.phase("diff", DIFF_JOBS, NH, lead=("rot_q", "rot_k"))
BANK.phase("norm1", NORM_JOBS, 1)
BANK.phase("norm2", NORM_JOBS, 1)
BANK.phase("odd", ODD_JOBS, NPAIR)
BANK.phase("norm3", NORM_JOBS, 1)
BANK.phase("norm4", NORM_JOBS[:1], 1)
BANK.phase("yt", XT_JOBS, 1)

_turns = [("dn", NH), ("diff", NH), ("out0", 2)]
for _l in (0, 1):
    if _l:
        _turns += [("odd", NPAIR), ("out1", 2)]
    for _n, (_, _c) in enumerate(HALVES):
        _turns += [(f"in{_l}{_n}", _c // 2), (f"ff{_l}{_n}", 4)]
UNIT = {}
_at = 0
for _name, _n in _turns:
    UNIT[_name] = _at
    _at += _n
UNITS = _at


def build(nc, T, out):
    ctx = ExitStack()
    with ctx:
        def sb(name, shape, dt=F32, where=ctx):
            return where.enter_context(nc.sbuf_tensor(name, shape, dt))

        sems = {}

        def sem(name):
            if name not in sems:
                sems[name] = ctx.enter_context(nc.semaphore(name))
            return sems[name]

        place = ExitStack()
        xs = sb("x_start", [P, KD, S], F32, place)
        place.close()
        rb = sb("rb", [16, 2 * REL + 1], F32, place)[:, :]
        fx = sb("fx", [16, GLEN], F32, place)[:, :]
        place.close()
        om = sb("om", [P, NH, S], F32, place)
        dx = {(n, h): sb(f"dn_{n}{h}", [P, S], F32, place)[:, :] for n in ("E32", "E64") for h in (0, 1)}
        place.close()
        x = sb("x", [P, KD, S])
        mh = sb("mh", [P, KD, S], R32)
        ml = sb("ml", [P, KD, S], R32)
        raw = [sb(f"raw{s}", [P, 2048]) for s in (0, 1)]
        wh = [sb(f"wh{s}", [P, 2048], R32) for s in (0, 1)]
        wl = [sb(f"wl{s}", [P, 2048], R32) for s in (0, 1)]
        cst = sb("cst", [P, C_WIDTH])
        pv = sb("pv", [P, 3 * P])
        rstd = sb("rstd", [P, S])
        rcol = sb("rcol", [P, NB])
        sdc = sb("sdc", [P, NB])
        ssum = sb("ssum", [P, S])
        sq = [sb(f"sq{s}", [P, S]) for s in (0, 1)]
        cb = [sb(f"cb{s}", [P, ALPHA + S]) for s in (0, 1)]
        cta = [sb(f"cta{s}", [P, S]) for s in (0, 1)]
        epsc = sb("epsc", [P, 1])

        gall = sb("gall", [P, NH, NB], F32, ctx)
        ball = sb("ball", [P, NH, NB], F32, ctx)
        lamc = sb("lamc", [P, 1], F32, ctx)
        abz = sb("abz", [P, NB, 8], F32, ctx)
        abt = [sb(f"abt{n}", [P, NB, NH], F32, ctx) for n in range(5)]
        dtb = sb("dtb", [P, NH], F32, ctx)
        alog = sb("alog", [P, NH], F32, ctx)
        lp = sb("lp", [P, 256], F32, ctx)
        lt = sb("lt", [P, 2, HD], F32, ctx)
        ls = sb("ls", [P, 4], F32, ctx)
        nq = sb("nq", [P, 2, NB], F32, ctx)
        sub8 = sb("sub8", [P, 1])

        def cblk(n):
            return cst[:, n * P:(n + 1) * P]

        ident, ones, triu = cblk(C_ID), cblk(C_ONE), cblk(C_TRIU)

        def rows(a):
            return a.unsqueeze(1).broadcast_to([P, NB, P])

        def cols(a):
            return a.unsqueeze(2).broadcast_to([P, NB, P])

        def blk(t):
            return t.rearrange("p (b n) -> p b n", b=NB)

        start = ExitStack()
        xin = sb("xin", [P, NB, D], F32, start)
        prow = sb("prow", [P, 3, P], F32, start)
        xsq = sb("xsq", [P, KD, S], F32, start)
        abw = sb("abw", [P, KD, 8], F32, start)
        abh = sb("abh", [P, KD, 8], R32, start)
        abl = sb("abl", [P, KD, 8], R32, start)
        abs_ = sb("abs", [8, S], F32, start)
        start.close()
        mix = ExitStack()
        own = ("gC", "sqq", "sqk", "qh", "kh", "decT", "decN", "qd", "qkD", "N", "A", "At", "A2", "A2t", "U")
        d = [{}, {}]
        for n in ("gC", "sqq", "sqk", "qh", "kh", "decT", "decN", "qd"):
            for h in (0, 1):
                d[h][n] = sb(f"dn_{n}{h}", [P, S], F32, mix)[:, :]
        for h, n in ((0, "qT"), (0, "kT"), (0, "vT"), (1, "qT"), (1, "kT"), (1, "vT"), (0, "gN"), (1, "gN")):
            d[h][n] = sb(f"dn_{n}{h}", [P, S], F32, mix)[:, :]
        for n in own[8:]:
            for h in (0, 1):
                d[h][n] = sb(f"dn_{n}{h}", [P, S], F32, mix)[:, :]
        gh, gc, eg, be, nr, vn, st = [], [], [], [], [], [], []
        for h in (0, 1):
            for n in ("E32", "E64"):
                d[h][n] = dx[n, h]
            for new, old in (("gbc", "decT"), ("kd", "kh"), ("kbg", "qh"), ("vb", "decN"), ("E128", "N"),
                             ("A4", "A"), ("A4t", "At"), ("A8", "A2"), ("T", "decT"), ("Y", "A2t"), ("wT", "E32"),
                             ("u", "E64"), ("sqo", "qd"), ("on", "A")):
                d[h][new] = d[h][old]
            gh.append(sb(f"gh{h}", [P, NB], F32, mix))
            gc.append(sb(f"gc{h}", [P, 3 * NB], F32, mix))
            eg.append(sb(f"eg{h}", [P, 3 * NB], F32, mix))
            be.append(sb(f"be{h}", [P, NB], F32, mix))
            nr.append(sb(f"nr{h}", [P, 6, NB], F32, mix))
            vn.append(sb(f"vn{h}", [P, P], F32, mix))
            st.append(sb(f"st{h}", [P, P], F32, mix))
        mix.close()
        mixer = ExitStack()
        oh = sb("oh", [P, KD, S], R32, mixer)
        ol = sb("ol", [P, KD, S], R32, mixer)
        att = ExitStack()
        qr0 = sb("qr0", [P, S], F32, att)
        qr1 = sb("qr1", [P, S], F32, att)
        vf = sb("vf", [P, S], F32, att)
        qc0 = sb("qc0", [P, S], F32, att)
        aq = sb("aq", [P, S], F32, att)
        ak = sb("ak", [P, S], F32, att)
        qc1 = sb("qc1", [P, S], F32, att)
        av = sb("av", [P, NB, P], F32, att)
        qr, qc = [qr0, qr1], [qc0, qc1]
        ns2 = sb("ns", [P, 2 * S], F32, att)
        pr2 = sb("pr", [P, 2 * S], F32, att)
        ns = [ns2[:, n * S:(n + 1) * S] for n in (0, 1)]
        pr = [pr2[:, n * S:(n + 1) * S] for n in (0, 1)]
        pn = [sb(f"pn{n}", [P, S], F32, att) for n in (0, 1)]
        pT = [sb(f"pT{n}", [P, S], F32, att) for n in (0, 1)]
        gb = [sb(f"gb{n}", [P, S], F32, att) for n in (0, 1)]
        osb = sb("osb", [P, S], F32, att)
        osd = sb("osd", [P, S], F32, att)
        nm = sb("nm", [P, 8], F32, att)
        rs = sb("rs", [P, 8], F32, att)
        rr = sb("rr", [P, 8], F32, att)
        att.close()
        mixer.close()
        mlp = ExitStack()
        ah = sb("ah", [P, 12, S], R32, mlp)
        al = sb("al", [P, 12, S], R32, mlp)
        sl = [sb(f"sl{s}", [P, S], F32, mlp) for s in (0, 1)]
        ur = [sb(f"ur{s}", [P, S], F32, mlp) for s in (0, 1)]
        pd = [sb(f"pd{s}", [P, S], F32, mlp) for s in (0, 1)]
        mlp.close()
        end = ExitStack()
        ob = [sb(f"ob{s}", [P, NB, P], F32, end) for s in (0, 1)]
        end.close()

        xscr = nc.dram_tensor("x_kept", (P, KD, S), F32).ap()
        gscr = nc.dram_tensor("rel_bias_extended", (16, P, GLEN), F32).ap()

        acc = [ctx.enter_context(nc.psum_tensor(f"acc{n}", [P, S], F32)) for n in range(4)]
        R = [ctx.enter_context(nc.psum_tensor(f"R{n}", [P, S], F32)) for n in range(4)]

        block = ctx.enter_context(nc.Block())

        def full(eng, phase, job, i):
            b, n = BANK.use(phase, job, i)
            eng.wait_ge(sem(f"R{b}_full"), n + 1)
            return R[b]

        def free(ins, phase, job, i):
            b, _ = BANK.use(phase, job, i)
            ins.then_inc(sem(f"R{b}_read"), 1)

        def read(eng, phase, job, i):
            b, n = BANK.use(phase, job, i)
            eng.wait_ge(sem(f"R{b}_read"), n + 1)

        def settled(eng, *waits):
            values = [v if isinstance(v, int) else eng.to_reg(v) for _, v in waits]
            eng.wait_ge(sem("cst_in"), 16)
            for (name, _), v in zip(waits, values):
                eng.wait_ge(sem(name), v)

        def is_full(phase, job, i):
            b, n = BANK.use(phase, job, i)
            return f"R{b}_full", n + 1

        def is_read(phase, job, i):
            b, n = BANK.use(phase, job, i)
            return f"R{b}_read", n + 1

        def dyn(t, k):
            return t[:, k, :] if isinstance(k, int) else t[:, bass.ds(k, 1), :].squeeze(1)

        def units_split_act(act, s, g):
            act.wait_ge(sem(f"raw_full{s}"), 32 * (g + 1))
            if not (isinstance(g, int) and g == 0):
                act.wait_ge(sem(f"tile_full{s}"), 2 * g)
            nc.scalar.activation(wh[s][:, :], raw[s][:, :], ACT.Copy).then_inc(sem(f"w_head{s}"), 1)

        def units_split_dve(dve, s, g):
            dve.wait_ge(sem(f"w_head{s}"), g + 1)
            nc.vector.tensor_tensor(wl[s][:, :], raw[s][:, :], wh[s][:, :].bitcast(F32),
                                    ALU.subtract).then_inc(sem(f"w_tail{s}"), 1)

        @block.sync
        def _(sp):
            def load(s, g, pieces):
                if not (isinstance(g, int) and g == 0):
                    sp.wait_ge(sem(f"w_tail{s}"), g)
                for dst, src in pieces:
                    sp.dma_start(dst, src).then_inc(sem(f"raw_full{s}"), 16)

            def pair(s, w, c0, c1):
                v = raw[s][:, :].rearrange("p (t k n) -> p t k n", t=2, k=KD)
                wv = w.rearrange("(k p) n -> p k n", p=P)
                return [(v[:, 0, :, :], wv[:, :, bass.ds(c0, P)]), (v[:, 1, :, :], wv[:, :, bass.ds(c1, P)])]

            def one(s, w, c0):
                v = raw[s][:, 0:KD * P].rearrange("p (k n) -> p k n", k=KD)
                wv = w.rearrange("(k p) n -> p k n", p=P)
                return [(v[:, 0:4, :], wv[:, 0:4, bass.ds(c0, P)]), (v[:, 4:8, :], wv[:, 4:8, bass.ds(c0, P)])]

            def down(s, w, j0, count, c0):
                v = raw[s][:, 0:count * P].rearrange("p (k n) -> p k n", k=count)
                wv = w[j0 * P:(j0 + count) * P, :].rearrange("(k p) n -> p k n", p=P)
                h = count // 2
                return [(v[:, 0:h, :], wv[:, 0:h, bass.ds(c0, P)]), (v[:, h:count, :], wv[:, h:count, bass.ds(c0, P)])]

            sp.dma_start(cst[:, 0:P], T["consts"][:, 0:P]).then_inc(sem("cst_in"), 16)
            xv = T["x"][0].rearrange("(b p) d -> p b d", p=P)
            for b in range(NB):
                sp.dma_start(xin[:, b, :], xv[:, b, :]).then_inc(sem("x_in"), 16)
            sp.dma_start(cst[:, P:], T["consts"][:, P:]).then_inc(sem("cst_rest"), 16)
            w0 = T["even_w_in"][0]
            load(0, 0, pair(0, w0, C_Q, C_K))
            load(1, 0, pair(1, w0, C_V, C_GATE))
            for k in range(4):
                read(sp, "xt", f"x{k + 4}", 0)
            sp.dma_start(xscr, xs[:, :, :]).then_inc(sem("x_kept"), 16)
            with sp.Fori(1, NH) as i:
                load(0, i, pair(0, w0, i * P + C_Q, i * P + C_K))
                load(1, i, pair(1, w0, i * P + C_V, i * P + C_GATE))
            with sp.Fori(0, NH) as i:
                load(0, i + UNIT["diff"], pair(0, w0, i * P + C_FQ, i * P + C_FK))
                load(1, i + UNIT["diff"], one(1, w0, i * P + C_FV))

            def out_proj(w, base):
                with sp.Fori(0, 2) as i:
                    for s in (0, 1):
                        load(s, i + base, pair(s, w, i * 512 + 256 * s, i * 512 + 256 * s + P))

            def mlp_loads(layer):
                wi, wo = T["ffn_w_in"][layer], T["ffn_w_out"][layer]
                for n, (j0, count) in enumerate(HALVES):
                    with sp.Fori(0, count // 2) as i:
                        for s in (0, 1):
                            c = i * 256 + (j0 + s) * P
                            load(s, i + UNIT[f"in{layer}{n}"], pair(s, wi, c, c + FF))
                    with sp.Fori(0, 4) as i:
                        for s in (0, 1):
                            load(s, i + UNIT[f"ff{layer}{n}"], down(s, wo, j0, count, i * 256 + s * P))

            out_proj(T["even_w_out"][0], UNIT["out0"])
            mlp_loads(0)
            wq = T["odd_w_qkv"][0]
            with sp.Fori(0, NPAIR) as i:
                load(0, i + UNIT["odd"], pair(0, wq, i * P, i * P + D))
                load(1, i + UNIT["odd"], one(1, wq, i * P + 2 * D))
            out_proj(T["odd_w_out"][0], UNIT["out1"])
            mlp_loads(1)
            ov = out.rearrange("(b p) (k n) -> p b k n", p=P, n=P)
            for k in range(KD):
                read(sp, "yt", f"x{k}", 0)
                sp.dma_start(ov[:, :, k, :], ob[k % 2][:, :, :]).then_inc(sem(f"out_done{k % 2}"), 16)
            for s in (0, 1):
                sp.wait_ge(sem(f"out_done{s}"), 16 * KD // 2)

        @block.gpsimd
        def _(pool):
            def pdma(dst, src):
                pool.dma_start(dst, src).then_inc(sem("p_in"), 16)

            def vec(src, r0, t):
                n = src.shape[0]
                pdma(prow[r0:r0 + n, t, :], src)

            v = "(k p) -> k p"
            vec(T["even_norm_mix"][0].rearrange(v, p=P), PV_EVEN, 0)
            for l in (0, 1):
                vec(T["ffn_norm"][l].rearrange(v, p=P), PV_FFN + 8 * l, 0)
            vec(T["odd_norm_mix"][0].rearrange(v, p=P), PV_ODD, 0)
            vec(T["final_norm"].rearrange(v, p=P), PV_FIN, 0)
            vec(T["even_dn_conv"][0].rearrange("t (k p) -> (t k) p", p=P), PV_DNC, 0)
            vec(T["even_dn_norm"], PV_DNN, 0)
            vec(T["even_diff_subln"], PV_SUB, 0)
            vec(T["ffn_conv_w"][0].rearrange("t (k p) -> (t k) p", p=P), 0, 1)
            vec(T["ffn_conv_b"].rearrange("l (k p) -> (l k) p", p=P), 66, 1)
            vec(T["ffn_conv_w"][1].rearrange("t (k p) -> (t k) p", p=P), 0, 2)
            pdma(dtb[:, :], T["even_dn_dt_bias"].broadcast_to([P, NH]))
            pdma(alog[:, :], T["even_dn_A_log"].broadcast_to([P, NH]))
            pdma(lp[:, :], T["even_diff_lambda"].rearrange("a b c -> a (b c)").broadcast_to([P, 256]))
            pdma(abw[:, :, :], T["even_w_in"][0].rearrange("(k p) n -> p k n", p=P)[:, :, C_AB:C_AB + 8])
            for s in (0, 1):
                pool.memset(cb[s][:, 0:ALPHA], 0.0).then_inc(sem("zeros"), 1)
            pool.memset(epsc[:, :], EPS).then_inc(sem("zeros"), 1)

            def sum_squares(norm):
                if norm:
                    read(pool, f"norm{norm - 1}", "col", 0)
                pool.memset(ssum[:, :], 0.0).then_inc(sem("ssum"), 1)
                if norm == 0:
                    for k in range(KD):
                        pool.wait_ge(sem("sq_full"), k + 1)
                        pool.wait_ge(sem("ssum"), k + 1)
                        pool.tensor_tensor(ssum[:, :], ssum[:, :], xsq[:, k, :], ALU.add).then_inc(sem("ssum"), 1)
                    return
                with pool.Fori(0, KD // 2) as i:
                    for s in (0, 1):
                        pool.wait_ge(sem("sq_full"), 2 * i + (KD * norm + s + 1))
                        pool.wait_ge(sem("ssum"), 2 * i + (9 * norm + s + 1))
                        pool.tensor_tensor(ssum[:, :], ssum[:, :], sq[s][:, :], ALU.add).then_inc(sem("ssum"), 1)

            sum_squares(0)

            pool.wait_ge(sem("x_kept"), 16)
            pool.wait_ge(sem("m_tail"), KD)
            pool.dma_start(rb, T["odd_rel_bias"][0]).then_inc(sem("rb_in"), 16)
            pool.wait_ge(sem("rb_in"), 16)
            pool.tensor_copy(fx[:, 255:GLEN - 1], rb[:, 0:384]).then_inc(sem("fx"), 1)
            pool.tensor_copy(fx[:, 0:255], rb[:, 0:1].broadcast_to([16, 255])).then_inc(sem("fx"), 1)
            pool.memset(fx[:, GLEN - 1:GLEN], 0.0).then_inc(sem("fx"), 1)
            pool.wait_ge(sem("fx"), 3)
            pool.dma_start(gscr, fx.unsqueeze(1).broadcast_to([16, P, GLEN])).then_inc(sem("fx_out"), 16)
            pool.wait_ge(sem("fx_out"), 16)

            for p in range(NH // 2):
                for h in (0, 1):
                    e = d[h]
                    pool.wait_ge(sem(f"gate_full{h}"), p + 1)
                    if p:
                        read(pool, "dn", "o1", p - 1)
                    pool.tensor_copy(e["gC"], e["gN"]).then_inc(sem(f"gC_full{h}"), 1)
                for h in (0, 1):
                    pool.wait_ge(sem(f"eT{h}"), p + 1)
                    pool.tensor_tensor(blk(d[h]["decT"]), blk(d[h]["decT"]), rows(triu), ALU.mult)\
                        .then_inc(sem(f"decT{h}"), 1)
                    pool.wait_ge(sem(f"eN{h}"), p + 1)
                    pool.tensor_tensor(blk(d[h]["decN"]), blk(d[h]["decN"]), rows(cblk(C_STRICT)), ALU.mult)\
                        .then_inc(sem(f"decN{h}"), 1)
                for h in (0, 1):
                    e = d[h]
                    pool.wait_ge(sem(f"N{h}"), p + 1)
                    pool.tensor_tensor(blk(e["A"]), blk(e["N"]), rows(cblk(C_M16)), ALU.mult).then_inc(sem(f"A_E{h}"), 1)
                for h in (0, 1):
                    e = d[h]
                    read(pool, "dn", f"rq{h}", p)
                    read(pool, "dn", f"grow{h}", p)
                    pool.tensor_tensor(e["qd"], e["qd"], e["qh"], ALU.mult).then_inc(sem(f"qd{h}"), 1)
                for h in (0, 1):
                    e = d[h]
                    for n, m in (("E32", C_M32), ("E64", C_M64), ("E128", C_M128)):
                        if n == "E128":
                            pool.wait_ge(sem(f"A_E{h}"), 4 * p + 3)
                        pool.tensor_tensor(blk(e[n]), blk(e["N"]), rows(cblk(m)), ALU.mult)\
                            .then_inc(sem(f"A_E{h}"), 1)

            pool.wait_ge(sem("A_E1"), 4 * (NH // 2))
            with pool.Fori(0, NH) as i:
                for n in (0, 1):
                    pool.wait_ge(sem("acc_free0"), 2 * i + (2 * UNIT["diff"] + n + 1))
                    pool.tensor_tensor(qc[n][:, :], qr[n][:, :], cst[:, C_COS:C_COS + S], ALU.mult)\
                        .then_inc(sem("qc_full"), 1)

            pool.wait_ge(sem("oc_tail"), NH)
            for k in range(0, KD, 2):
                pool.dma_start(x[:, k:k + 2, :], xscr[:, k:k + 2, :]).then_inc(sem("x_back"), 16)

            sum_squares(1)
            sum_squares(2)

            def load_bias(m, head):
                row = gscr[bass.ds(head, 1), :, :]
                for p0, p1, n in ((0, 64, 448), (64, P, S)):
                    src = bass.AP(tensor=row.tensor, offset=row.offset + (127 + p0 * (GLEN - 1)),
                                  ap=[[GLEN - 1, p1 - p0], [1, n]])
                    pool.dma_start(gb[m][p0:p1, 0:n], src).then_inc(sem(f"gb_full{m}"), 16)

            for m in (0, 1):
                pool.memset(gb[m][0:64, 448:S], NEG).then_inc(sem("gb_mask"), 1)
                load_bias(m, m)
            with pool.Fori(1, NPAIR) as i:
                for m in (0, 1):
                    read(pool, "odd", f"s{4 * m + 3}", i - 1)
                    load_bias(m, 2 * i + m)
            sum_squares(3)
            sum_squares(4)

        @block.tensor
        def _(pe):
            def job(phase, name, i, first=True):
                b, n = BANK.use(phase, name, i)
                if not (isinstance(n, int) and n == 0):
                    pe.wait_ge(sem(f"R{b}_read"), n)
                return R[b]

            def done(ins, phase, name, i):
                b, _ = BANK.use(phase, name, i)
                ins.then_inc(sem(f"R{b}_full"), 1)

            def mm3(o, ah_, al_, bh_, bl_, first, last):
                nc.tensor.matmul(o, ah_, bh_, start=first, stop=False)
                nc.tensor.matmul(o, ah_, bl_, start=False, stop=False)
                return nc.tensor.matmul(o, al_, bh_, start=False, stop=last)

            def begin(s, g):
                pe.wait_ge(sem(f"w_tail{s}"), g + 1)
                if not (isinstance(g, int) and g == 0):
                    pe.wait_ge(sem(f"acc_free{s}"), 2 * g)

            def features(s, g, mov, tiles=2, kn=KD, norm=None, srcwait=None):
                begin(s, g)
                ws = [w[s][:, 0:tiles * kn * P].rearrange("p (t k n) -> p t k n", t=tiles, k=kn) for w in (wh, wl)]
                for t in range(tiles):
                    for k in range(kn):
                        if norm is not None and s == 0 and t == 0:
                            pe.wait_ge(sem("m_tail"), KD * norm + k + 1)
                        if srcwait is not None and t == 0:
                            srcwait(k)
                        last = mm3(acc[2 * s + t][:, :], ws[0][:, t, k, :], ws[1][:, t, k, :],
                                   mov[0][:, k, :], mov[1][:, k, :], k == 0, k == kn - 1)
                        if k == kn - 1:
                            last.then_inc(sem(f"tile_full{s}"), 3 - tiles)
                        yield

            def both(a, b):
                yield from a
                yield from b

            def run(gen, n=1000):
                for _ in range(n):
                    if next(gen, 0) == 0:
                        return

            def token_sums(r, c0, squares):
                for b in range(NB):
                    last = nc.tensor.matmul(r[:, c0 + b:c0 + b + 1], squares[:, b * P:(b + 1) * P], ones[:, 0:1],
                                            start=True, stop=True)
                return last

            def norm_sums(n):
                pe.wait_ge(sem("ssum"), 9 * n + 9)
                r = job(f"norm{n}", "col", 0)
                done(token_sums(r, 0, ssum), f"norm{n}", "col", 0)

            def norm_rows(n):
                pe.wait_ge(sem("diag"), n + 1)
                r = job(f"norm{n}", "row", 0)
                done(nc.tensor.matmul(r[:, :], ones, sq[0][:, :], start=True, stop=True), f"norm{n}", "row", 0)

            pe.wait_ge(sem("cst_in"), 16)
            pe.wait_ge(sem("x_in"), 64)
            for k in range(KD):
                r = job("xt", f"x{k}", 0)
                for b in range(NB):
                    last = nc.tensor.transpose(r[:, b * P:(b + 1) * P], xin[:, b, k * P:(k + 1) * P], ident)
                done(last, "xt", f"x{k}", 0)
            pe.wait_ge(sem("p_in"), 16 * 15)
            for t, n in ((0, 90), (1, 110), (2, 66)):
                last = nc.tensor.transpose(acc[0][:, t * P:t * P + n], prow[0:n, t, :], cst[0:n, 0:n])
            last.then_inc(sem("pv_full"), 1)
            pe.wait_ge(sem("cst_rest"), 16)

            pe.wait_ge(sem("ab_split"), 1)
            r = job("ab", "abT", 0)
            for k in range(KD):
                pe.wait_ge(sem("m_tail"), k + 1)
                last = mm3(r[0:8, :], abh[:, k, :], abl[:, k, :], mh[:, k, :], ml[:, k, :], k == 0, k == KD - 1)
            done(last, "ab", "abT", 0)

            def ab_tokens():
                read(pe, "ab", "abT", 0)
                r = job("ab", "ab", 0)
                for b in range(NB):
                    last = nc.tensor.transpose(r[:, b * 8:b * 8 + 8], abs_[:, b * P:(b + 1) * P], cst[0:8, 0:8])
                done(last, "ab", "ab", 0)

            def dn_units(g):
                return both(features(0, g, (mh, ml)), features(1, g, (mh, ml)))

            def dn_pair(p, fill):
                def each(name, h, a, b, tr=False):
                    r = job("dn", f"{name}{h}", p)
                    for n in range(NB):
                        t = slice(n * P, (n + 1) * P)
                        lhs = a if a is ones else a[:, t]
                        if tr:
                            last = nc.tensor.transpose(r[:, t], lhs, ident)
                        else:
                            last = nc.tensor.matmul(r[:, t], lhs, triu if b is triu else b[:, t], start=True, stop=True)
                    done(last, "dn", f"{name}{h}", p)
                    run(fill, 1)

                def step(name, a, b, reads=(), need=()):
                    for h in (0, 1):
                        for s_, v_ in need:
                            pe.wait_ge(sem(f"{s_}{h}"), v_)
                        for n in reads:
                            read(pe, "dn", f"{n}{h}", p)
                        e = d[h]
                        each(name, h, e[a] if a else ones, triu if b == "triu" else e[b] if b else None, tr=b is None)

                def spread(name, src, need):
                    for h in (0, 1):
                        pe.wait_ge(sem(f"{need}{h}"), p + 1)
                        r = job("dn", f"{name}{h}", p)
                        done(nc.tensor.matmul(r[:, :], ones, d[h][src], start=True, stop=True), "dn", f"{name}{h}", p)
                        run(fill, 1)

                for h in (0, 1):
                    pe.wait_ge(sem(f"sqk{h}"), p + 1)
                    r = job("dn", f"sq_c{h}", p)
                    token_sums(r, 0, d[h]["sqq"])
                    done(token_sums(r, NB, d[h]["sqk"]), "dn", f"sq_c{h}", p)
                for h in (0, 1):
                    pe.wait_ge(sem(f"gbc{h}"), p + 1)
                    each("grow", h, d[h]["gbc"], triu)
                    r = job("dn", f"gcol{h}", p)
                    nc.tensor.matmul(r[:, 0:NB], triu, gh[h][:, :], start=True, stop=True)
                    done(nc.tensor.matmul(r[:, NB:2 * NB], ones, gh[h][:, :], start=True, stop=True), "dn", f"gcol{h}", p)
                    run(fill, 1)
                spread("rk", "sqk", "dk")
                step("kk", "kh", "kh", ["rk"])
                spread("rq", "sqq", "dq")
                step("qk", "kh", "qh", ["rq"])
                step("ktok", "kh", None)
                step("vtok", "vT", None)
                step("At", "A", None, need=[("A_E", 4 * p + 1)])
                step("A2", "At", "A", ["At"])
                step("A2t", "A", "At")
                step("U1", "A2", "U", ["A2"], [("U0", p + 1)])
                step("A4", "A2t", "A2", ["A2t"])
                step("A4t", "A2", "A2t")
                step("U2", "A4", "U", ["U1", "A4"])
                step("A8", "A4t", "A4", ["A4t"])
                step("U3", "A8", "U", ["U2", "A8"])
                last = "U3"
                for w, e in (("16", "E32"), ("32", "E64"), ("64", "E128")):
                    step("T" + w, "U", None, [last], [("A_E", 4 * p + 4)] if w == "16" else [])
                    step("Y" + w, e, "U")
                    step("X" + w, "T", "Y", ["T" + w, "Y" + w])
                    last = "X" + w
                step("u", "U", "vb", [last, "vtok"])
                step("wT", "kbg", "U", ["ktok"])
                o = []
                for b in range(NB):
                    t = slice(b * P, (b + 1) * P)
                    for h in (0, 1) if b else ():
                        e = d[h]
                        read(pe, "dn", f"kv{b - 1}{h}", p)
                        if b == 1:
                            read(pe, "dn", f"wT{h}", p)
                        r = job("dn", f"ws{b}{h}", p)
                        done(nc.tensor.matmul(r[:, 0:P], e["wT"][:, t], st[h][:, :], start=True, stop=True),
                             "dn", f"ws{b}{h}", p)
                        nc.tensor.matmul(o[h][:, t], st[h][:, :], e["qd"][:, t], start=True, stop=False)
                        run(fill, 1)
                    for h in (0, 1):
                        e = d[h]
                        if b:
                            read(pe, "dn", f"ws{b}{h}", p)
                        else:
                            pe.wait_ge(sem(f"vn{h}"), p + 1)
                        if b < NB - 1:
                            r = job("dn", f"kv{b}{h}", p)
                            done(nc.tensor.matmul(r[:, 0:P], e["kd"][:, t], vn[h][:, :], start=True, stop=True),
                                 "dn", f"kv{b}{h}", p)
                        if b == 0:
                            o.append(job("dn", f"o{h}", p))
                            pe.wait_ge(sem(f"qd{h}"), p + 1)
                            read(pe, "dn", f"qk{h}", p)
                        last = nc.tensor.matmul(o[h][:, t], vn[h][:, :], e["qkD"][:, t], start=(b == 0), stop=True)
                        if b == NB - 1:
                            done(last, "dn", f"o{h}", p)
                        else:
                            last.then_inc(sem(f"o_step{h}"), 1)
                        run(fill, 1)
                run(fill)
                for h in (0, 1):
                    pe.wait_ge(sem(f"sqo_dn{h}"), p + 1)
                    r = job("dn", f"oc{h}", p)
                    done(token_sums(r, 0, d[h]["sqo"]), "dn", f"oc{h}", p)
                spread("ro", "sqo", "do")

            def rope_products(i):
                for n, nm_ in enumerate(("rot_q", "rot_k")):
                    pe.wait_ge(sem("acc_free0"), 2 * i + (2 * UNIT["diff"] + n + 3))
                    r = job("diff", nm_, i)
                    done(nc.tensor.matmul(r[:, :], cblk(C_PERM), qr[n][:, :], start=True, stop=True),
                         "diff", nm_, i)

            def attention(ph, i, fill, more=True):
                diff = ph == "diff"
                items = [(m, b) for b in range(NB) for m in (0, 1)] if diff else \
                    [(m, b) for m in (0, 1) for b in range(NB)]
                trs = [b for b in range(NB)] if diff else list(range(8))
                if diff:
                    pe.wait_ge(sem("roped"), 2 * i + 2)
                else:
                    pe.wait_ge(sem("acc_free0"), 2 * i + (2 * UNIT[ph] + 2))
                o = None
                per = 4 if diff else 8
                for t in range(8 + 4):
                    if t < 8:
                        m, b = items[t]
                        r = job(ph, f"s{t}", i)
                        rw = slice(HD * m, HD * m + HD)
                        done(nc.tensor.matmul(r[:, 0:(b + 1) * P], aq[rw, b * P:(b + 1) * P], ak[rw, 0:(b + 1) * P],
                                              start=True, stop=True), ph, f"s{t}", i)
                    if t == 1:
                        pe.wait_ge(sem("acc_free1"), 2 * i + (2 * UNIT[ph] + 2))
                        r = job(ph, "vt", i)
                        for b in range(NB):
                            last = nc.tensor.transpose(r[:, b * P:(b + 1) * P], vf[:, b * P:(b + 1) * P], ident)
                        done(last, ph, "vt", i)
                    run(fill, 2 if t < 8 else 1)
                    z = (t - 3) // 2 if diff and (t - 3) % 2 == 0 else t - 2 if not diff else -1
                    if 0 <= z < per:
                        b = z if diff else items[z][1]
                        pe.wait_ge(sem("pn_" + ph), per * i + z + 1)
                        r = job(ph, f"t{z}", i)
                        for k in range(b + 1):
                            last = nc.tensor.transpose(r[:, k * P:(k + 1) * P], pn[z % 2][:, k * P:(k + 1) * P], ident)
                        done(last, ph, f"t{z}", i)
                    y = (t - 4) // 2 if diff and (t - 4) % 2 == 0 else t - 3 if not diff else -1
                    if 0 <= y < per:
                        b = y if diff else items[y][1]
                        if o is None:
                            o = job(ph, "pv", i)
                        read(pe, ph, f"t{y}", i)
                        if diff:
                            dst, vc = o[:, b * P:(b + 1) * P], slice(0, P)
                        else:
                            m = items[y][0]
                            dst, vc = o[HD * m:HD * m + HD, b * P:(b + 1) * P], slice(HD * m, HD * m + HD)
                        for k in range(b + 1):
                            last = nc.tensor.matmul(dst, av[:, k, vc], pT[y % 2][:, k * P:(k + 1) * P],
                                                    start=(k == 0), stop=(k == b))
                        if y == per - 1:
                            done(last, ph, "pv", i)
                        else:
                            last.then_inc(sem("pv_" + ph), 1)
                    if t == 9 and diff and more:
                        rope_products(i)
                run(fill)
                if diff:
                    pe.wait_ge(sem("sqo_diff"), i + 1)
                    r = job(ph, "oc", i)
                    done(token_sums(r, 0, osd), ph, "oc", i)
                    pe.wait_ge(sem("do_diff"), i + 1)
                    r = job(ph, "ro", i)
                    done(nc.tensor.matmul(r[:, :], ones, osd[:, :], start=True, stop=True), ph, "ro", i)

            def attn_units(g):
                return both(features(0, g, (mh, ml)), features(1, g, (mh, ml), tiles=1))

            def out_terms(base, heads, last, srcwait):
                for s in (0, 1):
                    begin(s, base)
                    ws = [w[s][:, :].rearrange("p (t k n) -> p t k n", t=2, k=KD) for w in (wh, wl)]
                    for t in (0, 1) if s == 0 else (0,):
                        for k in heads:
                            if (s, t) == (0, 0):
                                srcwait(k)
                            ins = mm3(acc[2 * s + t][:, :], ws[0][:, t, k, :], ws[1][:, t, k, :],
                                      oh[:, k, :], ol[:, k, :], k == 0, k == last)
                            if k == last:
                                ins.then_inc(sem(f"tile_full{s}"), 1)
                            yield

            def out_rest(base, last, srcwait):
                srcwait(last)
                for s, t in ((0, 0), (0, 1), (1, 0)):
                    ws = [w[s][:, :].rearrange("p (t k n) -> p t k n", t=2, k=KD) for w in (wh, wl)]
                    mm3(acc[2 * s + t][:, :], ws[0][:, t, last, :], ws[1][:, t, last, :],
                        oh[:, last, :], ol[:, last, :], False, True).then_inc(sem(f"tile_full{s}"), 1)
                for k in range(KD):
                    ins = mm3(acc[3][:, :], ws[0][:, 1, k, :], ws[1][:, 1, k, :], oh[:, k, :], ol[:, k, :],
                              k == 0, k == KD - 1)
                ins.then_inc(sem("tile_full1"), 1)
                for s in (0, 1):
                    run(features(s, base + 1, (oh, ol)))

            def mlp_layer(layer, norm):
                for n, (j0, count) in enumerate(HALVES):
                    g0 = UNIT[f"in{layer}{n}"]
                    if n == 0:
                        first = features(0, g0, (mh, ml), norm=norm)
                        run(first, KD)
                        norm_sums(norm)
                        run(first, 4)
                        norm_rows(norm)
                        run(first)
                        run(features(1, g0, (mh, ml)))
                    with pe.Fori(1 if n == 0 else 0, count // 2) as i:
                        for s in (0, 1):
                            run(features(s, i + g0, (mh, ml)))
                    g0 = UNIT[f"ff{layer}{n}"]
                    before = 12 * n + JF * layer

                    def products(g, src=None):
                        for s in (0, 1):
                            run(features(s, g, (ah, al), tiles=1, kn=count, srcwait=src))

                    products(g0, lambda k: pe.wait_ge(sem("a_tail"), before + k + 1))
                    with pe.Fori(1, 4) as i:
                        products(i + g0)

            first = dn_units(0)
            run(first, KD)
            ab_tokens()
            norm_sums(0)
            run(first, 4)
            norm_rows(0)
            run(both(first, dn_units(1)))
            dn_pair(0, both(dn_units(2), dn_units(3)))
            dn_pair(1, attn_units(UNIT["diff"]))
            rope_products(-1)
            with pe.Fori(0, NH - 1) as i:
                attention("diff", i, attn_units(i + (UNIT["diff"] + 1)))

            def heads_wait(k):
                pe.wait_ge(sem("oc_tail" if k < NH else "o_tail"), k % NH + 1)

            attention("diff", NH - 1, out_terms(UNIT["out0"], (0, 1, 2, 4, 5, 6, 3), KD - 1, heads_wait), more=False)
            out_rest(UNIT["out0"], KD - 1, heads_wait)
            mlp_layer(0, 1)
            first = both(features(0, UNIT["odd"], (mh, ml), norm=2), features(1, UNIT["odd"], (mh, ml), tiles=1))
            run(first, KD)
            norm_sums(2)
            run(first, 4)
            norm_rows(2)
            run(first)
            with pe.Fori(0, NPAIR - 1) as i:
                attention("odd", i, attn_units(i + (UNIT["odd"] + 1)))


            def pairs_wait(k):
                read(pe, "odd", "pv", k)

            attention("odd", NPAIR - 1, out_terms(UNIT["out1"], range(KD - 1), KD - 1, pairs_wait))
            out_rest(UNIT["out1"], KD - 1, pairs_wait)
            mlp_layer(1, 3)
            norm_sums(4)
            for k in range(KD):
                r = job("yt", f"x{k}", 0)
                pe.wait_ge(sem("x_gain"), k + 1)
                for b in range(NB):
                    last = nc.tensor.transpose(r[:, b * P:(b + 1) * P], x[:, k, b * P:(b + 1) * P], ident)
                done(last, "yt", f"x{k}", 0)

        @block.scalar
        def _(act):
            A = nc.scalar.activation

            def x_tile(norm, k, s):
                g = pv[:, bass.ds(k + PV_NORM[norm], 1)]
                if norm < 4:
                    A(dyn(mh, k), dyn(x, k), ACT.Copy, scale=g).then_inc(sem("m_head"), 1)
                settled(act, ("ssum", k + max(9 * norm, 1)))
                A(sq[s][:, :], dyn(x, k), ACT.Square).then_inc(sem("sq_full"), 1)
                if norm == 4:
                    settled(act, ("sq_full", k + (KD * norm + 1)))
                    A(dyn(x, k), dyn(x, k), ACT.Copy, scale=g).then_inc(sem("x_gain"), 1)

            def norm_roots(n):
                if n:
                    act.wait_ge(sem("rstd"), n)
                r = full(act, f"norm{n}", "col", 0)
                free(A(sdc[:, :], r[:, 0:NB], ACT.Sqrt, bias=epsc[:, :], scale=1.0 / D), f"norm{n}", "col", 0)

            for k in range(KD):
                r = full(act, "xt", f"x{k}", 0)
                free(A(xs[:, k, :], r[:, :], ACT.Copy), "xt", f"x{k}", 0)
            for k in range(KD):
                read(act, "xt", f"x{k}", 0)
                A(xsq[:, k, :], xs[:, k, :], ACT.Square).then_inc(sem("sq_full"), 1)
            act.wait_ge(sem("zeros"), 3)
            act.wait_ge(sem("pv_copied"), 1)
            act.wait_ge(sem("p_in"), 16 * 15)
            A(abh[:, :, :], abw[:, :, :], ACT.Copy).then_inc(sem("ab_head"), 1)
            for k in range(KD):
                read(act, "xt", f"x{k}", 0)
                A(mh[:, k, :], xs[:, k, :], ACT.Copy, scale=pv[:, k:k + 1]).then_inc(sem("m_head"), 1)
            for s in (0, 1):
                units_split_act(act, s, 0)
            norm_roots(0)

            def silu(i, c, dst):
                act.wait_ge(sem("conv"), 12 * i + (4 * c + 4))
                A(dst, cta[(3 * i + c) % 2][:, :], ACT.Silu).then_inc(sem("silu"), 1)

            def dn_evac(i, g):
                h, p = i % 2, i // 2
                e = d[h]
                yield silu(i, 0, e["qT"])
                silu(i, 1, e["kT"])
                act.wait_ge(sem("silu"), 3 * i + 2)
                if p:
                    full(act, "dn", f"rq{h}", p - 1)
                for n, src in (("sqq", "qT"), ("sqk", "kT")):
                    A(e[n], e[src], ACT.Square).then_inc(sem(f"{n}{h}"), 1)
                yield
                yield units_split_act(act, 0, g + 1)
                yield silu(i, 2, e["vT"])
                act.wait_ge(sem("acc_free1"), 2 * g + 2)
                A(e["gN"], e["gN"], ACT.Silu).then_inc(sem(f"gate_full{h}"), 1)
                yield
                yield units_split_act(act, 1, g + 1)

            def feat_evac(ph, g):
                yield
                yield units_split_act(act, 0, g + 1)
                yield
                yield units_split_act(act, 1, g + 1)

            def each4(gen):
                for _ in range(4):
                    next(gen, 0)

            def chained(*gens):
                for g in gens:
                    yield from g

            def copy_out(name, dst, p):
                for h in (0, 1):
                    r = full(act, "dn", f"{name}{h}", p)
                    free(A(d[h][dst], r[:, :], ACT.Copy), "dn", f"{name}{h}", p)

            def dn_pair(p, evac):
                for h in (0, 1):
                    r = full(act, "dn", f"sq_c{h}", p)
                    free(A(nr[h][:, 0:2, :], r[:, 0:2 * NB].rearrange("p (a b) -> p a b", a=2), ACT.Sqrt,
                           bias=epsc[:, :]), "dn", f"sq_c{h}", p)
                for h in (0, 1):
                    e = d[h]
                    act.wait_ge(sem(f"gc{h}"), p + 1)
                    A(eg[h][:, :], gc[h][:, :], ACT.Exp).then_inc(sem(f"eg{h}"), 1)
                    r = full(act, "dn", f"grow{h}", p)
                    act.wait_ge(sem(f"dm{h}"), p + 1)
                    free(A(e["qd"], r[:, :], ACT.Exp), "dn", f"grow{h}", p)
                    A(e["decN"], e["decN"], ACT.Exp, scale=-1.0).then_inc(sem(f"eN{h}"), 1)
                    A(e["decT"], e["decT"], ACT.Exp).then_inc(sem(f"eT{h}"), 1)
                copy_out("At", "At", p)
                copy_out("A2", "A2", p)
                next(evac, 0)
                copy_out("A4", "A4", p)
                next(evac, 0)
                next(evac, 0)
                copy_out("A8", "A8", p)
                copy_out("T16", "T", p)
                next(evac, 0)
                copy_out("T32", "T", p)
                next(evac, 0)
                next(evac, 0)
                copy_out("T64", "T", p)
                for _ in range(3):
                    next(evac, 0)
                copy_out("wT", "wT", p)
                next(evac, 0)
                for h in (0, 1):
                    r = full(act, "dn", f"o{h}", p)
                    A(d[h]["sqo"], r[:, :], ACT.Square).then_inc(sem(f"sqo_dn{h}"), 1)
                for h in (0, 1):
                    r = full(act, "dn", f"oc{h}", p)
                    free(A(nr[h][:, 4, :], r[:, 0:NB], ACT.Sqrt, bias=epsc[:, :], scale=1.0 / P), "dn", f"oc{h}", p)
                next(evac, 0)
                next(evac, 0)

            for _ in dn_evac(0, 0):
                pass

            act.wait_ge(sem("ab_in"), 1)
            A(abt[1][:, :, :], abt[1][:, :, :], ACT.Exp, scale=-1.0).then_inc(sem("ab_e"), 1)
            A(abt[2][:, :, :], abz[:, :, 4:8], ACT.Exp, scale=-1.0).then_inc(sem("ab_e"), 1)
            A(alog[:, :], alog[:, :], ACT.Exp).then_inc(sem("ab_e"), 1)
            A(ls[:, 0:2], ls[:, 0:2], ACT.Exp).then_inc(sem("ab_e"), 1)
            act.wait_ge(sem("ab_e"), 4)
            A(abt[1][:, :, :], abt[1][:, :, :], ACT.Ln, bias=1.0).then_inc(sem("ab_e"), 1)

            for _ in dn_evac(1, 1):
                pass
            dn_pair(0, chained(dn_evac(2, 2), dn_evac(3, 3)))
            dn_pair(1, feat_evac("diff", UNIT["diff"]))

            def attention(ph, i, o0, evac):
                diff = ph == "diff"
                items = [(m, b) for b in range(NB) for m in (0, 1)] if diff else \
                    [(m, b) for m in (0, 1) for b in range(NB)]
                per = 4 if diff else 8
                for t in range(8 + 4):
                    if t < 8:
                        w = (items[t][1] + 1) * P
                        read(act, ph, f"s{t}", i)
                        if t >= 2 and diff:
                            act.wait_ge(sem("pn_diff"), 4 * i + t // 2)
                        elif t >= 2:
                            act.wait_ge(sem("pn_odd"), 8 * i + (t - 1))
                        A(pr[t % 2][:, 0:w], ns[t % 2][:, 0:w], ACT.Exp, bias=nm[:, t:t + 1], scale=-1.0,
                          accum_out=rs[:, t:t + 1]).then_inc(sem("exp_" + ph), 1)
                    if t == 1:
                        r = full(act, ph, "vt", i)
                        free(A(av[:, :, :], blk(r[:, :]), ACT.Copy), ph, "vt", i)
                    z = (t - 3) // 2 if diff and (t - 3) % 2 == 0 else t - 2 if not diff else -1
                    if 0 <= z < per:
                        b = z if diff else items[z][1]
                        pv_wait(ph, i, z, per)
                        r = full(act, ph, f"t{z}", i)
                        free(A(pT[z % 2][:, 0:(b + 1) * P], r[:, 0:(b + 1) * P], ACT.Copy), ph, f"t{z}", i)
                    if t == 0 and diff:
                        read(act, "dn", "o1", 1)
                        A(dyn(oh, i), dyn(om, i), ACT.Copy).then_inc(sem("oc_head"), 1)
                    if t == 8:
                        next(evac, 0)
                        next(evac, 0)
                if diff:
                    r = full(act, ph, "pv", i)
                    A(osd[:, :], r[:, :], ACT.Square).then_inc(sem("sqo_diff"), 1)
                    r = full(act, ph, "oc", i)
                    free(A(nq[:, 0, :], r[:, 0:NB], ACT.Sqrt, bias=epsc[:, :], scale=1.0 / P), ph, "oc", i)
                    next(evac, 0)
                    next(evac, 0)
                    settled(act, is_full(ph, "ro", i))
                    free(A(osd[:, :], R[2][:, :], ACT.Copy, scale=sub8[:, :]), ph, "ro", i)
                    settled(act, is_read(ph, "pv", i))
                    A(dyn(oh, i + o0), osb[:, :], ACT.Copy).then_inc(sem("o_head"), 1)
                else:
                    settled(act, is_full(ph, "pv", i))
                    A(dyn(oh, i + o0), R[3][:, :], ACT.Copy).then_inc(sem("o_head"), 1)
                next(evac, 0)
                next(evac, 0)

            def pv_wait(ph, i, z, per):
                if z >= 2:
                    act.wait_ge(sem("pv_" + ph), (per - 1) * i + z - 1)
                elif z == 1:
                    if not (isinstance(i, int) and i == 0):
                        b, n = BANK.use(ph, "pv", i)
                        act.wait_ge(sem(f"R{b}_full"), n)

            with act.Fori(0, NH - 1) as i:
                attention("diff", i, NH, feat_evac("diff", i + (UNIT["diff"] + 1)))
            attention("diff", NH - 1, NH, iter(()))

            def out_proj(base, norm):
                with act.Fori(0, 2) as i:
                    for s in (0, 1):
                        units_split_act(act, s, i + (base + 1))
                        for t in (0, 1):
                            settled(act, (f"acc_free{s}", 2 * i + (2 * base + t + 1)))
                            x_tile(norm, 4 * i + (2 * s + t), t)

            def mlp(layer, norm_after, last):
                for n, (j0, count) in enumerate(HALVES):
                    g0 = UNIT[f"in{layer}{n}"]
                    base = 11 * layer + 6 * n
                    with act.Fori(0, count // 2) as i:
                        for s in (0, 1):
                            j = 2 * i + (j0 + s)
                            settled(act, (f"acc_free{s}", 2 * i + (2 * g0 + 1)))
                            A(cta[s][:, :], cb[s][:, ALPHA - 2:ALPHA - 2 + S], ACT.Identity,
                              bias=pv[:, bass.ds(j + (PV_CB + JF * layer), 1)],
                              scale=pv[:, bass.ds(j + PV_CW[layer], 1)]).then_inc(sem("mtap"), 1)
                            act.wait_ge(sem(f"mconv{s}"), 2 * i + (2 * base + 2))
                            A(sl[s][:, :], cta[s][:, :], ACT.Silu).then_inc(sem("msilu"), 1)
                            settled(act, ("prod", 2 * i + (2 * base + s + 1)))
                            A(dyn(ah, 2 * i + s), pd[s][:, :], ACT.Copy).then_inc(sem("a_head"), 1)
                            units_split_act(act, s, i + (g0 + 1))
                    g0 = UNIT[f"ff{layer}{n}"]

                    def x_tiles(i, g, split):
                        for s in (0, 1):
                            if n == 1:
                                settled(act, (f"acc_free{s}", 2 * g + 2))
                                x_tile(norm_after, 2 * i + s, s)
                            if split:
                                units_split_act(act, s, g + 1)

                    with act.Fori(0, 3 if last and n == 1 else 4) as i:
                        x_tiles(i, i + g0, True)
                    if last and n == 1:
                        x_tiles(3, g0 + 3, False)

            out_proj(UNIT["out0"], 1)
            norm_roots(1)
            mlp(0, 2, False)
            norm_roots(2)
            each4(feat_evac("odd", UNIT["odd"]))
            with act.Fori(0, NPAIR - 1) as i:
                attention("odd", i, 0, feat_evac("odd", i + (UNIT["odd"] + 1)))
            attention("odd", NPAIR - 1, 0, iter(()))
            out_proj(UNIT["out1"], 3)
            norm_roots(3)
            mlp(1, 4, True)
            norm_roots(4)

        @block.vector
        def _(dve):
            V = nc.vector
            step = sem("dve_step")

            def norm_rstd(n):
                read(dve, f"norm{n}", "col", 0)
                V.reciprocal(rcol[:, :], sdc[:, :]).then_inc(sem("rstd"), 1)
                dve.wait_ge(sem("rstd"), n + 1)
                if n == 4:
                    return
                V.tensor_tensor(blk(sq[0][:, :]), rows(ident), cols(rcol[:, :]), ALU.mult).then_inc(sem("diag"), 1)
                r = full(dve, f"norm{n}", "row", 0)
                free(V.tensor_copy(rstd[:, :], r[:, :]), f"norm{n}", "row", 0)
                read(dve, f"norm{n}", "row", 0)

            def x_tail(norm, k):
                dve.wait_ge(sem("m_head"), k + (KD * norm + 1))
                V.scalar_tensor_tensor(out=dyn(ml, k), in0=dyn(x if norm else xs, k), scalar=pv[:, bass.ds(k + PV_NORM[norm], 1)],
                                       in1=dyn(mh, k).bitcast(F32), op0=ALU.mult, op1=ALU.subtract)\
                    .then_inc(sem("m_tail"), 1)

            dve.wait_ge(sem("pv_full"), 1)
            for t, n in ((0, 90), (1, 110), (2, 66)):
                ins = V.tensor_copy(pv[:, t * P:t * P + n], acc[0][:, t * P:t * P + n])
            ins.then_inc(sem("pv_copied"), 1)
            dve.wait_ge(sem("pv_copied"), 1)
            dve.wait_ge(sem("ab_head"), 1)
            V.tensor_tensor(abl[:, :, :], abw[:, :, :], abh[:, :, :].bitcast(F32), ALU.subtract)\
                .then_inc(sem("ab_split"), 1)
            for k in range(KD):
                x_tail(0, k)
            units_split_dve(dve, 0, 0)
            r = full(dve, "ab", "abT", 0)
            free(V.tensor_copy(abs_[:, :], r[0:8, :]), "ab", "abT", 0)
            units_split_dve(dve, 1, 0)
            V.tensor_scalar(sub8[:, :], pv[:, PV_SUB:PV_SUB + 1], 1.0 - LAM_INIT, None, ALU.mult).then_inc(step, 1)
            norm_rstd(0)

            def conv(i, c, slot, g, tile):
                buf, to, n = cb[c % 2], cta[(3 * i + c) % 2], 12 * i + 4 * c
                dve.wait_ge(sem(f"tile_full{slot}"), g)
                if n:
                    dve.wait_ge(sem("conv"), n)
                V.tensor_tensor(buf[:, ALPHA:ALPHA + S], acc[c][:, :], rstd[:, :], ALU.mult)\
                    .then_inc(sem(f"acc_free{slot}"), 1)
                dve.wait_ge(sem(f"acc_free{slot}"), g)
                for tap in range(4):
                    w = pv[:, PV_DNC + 12 * tap + tile + i:PV_DNC + 12 * tap + tile + i + 1]
                    o = ALPHA - 3 + tap
                    if tap == 0:
                        if 3 * i + c >= 2:
                            dve.wait_ge(sem("silu"), 3 * i + c - 1)
                        ins = V.tensor_scalar(to[:, :], buf[:, o:o + S], w, None, ALU.mult)
                    else:
                        dve.wait_ge(sem("conv"), n + tap)
                        ins = V.scalar_tensor_tensor(out=to[:, :], in0=buf[:, o:o + S], scalar=w, in1=to[:, :],
                                                     op0=ALU.mult, op1=ALU.add)
                    ins.then_inc(sem("conv"), 1)

            def dn_evac(i, g):
                h, p = i % 2, i // 2
                yield conv(i, 0, 0, 2 * g + 1, 0)
                yield conv(i, 1, 0, 2 * g + 2, 4)
                yield units_split_dve(dve, 0, g + 1)
                yield conv(i, 2, 1, 2 * g + 1, 8)
                dve.wait_ge(sem("tile_full1"), 2 * g + 2)
                if p:
                    dve.wait_ge(sem(f"gC_full{h}"), p)
                V.tensor_tensor(d[h]["gN"], acc[3][:, :], rstd[:, :], ALU.mult).then_inc(sem("acc_free1"), 1)
                yield
                yield units_split_dve(dve, 1, g + 1)

            def att_evac(ph, i, g):
                diff = ph == "diff"
                prev = not (isinstance(i, int) and i == 0)
                dve.wait_ge(sem("tile_full0"), 2 * g + 1)
                if diff:
                    V.scalar_tensor_tensor(out=qr[0][:, :], in0=acc[0][:, :], scalar=QSCALE, in1=rstd[:, :],
                                           op0=ALU.mult, op1=ALU.mult).then_inc(sem("acc_free0"), 1)
                    dve.wait_ge(sem("tile_full0"), 2 * g + 2)
                    V.tensor_tensor(qr[1][:, :], acc[1][:, :], rstd[:, :], ALU.mult).then_inc(sem("acc_free0"), 1)
                else:
                    if prev:
                        full(dve, ph, "s7", i - 1)
                    V.scalar_tensor_tensor(out=aq[:, :], in0=acc[0][:, :], scalar=QSCALE, in1=rstd[:, :],
                                           op0=ALU.mult, op1=ALU.mult).then_inc(sem("acc_free0"), 1)
                    dve.wait_ge(sem("tile_full0"), 2 * g + 2)
                    V.tensor_tensor(ak[:, :], acc[1][:, :], rstd[:, :], ALU.mult).then_inc(sem("acc_free0"), 1)
                yield
                yield units_split_dve(dve, 0, g + 1)
                dve.wait_ge(sem("tile_full1"), 2 * g + 2)
                if prev:
                    full(dve, ph, "vt", i - 1)
                V.tensor_tensor(vf[:, :], acc[2][:, :], rstd[:, :], ALU.mult)\
                    .then_inc(sem("acc_free1"), 2)
                yield
                yield units_split_dve(dve, 1, g + 1)

            def rope(i):
                for n, (name, dst) in enumerate((("rot_q", aq), ("rot_k", ak))):
                    b, u = BANK.use("diff", name, i - 1)
                    dve.wait_ge(sem(f"R{b}_full"), u + 1)
                    V.tensor_tensor(dst[:, :], R[b][:, :], cst[:, C_SIN:C_SIN + S], ALU.mult)\
                        .then_inc(sem(f"R{b}_read"), 1)
                    dve.wait_ge(sem(f"R{b}_read"), u + 1)
                    dve.wait_ge(sem("qc_full"), 2 * i + n + 1)
                    V.tensor_tensor(dst[:, :], dst[:, :], qc[n][:, :], ALU.add).then_inc(sem("roped"), 1)

            def dn_pair(p, evac):
                def own(ins, name, n):
                    ins.then_inc(sem(name), 1)
                    dve.wait_ge(sem(name), n)

                def beta(h):
                    return ball[:, 2 * p + h, :]

                for h in (0, 1):
                    g_i = gall[:, 2 * p + h, :]
                    V.tensor_copy(gh[h][:, :], g_i)
                    V.tensor_copy(blk(d[h]["gbc"]), cols(g_i)).then_inc(sem(f"gbc{h}"), 1)
                for h in (0, 1):
                    e = d[h]
                    read(dve, "dn", f"sq_c{h}", p)
                    own(V.reciprocal(nr[h][:, 2:4, :], nr[h][:, 0:2, :]), f"inv{h}", p + 1)
                    V.tensor_tensor(blk(e["sqk"]), rows(ident), cols(nr[h][:, 3, :]), ALU.mult)\
                        .then_inc(sem(f"dk{h}"), 1)
                for h in (0, 1):
                    e = d[h]
                    r = full(dve, "dn", f"gcol{h}", p)
                    free(V.tensor_copy(gc[h][:, 0:2 * NB], r[:, 0:2 * NB]), "dn", f"gcol{h}", p)
                    read(dve, "dn", f"gcol{h}", p)
                    own(V.tensor_tensor(gc[h][:, 2 * NB:], gc[h][:, NB:2 * NB], gc[h][:, 0:NB], ALU.subtract),
                        f"gc{h}", p + 1)
                    r = full(dve, "dn", f"grow{h}", p)
                    own(V.tensor_tensor(blk(e["decT"]), blk(r[:, :]), cols(gc[h][:, 0:NB]), ALU.subtract),
                        f"diffs{h}", 2 * p + 1)
                    own(V.tensor_scalar(e["decN"], e["decT"], 0.0, None, ALU.max), f"diffs{h}", 2 * p + 2)
                    V.tensor_scalar(e["decT"], e["decT"], 0.0, None, ALU.min).then_inc(sem(f"dm{h}"), 1)
                for h in (0, 1):
                    e = d[h]
                    r = full(dve, "dn", f"rk{h}", p)
                    free(V.tensor_tensor(e["kh"], r[:, :], e["kT"], ALU.mult), "dn", f"rk{h}", p)
                    V.tensor_tensor(blk(e["sqq"]), rows(ident), cols(nr[h][:, 2, :]), ALU.mult)\
                        .then_inc(sem(f"dq{h}"), 1)
                for h in (0, 1):
                    e = d[h]
                    r = full(dve, "dn", f"kk{h}", p)
                    free(V.tensor_tensor(blk(e["N"]), blk(r[:, :]), cols(beta(h)), ALU.mult), "dn", f"kk{h}", p)
                    read(dve, "dn", f"kk{h}", p)
                    dve.wait_ge(sem(f"decN{h}"), p + 1)
                    own(V.tensor_tensor(e["N"], e["N"], e["decN"], ALU.mult), f"N{h}", p + 1)
                for h in (0, 1):
                    e = d[h]
                    r = full(dve, "dn", f"rq{h}", p)
                    free(V.scalar_tensor_tensor(out=e["qh"], in0=r[:, :], scalar=float(P) ** -0.5, in1=e["qT"],
                                                op0=ALU.mult, op1=ALU.mult), "dn", f"rq{h}", p)
                for h in (0, 1):
                    e = d[h]
                    dve.wait_ge(sem(f"eg{h}"), p + 1)
                    V.tensor_tensor(be[h][:, :], beta(h), eg[h][:, 0:NB], ALU.mult).then_inc(sem(f"be{h}"), 1)
                    r = full(dve, "dn", f"qk{h}", p)
                    dve.wait_ge(sem(f"decT{h}"), p + 1)
                    free(V.tensor_tensor(e["qkD"], r[:, :], e["decT"], ALU.mult), "dn", f"qk{h}", p)
                for h in (0, 1):
                    e = d[h]
                    r = full(dve, "dn", f"ktok{h}", p)
                    dve.wait_ge(sem(f"be{h}"), p + 1)
                    V.tensor_tensor(blk(e["kd"]), blk(r[:, :]), cols(eg[h][:, 2 * NB:]), ALU.mult)
                    dve.wait_ge(sem(f"qd{h}"), p + 1)
                    free(V.tensor_tensor(blk(e["kbg"]), blk(r[:, :]), cols(be[h][:, :]), ALU.mult), "dn", f"ktok{h}", p)
                    r = full(dve, "dn", f"vtok{h}", p)
                    free(V.tensor_tensor(blk(e["vb"]), blk(r[:, :]), cols(beta(h)), ALU.mult), "dn", f"vtok{h}", p)
                for h in (0, 1):
                    e = d[h]
                    read(dve, "dn", f"At{h}", p)
                    V.tensor_tensor(blk(e["U"]), rows(ident), blk(e["At"]), ALU.subtract).then_inc(sem(f"U0{h}"), 1)

                def copy(name, dst):
                    for h in (0, 1):
                        r = full(dve, "dn", f"{name}{h}", p)
                        free(V.tensor_copy(d[h][dst], r[:, :]), "dn", f"{name}{h}", p)

                def update(name, op, before=None):
                    for h in (0, 1):
                        r = full(dve, "dn", f"{name}{h}", p)
                        if before:
                            read(dve, "dn", f"{before}{h}", p)
                        else:
                            dve.wait_ge(sem(f"U0{h}"), p + 1)
                        free(V.tensor_tensor(d[h]["U"], d[h]["U"], r[:, :], op), "dn", f"{name}{h}", p)

                next(evac, 0)
                copy("A2t", "A2t")
                update("U1", ALU.add)
                next(evac, 0)
                copy("A4t", "A4t")
                update("U2", ALU.add, "U1")
                next(evac, 0)
                update("U3", ALU.add, "U2")
                copy("Y16", "Y")
                next(evac, 0)
                update("X16", ALU.subtract, "U3")
                next(evac, 0)
                copy("Y32", "Y")
                next(evac, 0)
                update("X32", ALU.subtract, "X16")
                next(evac, 0)
                copy("Y64", "Y")
                update("X64", ALU.subtract, "X32")
                next(evac, 0)
                for h in (0, 1):
                    e = d[h]
                    r = full(dve, "dn", f"u{h}", p)
                    V.tensor_copy(vn[h][:, :], r[:, 0:P]).then_inc(sem(f"vn{h}"), 1)
                    free(V.tensor_copy(e["u"], r[:, :]), "dn", f"u{h}", p)
                    read(dve, "dn", f"u{h}", p)
                for b in range(NB - 1):
                    for h in (0, 1):
                        r = full(dve, "dn", f"kv{b}{h}", p)
                        if b == 0:
                            ins = V.tensor_copy(st[h][:, :], r[:, 0:P])
                        else:
                            read(dve, "dn", f"kv{b - 1}{h}", p)
                            ins = V.scalar_tensor_tensor(out=st[h][:, :], in0=st[h][:, :],
                                                         scalar=eg[h][:, NB + b:NB + b + 1],
                                                         in1=r[:, 0:P], op0=ALU.mult, op1=ALU.add)
                        free(ins, "dn", f"kv{b}{h}", p)
                    for h in (0, 1):
                        dve.wait_ge(sem(f"o_step{h}"), 3 * p + b + 1)
                        r = full(dve, "dn", f"ws{b + 1}{h}", p)
                        free(V.tensor_tensor(vn[h][:, :], d[h]["u"][:, (b + 1) * P:(b + 2) * P], r[:, 0:P],
                                             ALU.subtract), "dn", f"ws{b + 1}{h}", p)
                    if b == 0:
                        next(evac, 0)
                    if b == 1:
                        next(evac, 0)
                next(evac, 0)
                for h in (0, 1):
                    e = d[h]
                    read(dve, "dn", f"oc{h}", p)
                    own(V.reciprocal(nr[h][:, 5, :], nr[h][:, 4, :]), f"inv_o{h}", p + 1)
                    V.tensor_tensor(blk(e["sqo"]), rows(ident), cols(nr[h][:, 5, :]), ALU.mult)\
                        .then_inc(sem(f"do{h}"), 1)
                for h in (0, 1):
                    e = d[h]
                    r = full(dve, "dn", f"ro{h}", p)
                    dve.wait_ge(sem(f"gC_full{h}"), p + 1)
                    free(V.tensor_tensor(e["on"], r[:, :], e["gC"], ALU.mult), "dn", f"ro{h}", p)
                    read(dve, "dn", f"ro{h}", p)
                    dve.wait_ge(sem("x_kept"), 16)
                    full(dve, "dn", f"o{h}", p)
                    free(V.scalar_tensor_tensor(out=om[:, 2 * p + h, :], in0=R[BANK.use("dn", f"o{h}", p)[0]][:, :],
                                                scalar=pv[:, PV_DNN:PV_DNN + 1], in1=e["on"], op0=ALU.mult,
                                                op1=ALU.mult), "dn", f"o{h}", p)
                next(evac, 0)

            def chained(*gens):
                for g in gens:
                    yield from g

            for _ in dn_evac(0, 0):
                pass

            n_step = [1]

            def chain(ins):
                n_step[0] += 1
                ins.then_inc(step, 1)
                dve.wait_ge(step, n_step[0])

            r = full(dve, "ab", "ab", 0)
            ins = V.tensor_tensor(abz[:, :, :], r[:, 0:NB * 8].rearrange("p (b n) -> p b n", n=8),
                                  rcol[:, :].unsqueeze(2).broadcast_to([P, NB, 8]), ALU.mult)
            free(ins, "ab", "ab", 0)
            read(dve, "ab", "ab", 0)
            chain(V.tensor_tensor(abt[0][:, :, :], abz[:, :, 0:4], dtb[:, :].unsqueeze(1).broadcast_to([P, NB, NH]),
                                  ALU.add))
            chain(V.tensor_tensor(lt[:, :, :], lp[:, :].rearrange("p (a b n) -> p a b n", a=2, b=2)[:, :, 0, :],
                                  lp[:, :].rearrange("p (a b n) -> p a b n", a=2, b=2)[:, :, 1, :], ALU.mult))
            chain(V.reduce_sum(ls[:, 0:2], lt[:, :, :], mybir.AxisListType.X))
            chain(V.tensor_scalar(abt[4][:, :, :], abt[0][:, :, :], -1.0, None, ALU.mult))
            V.tensor_tensor(abt[1][:, :, :], abt[0][:, :, :], abt[4][:, :, :], ALU.max).then_inc(sem("ab_in"), 1)
            chain(V.tensor_scalar(abt[0][:, :, :], abt[0][:, :, :], 0.0, None, ALU.max))
            dve.wait_ge(sem("ab_e"), 5)
            chain(V.tensor_tensor(abt[0][:, :, :], abt[0][:, :, :], abt[1][:, :, :], ALU.add))
            chain(V.tensor_tensor(abt[3][:, :, :], abt[0][:, :, :], alog[:, :].unsqueeze(1).broadcast_to([P, NB, NH]),
                                  ALU.mult))
            chain(V.tensor_scalar(gall[:, :, :], abt[3][:, :, :].rearrange("p b h -> p h b"), -1.0, None, ALU.mult))
            chain(V.tensor_scalar(abt[2][:, :, :], abt[2][:, :, :], 1.0, None, ALU.add))
            chain(V.reciprocal(ball[:, :, :], abt[2][:, :, :].rearrange("p b h -> p h b")))
            chain(V.tensor_tensor(ls[:, 2:3], ls[:, 1:2], ls[:, 0:1], ALU.subtract))
            chain(V.tensor_scalar(lamc[:, :], ls[:, 2:3], -LAM_INIT, None, ALU.add))

            for _ in dn_evac(1, 1):
                pass
            dn_pair(0, chained(dn_evac(2, 2), dn_evac(3, 3)))
            dn_pair(1, att_evac("diff", 0, UNIT["diff"]))
            rope(0)

            def attention(ph, i, o0, h0, evac, more=True):
                diff = ph == "diff"
                items = [(m, b) for b in range(NB) for m in (0, 1)] if diff else \
                    [(m, b) for m in (0, 1) for b in range(NB)]
                for t in range(8 + 2):
                    if t == 9 and diff and more:
                        next(evac, 0)
                        rope(i + 1)
                    if t < 8:
                        m, b = items[t]
                        w = (b + 1) * P
                        waits = [is_full(ph, f"s{t}", i)]
                        if t >= 2:
                            waits.append(("exp_" + ph, 8 * i + (t - 1)))
                        bias = cst[:, C_MASK + S - w:C_MASK + S] if diff else gb[m][:, S - w:S]
                        if not diff and b == 0:
                            waits += [(f"gb_full{m}", 32 * i + 32), ("gb_mask", 2)]
                        settled(dve, *waits)
                        r = R[BANK.use(ph, f"s{t}", i)[0]]
                        free(V.tensor_tensor_reduce(out=ns[t % 2][:, 0:w], in0=r[:, 0:w], in1=bias, scale=-1.0,
                                                    scalar=3e38, op0=ALU.add, op1=ALU.min,
                                                    accum_out=nm[:, t:t + 1]), ph, f"s{t}", i)
                    if diff:
                        if t % 2 == 0 and 2 <= t:
                            z = (t - 2) // 2
                            w = (z + 1) * P
                            dve.wait_ge(sem("exp_diff"), 8 * i + (2 * z + 2))
                            if z:
                                dve.wait_ge(sem("pn_diff"), 4 * i + z)
                            V.reciprocal(rr[:, 0:2], rs[:, 2 * z:2 * z + 2]).then_inc(sem("nrm_diff"), 1)
                            dve.wait_ge(sem("nrm_diff"), 12 * i + (3 * z + 1))
                            V.tensor_tensor(rr[:, 2:3], rr[:, 1:2], lamc[:, :], ALU.mult).then_inc(sem("nrm_diff"), 1)
                            dve.wait_ge(sem("nrm_diff"), 12 * i + (3 * z + 2))
                            if z >= 2:
                                tb, tu = BANK.use("diff", f"t{z - 2}", i)
                                dve.wait_ge(sem(f"R{tb}_full"), tu + 1)
                            V.tensor_scalar(pn[z % 2][:, 0:w], pr[1][:, 0:w], rr[:, 2:3], None, ALU.mult)\
                                .then_inc(sem("nrm_diff"), 1)
                            dve.wait_ge(sem("nrm_diff"), 12 * i + (3 * z + 3))
                            V.scalar_tensor_tensor(out=pn[z % 2][:, 0:w], in0=pr[0][:, 0:w], scalar=rr[:, 0:1],
                                                   in1=pn[z % 2][:, 0:w], op0=ALU.mult, op1=ALU.add)\
                                .then_inc(sem("pn_diff"), 1)
                    elif 1 <= t <= 8:
                        z = t - 1
                        w = (items[z][1] + 1) * P
                        dve.wait_ge(sem("exp_odd"), 8 * i + (z + 1))
                        if z >= 2:
                            dve.wait_ge(sem("pn_odd"), 8 * i + (z - 1))
                        V.reciprocal(rr[:, z % 2:z % 2 + 1], rs[:, z:z + 1]).then_inc(sem("nrm_odd"), 1)
                        dve.wait_ge(sem("nrm_odd"), 8 * i + (z + 1))
                        if z >= 2:
                            tb, tu = BANK.use("odd", f"t{z - 2}", i)
                            dve.wait_ge(sem(f"R{tb}_full"), tu + 1)
                        V.tensor_scalar(pn[z % 2][:, 0:w], pr[z % 2][:, 0:w], rr[:, z % 2:z % 2 + 1], None, ALU.mult)\
                            .then_inc(sem("pn_odd"), 1)
                    if t == 1 and diff:
                        dve.wait_ge(sem("oc_head"), i + 1)
                        V.tensor_tensor(dyn(ol, i), dyn(om, i), dyn(oh, i).bitcast(F32), ALU.subtract)\
                            .then_inc(sem("oc_tail"), 1)
                    if t == 8 and not diff:
                        next(evac, 0)
                        next(evac, 0)
                next(evac, 0)
                if diff:
                    next(evac, 0)
                full(dve, ph, "pv", i)
                r = R[3]
                if diff:
                    read(dve, ph, "oc", i)
                    V.reciprocal(nq[:, 1, :], nq[:, 0, :]).then_inc(sem("inv_od"), 1)
                    dve.wait_ge(sem("inv_od"), i + 1)
                    V.tensor_tensor(blk(osd[:, :]), rows(ident), cols(nq[:, 1, :]), ALU.mult)\
                        .then_inc(sem("do_diff"), 1)
                    next(evac, 0)
                    read(dve, ph, "ro", i)
                    free(V.tensor_tensor(osb[:, :], r[:, :], osd[:, :], ALU.mult), ph, "pv", i)
                    src = osb[:, :]
                    dve.wait_ge(sem("o_head"), i + (h0 + 1))
                    V.tensor_tensor(dyn(ol, i + o0), src, dyn(oh, i + o0).bitcast(F32), ALU.subtract)\
                        .then_inc(sem("o_tail"), 1)
                else:
                    dve.wait_ge(sem("o_head"), i + (h0 + 1))
                    free(V.tensor_tensor(dyn(ol, i + o0), r[:, :], dyn(oh, i + o0).bitcast(F32), ALU.subtract),
                         ph, "pv", i)
                next(evac, 0)

            def out_proj(base, norm):
                with dve.Fori(0, 2) as i:
                    for s in (0, 1):
                        for t in (0, 1):
                            k = 4 * i + (2 * s + t)
                            dve.wait_ge(sem(f"tile_full{s}"), 2 * i + (2 * base + t + 1))
                            if norm == 1:
                                dve.wait_ge(sem("x_back"), 16 * KD // 2)
                            V.tensor_tensor(dyn(x, k), dyn(x, k), acc[2 * s + t][:, :], ALU.add)\
                                .then_inc(sem(f"acc_free{s}"), 1)
                        units_split_dve(dve, s, i + (base + 1))
                        for t in (0, 1):
                            x_tail(norm, 4 * i + (2 * s + t))

            def mlp(layer, norm_after, last):
                for n, (j0, count) in enumerate(HALVES):
                    g0 = UNIT[f"in{layer}{n}"]
                    base = 11 * layer + 6 * n
                    with dve.Fori(0, count // 2) as i:
                        for s in (0, 1):
                            j = 2 * i + (j0 + s)
                            w0 = PV_CW[layer]
                            dve.wait_ge(sem(f"tile_full{s}"), 2 * i + (2 * g0 + 1))
                            V.tensor_tensor(cb[s][:, ALPHA:ALPHA + S], acc[2 * s][:, :], rstd[:, :], ALU.mult)\
                                .then_inc(sem(f"acc_free{s}"), 1)
                            dve.wait_ge(sem("mtap"), 2 * i + (2 * base + s + 1))
                            for tap in (1, 2):
                                if tap == 2:
                                    dve.wait_ge(sem(f"mconv{s}"), 2 * i + (2 * base + 1))
                                o = ALPHA - 2 + tap
                                V.scalar_tensor_tensor(out=cta[s][:, :], in0=cb[s][:, o:o + S],
                                                       scalar=pv[:, bass.ds(j + (w0 + JF * tap), 1)],
                                                       in1=cta[s][:, :], op0=ALU.mult, op1=ALU.add)\
                                    .then_inc(sem(f"mconv{s}"), 1)
                            dve.wait_ge(sem(f"tile_full{s}"), 2 * i + (2 * g0 + 2))
                            V.tensor_tensor(ur[s][:, :], acc[2 * s + 1][:, :], rstd[:, :], ALU.mult)\
                                .then_inc(sem(f"acc_free{s}"), 1)
                            dve.wait_ge(sem("msilu"), 2 * i + (2 * base + s + 1))
                            dve.wait_ge(sem(f"acc_free{s}"), 2 * i + (2 * g0 + 2))
                            V.tensor_tensor(pd[s][:, :], ur[s][:, :], sl[s][:, :], ALU.mult).then_inc(sem("prod"), 1)
                            dve.wait_ge(sem("a_head"), 2 * i + (2 * base + s + 1))
                            V.tensor_tensor(dyn(al, 2 * i + s), pd[s][:, :], dyn(ah, 2 * i + s).bitcast(F32),
                                            ALU.subtract).then_inc(sem("a_tail"), 1)
                            units_split_dve(dve, s, i + (g0 + 1))
                    g0 = UNIT[f"ff{layer}{n}"]

                    def x_tiles(i, g, split):
                        for s in (0, 1):
                            k = 2 * i + s
                            dve.wait_ge(sem(f"tile_full{s}"), 2 * g + 2)
                            V.tensor_tensor(dyn(x, k), dyn(x, k), acc[2 * s][:, :], ALU.add)\
                                .then_inc(sem(f"acc_free{s}"), 2)
                            if n == 1 and norm_after < 4:
                                x_tail(norm_after, k)
                            if split:
                                units_split_dve(dve, s, g + 1)

                    with dve.Fori(0, 3 if last and n == 1 else 4) as i:
                        x_tiles(i, i + g0, True)
                    if last and n == 1:
                        x_tiles(3, g0 + 3, False)

            with dve.Fori(0, NH - 1) as i:
                attention("diff", i, NH, 0, att_evac("diff", i + 1, i + (UNIT["diff"] + 1)))
            attention("diff", NH - 1, NH, 0, iter(()), more=False)
            out_proj(UNIT["out0"], 1)
            norm_rstd(1)
            mlp(0, 2, False)
            norm_rstd(2)
            for _ in att_evac("odd", 0, UNIT["odd"]):
                pass
            with dve.Fori(0, NPAIR - 1) as i:
                attention("odd", i, 0, NH, att_evac("odd", i + 1, i + (UNIT["odd"] + 1)))
            attention("odd", NPAIR - 1, 0, NH, iter(()))
            out_proj(UNIT["out1"], 3)
            norm_rstd(3)
            mlp(1, 4, True)
            norm_rstd(4)
            for k in range(KD):
                r = full(dve, "yt", f"x{k}", 0)
                if k >= 2:
                    dve.wait_ge(sem(f"out_done{k % 2}"), 16 * (k // 2))
                free(V.tensor_tensor(ob[k % 2][:, :, :], blk(r[:, :]), cols(rcol[:, :]), ALU.mult), "yt", f"x{k}", 0)


_INS = ["x", "even_norm_mix", "even_w_in", "even_dn_conv", "even_dn_A_log", "even_dn_dt_bias", "even_dn_norm",
        "even_diff_lambda", "even_diff_subln", "even_w_out", "odd_norm_mix", "odd_w_qkv", "odd_rel_bias",
        "odd_w_out", "ffn_norm", "ffn_w_in", "ffn_conv_w", "ffn_conv_b", "ffn_w_out", "final_norm"]


def kernel(**inputs):
    import numpy as _np
    import concourse.bacc as _bacc
    from concourse import mybir as _mybir
    from concourse.bass_utils import run_bass_kernel_spmd as _run

    nc = _bacc.Bacc("TRN2", target_bir_lowering=False, num_devices=1)
    arrays, aps = {}, {}
    given = {name: _np.ascontiguousarray(inputs[name]) for name in _INS}
    given["consts"] = constants()
    for name, a in given.items():
        arrays[f"in_{name}"] = a
        aps[name] = nc.dram_tensor(f"in_{name}", a.shape, _mybir.dt.from_np(a.dtype), kind="ExternalInput").ap()
    out = nc.dram_tensor("out_0", (S, D), _mybir.dt.float32, kind="ExternalOutput").ap()
    build(nc, aps, out)
    r = _run(nc, [arrays], core_ids=[0])
    return r.results[0]["out_0"].reshape(1, S, D)
```
